# Optimizing a Trainium2 kernel written in Bass

```python
import math
import jax
import jax.numpy as jnp
from jax import lax
import numpy as np

D_MODEL = 1024
BATCH = 1
SEQ = 1024
DEPTH = 2
DEC_BATCH = 8
DEC_SEQ = 4
PAST_LEN = 8192
PAGE_SIZE = 128

MIX_W = D_MODEL
N_MIXERS = 4
BRANCH_W = MIX_W // N_MIXERS
S5_CH = 16
S5_GROUPS = BRANCH_W // S5_CH
S5_STATE = 64
HGRN_HEADS = 4
HGRN_DK = 64
HGRN_DV = BRANCH_W // HGRN_HEADS
MLSTM_HEADS = 4
MLSTM_DH = BRANCH_W // MLSTM_HEADS
RET_HEADS = 4
RET_DK = 32
RET_DV = BRANCH_W // RET_HEADS
ROPE_BASE = 10000.0
CHUNK = 64
EPS = 1e-6
LOGI_PAD = -1e30

PROJ_SIZES = (
    BRANCH_W, BRANCH_W,
    HGRN_HEADS * HGRN_DK, HGRN_HEADS * HGRN_DK, BRANCH_W, BRANCH_W,
    BRANCH_W, BRANCH_W, BRANCH_W, BRANCH_W, MLSTM_HEADS, MLSTM_HEADS, BRANCH_W,
    RET_HEADS * RET_DK, RET_HEADS * RET_DK, BRANCH_W, BRANCH_W,
)
D_IN = sum(PROJ_SIZES)

kernel_name = 'hymba_style_s5_hgrn2_mlstm_retnet_step'

def rmsnorm(x, w):
    xf = x.astype(jnp.float32)
    xf = xf * lax.rsqrt(jnp.mean(xf * xf, axis=-1, keepdims=True) + EPS)
    return (xf * w.astype(jnp.float32)).astype(x.dtype)

def head_norm(o):
    mu = jnp.mean(o, axis=-1, keepdims=True)
    var = jnp.mean(jnp.square(o - mu), axis=-1, keepdims=True)
    return (o - mu) * lax.rsqrt(var + EPS)

def to_heads(t, n_heads):
    b, l, _ = t.shape
    return t.reshape(b, l, n_heads, -1).transpose(0, 2, 1, 3)

def from_heads(t):
    b, h, l, d = t.shape
    return t.transpose(0, 2, 1, 3).reshape(b, l, h * d)

def pad_time(t, pad, value=0.0):
    widths = [(0, 0)] * t.ndim
    widths[2] = (0, pad)
    return jnp.pad(t, widths, constant_values=value)

def to_blocks(t, n_blk, c):
    b, h = t.shape[:2]
    return jnp.moveaxis(t.reshape((b, h, n_blk, c) + t.shape[3:]), 2, 0)

def rotary(t, pos):
    half = t.shape[-1] // 2
    inv_freq = ROPE_BASE ** (-jnp.arange(half, dtype=jnp.float32) / half)
    ang = pos.astype(jnp.float32)[:, None] * inv_freq[None, :]
    cos, sin = jnp.cos(ang), jnp.sin(ang)
    t1, t2 = t[..., :half], t[..., half:]
    return jnp.concatenate([t1 * cos - t2 * sin, t1 * sin + t2 * cos], axis=-1)

def chunked_gated_recurrence(q, k, v, log_f, s0):
    b_, h_, l_, _ = q.shape
    c = min(CHUNK, l_)
    n_blk = -(-l_ // c)
    pad = n_blk * c - l_
    if pad:
        q, k, v, log_f = (pad_time(t, pad) for t in (q, k, v, log_f))
    scalar_decay = log_f.shape[-1] == 1
    idx = jnp.arange(c)
    causal = idx[:, None] >= idx[None, :]

    def step(s, inp):
        qc, kc, vc, gc = inp
        cum = jnp.cumsum(gc, axis=2)
        inter = jnp.einsum('bhtk,bhkv->bhtv', qc * jnp.exp(cum), s)
        rel = cum[:, :, :, None, :] - cum[:, :, None, :, :]
        decay = jnp.exp(jnp.where(causal[:, :, None], rel, -jnp.inf))
        if scalar_decay:
            scores = jnp.einsum('bhtk,bhsk->bhts', qc, kc) * decay[..., 0]
        else:
            scores = jnp.einsum('bhtk,bhtsk,bhsk->bhts', qc, decay, kc)
        o = inter + jnp.einsum('bhts,bhsv->bhtv', scores, vc)
        last = cum[:, :, -1:, :]
        s = jnp.exp(last[:, :, 0, :])[..., None] * s + jnp.einsum('bhsk,bhsv->bhkv', kc * jnp.exp(last - cum), vc)
        return s, o

    s_fin, o = lax.scan(step, s0, tuple(to_blocks(t, n_blk, c) for t in (q, k, v, log_f)))
    o = jnp.moveaxis(o, 0, 2).reshape(b_, h_, n_blk * c, -1)[:, :, :l_]
    return o, s_fin

def mlstm_chunked(q, k, v, log_i, log_f, c0, n0, m0):
    b_, h_, l_, _ = q.shape
    c = min(CHUNK, l_)
    n_blk = -(-l_ // c)
    pad = n_blk * c - l_
    if pad:
        q, k, v, log_f = (pad_time(t, pad) for t in (q, k, v, log_f))
        log_i = pad_time(log_i, pad, LOGI_PAD)
    idx = jnp.arange(c)
    causal = idx[:, None] >= idx[None, :]

    def step(carry, inp):
        cs, ns, ms = carry
        qc, kc, vc, ic, fc = inp
        cum = jnp.cumsum(fc, axis=-1)
        w_prev = cum + ms[..., None]
        log_d = jnp.where(causal, cum[..., :, None] - cum[..., None, :] + ic[..., None, :], -jnp.inf)
        m_t = jnp.maximum(w_prev, jnp.max(log_d, axis=-1))
        d_mat = jnp.exp(log_d - m_t[..., None])
        s_prev = jnp.exp(w_prev - m_t)
        scores = jnp.einsum('bhtk,bhsk->bhts', qc, kc) * d_mat
        num = s_prev[..., None] * jnp.einsum('bhtk,bhkv->bhtv', qc, cs) + jnp.einsum('bhts,bhsv->bhtv', scores, vc)
        den = s_prev * jnp.einsum('bhtk,bhk->bht', qc, ns) + jnp.sum(scores, axis=-1)
        h = num / jnp.maximum(jnp.abs(den), jnp.exp(-m_t))[..., None]
        m_new = m_t[..., -1]
        w_k = jnp.exp(cum[..., -1:] - cum + ic - m_new[..., None])
        carry_scale = jnp.exp(cum[..., -1] + ms - m_new)
        cs = carry_scale[..., None, None] * cs + jnp.einsum('bhs,bhsk,bhsv->bhkv', w_k, kc, vc)
        ns = carry_scale[..., None] * ns + jnp.einsum('bhs,bhsk->bhk', w_k, kc)
        return (cs, ns, m_new), h

    (c_fin, n_fin, m_fin), h = lax.scan(
        step, (c0, n0, m0), tuple(to_blocks(t, n_blk, c) for t in (q, k, v, log_i, log_f)))
    h = jnp.moveaxis(h, 0, 2).reshape(b_, h_, n_blk * c, -1)[:, :, :l_]
    return h, c_fin, n_fin, m_fin

def s5_mixer(u, h0_re, h0_im, lam_re, lam_im, b_re, b_im, c_re, c_im, d_skip, log_dt, w_glu):
    bsz, l_, _ = u.shape
    f32 = jnp.float32
    lam = lax.complex(lam_re.astype(f32), lam_im.astype(f32))
    dt = jnp.exp(log_dt.astype(f32))[:, None]
    a_bar = jnp.exp(lam * dt)
    b_bar = ((a_bar - 1.0) / lam)[:, :, None] * lax.complex(b_re.astype(f32), b_im.astype(f32))
    c_mat = lax.complex(c_re.astype(f32), c_im.astype(f32))
    ug = u.reshape(bsz, l_, S5_GROUPS, S5_CH).astype(jnp.complex64)
    bu = jnp.einsum('gpc,blgc->blgp', b_bar, ug)
    bu = bu.at[:, 0].add(a_bar * lax.complex(h0_re.astype(f32), h0_im.astype(f32)))
    a_all = jnp.broadcast_to(a_bar, bu.shape)

    def combine(e1, e2):
        a1, x1 = e1
        a2, x2 = e2
        return a2 * a1, a2 * x1 + x2

    _, h = lax.associative_scan(combine, (a_all, bu), axis=1)
    y = jnp.real(jnp.einsum('gcp,blgp->blgc', c_mat, h)).reshape(bsz, l_, BRANCH_W) + d_skip.astype(f32) * u
    y = jax.nn.gelu(y)
    y = y * jax.nn.sigmoid(y @ w_glu.astype(f32))
    return y, jnp.real(h[:, -1]), jnp.imag(h[:, -1])

def trunk(x, pos, states, params):
    s5_re, s5_im, hg_s, ml_c, ml_n, ml_m, rt_s = states
    (norm_w, w_in, w_out, final_norm_w, lam_re, lam_im, b_re, b_im, c_re, c_im,
     s5_d, s5_log_dt, s5_w_glu, hgrn_lb_logits, mlstm_b_i, mlstm_b_f) = params
    f32 = jnp.float32
    split_points = [int(v) for v in np.cumsum(PROJ_SIZES)[:-1]]
    lower_bounds = jnp.cumsum(jax.nn.softmax(hgrn_lb_logits.astype(f32), axis=0), axis=0)
    lower_bounds = lower_bounds - lower_bounds[0]
    ret_log_decay = jnp.log(1.0 - 2.0 ** (-5.0 - jnp.arange(RET_HEADS, dtype=f32)))
    new = [[] for _ in range(7)]
    for l in range(DEPTH):
        h = rmsnorm(x, norm_w[l])
        proj = jnp.einsum('bld,de->ble', h, w_in[l]).astype(f32)
        (s5_x, s5_g, hg_q, hg_f, hg_i, hg_g, ml_q, ml_k, ml_v, ml_o, ml_i, ml_f, ml_g,
         rt_q, rt_k, rt_v, rt_g) = jnp.split(proj, split_points, axis=-1)

        s5_out, s5_hre, s5_him = s5_mixer(s5_x, s5_re[l], s5_im[l], lam_re[l], lam_im[l], b_re[l], b_im[l],
                                          c_re[l], c_im[l], s5_d[l], s5_log_dt[l], s5_w_glu[l])

        lb = lower_bounds[l].reshape(HGRN_HEADS, 1, HGRN_DK)
        hq = jax.nn.silu(to_heads(hg_q, HGRN_HEADS))
        log_f = jnp.logaddexp(jnp.log(lb), jnp.log1p(-lb) + jax.nn.log_sigmoid(to_heads(hg_f, HGRN_HEADS)))
        hk = -jnp.expm1(log_f)
        ho, hg_new = chunked_gated_recurrence(hq, hk, to_heads(hg_i, HGRN_HEADS), log_f, hg_s[l].astype(f32))
        hg_out = from_heads(head_norm(ho))

        mq = to_heads(ml_q, MLSTM_HEADS)
        mk = to_heads(ml_k, MLSTM_HEADS) * (MLSTM_DH ** -0.5)
        mv = to_heads(ml_v, MLSTM_HEADS)
        log_ig = (ml_i + mlstm_b_i[l].astype(f32)).transpose(0, 2, 1)
        log_fg = jax.nn.log_sigmoid(ml_f + mlstm_b_f[l].astype(f32)).transpose(0, 2, 1)
        mh, mc_new, mn_new, mm_new = mlstm_chunked(mq, mk, mv, log_ig, log_fg, ml_c[l].astype(f32),
                                                   ml_n[l].astype(f32), ml_m[l].astype(f32))
        ml_out = from_heads(head_norm(jax.nn.sigmoid(to_heads(ml_o, MLSTM_HEADS)) * mh))

        rq = rotary(to_heads(rt_q, RET_HEADS), pos)
        rk = rotary(to_heads(rt_k, RET_HEADS), pos) * (RET_DK ** -0.5)
        rv = to_heads(rt_v, RET_HEADS)
        log_g = jnp.broadcast_to(ret_log_decay[None, :, None, None], rq.shape[:3] + (1,))
        ro, rt_new = chunked_gated_recurrence(rq, rk, rv, log_g, rt_s[l].astype(f32))
        rt_out = from_heads(head_norm(ro))

        mixed = jnp.concatenate([s5_out * jax.nn.silu(s5_g), hg_out * jax.nn.silu(hg_g),
                                 ml_out * jax.nn.silu(ml_g), rt_out * jax.nn.silu(rt_g)], axis=-1)
        x = x + jnp.einsum('ble,ed->bld', mixed.astype(x.dtype), w_out[l])
        for lst, val in zip(new, (s5_hre, s5_him, hg_new, mc_new, mn_new, mm_new, rt_new)):
            lst.append(val)
    y = rmsnorm(x, final_norm_w)
    return y, [jnp.stack(v, axis=0) for v in new]

def setup_inputs(seed: int = 0) -> dict:
    key = jax.random.key(seed)
    ks = jax.random.split(key, 24)
    f32 = jnp.float32

    def nrm(k, shape, s):
        return jax.random.normal(k, shape, f32) * s

    return {
        'x_prompt': nrm(ks[0], (BATCH, SEQ, D_MODEL), 1.0),
        'x_sample': nrm(ks[1], (DEC_BATCH, DEC_SEQ, D_MODEL), 1.0),
        'state_s5_re': nrm(ks[2], (DEPTH, DEC_BATCH, S5_GROUPS, S5_STATE), 0.5),
        'state_s5_im': nrm(ks[3], (DEPTH, DEC_BATCH, S5_GROUPS, S5_STATE), 0.5),
        'state_hgrn': nrm(ks[4], (DEPTH, DEC_BATCH, HGRN_HEADS, HGRN_DK, HGRN_DV), 0.5),
        'state_mlstm_C': nrm(ks[5], (DEPTH, DEC_BATCH, MLSTM_HEADS, MLSTM_DH, MLSTM_DH), 0.5),
        'state_mlstm_n': nrm(ks[6], (DEPTH, DEC_BATCH, MLSTM_HEADS, MLSTM_DH), 0.5),
        'state_mlstm_m': nrm(ks[7], (DEPTH, DEC_BATCH, MLSTM_HEADS), 1.0),
        'state_ret': nrm(ks[8], (DEPTH, DEC_BATCH, RET_HEADS, RET_DK, RET_DV), 0.5),
        'norm_w': 1.0 + nrm(ks[9], (DEPTH, D_MODEL), 0.02),
        'w_in': nrm(ks[10], (DEPTH, D_MODEL, D_IN), D_MODEL ** -0.5),
        'w_out': nrm(ks[11], (DEPTH, MIX_W, D_MODEL), 0.5 * MIX_W ** -0.5),
        'final_norm_w': 1.0 + nrm(ks[12], (D_MODEL,), 0.02),
        's5_lambda_re': -0.5 + nrm(ks[13], (DEPTH, S5_GROUPS, S5_STATE), 0.01),
        's5_lambda_im': math.pi * jnp.arange(S5_STATE, dtype=f32) + nrm(ks[14], (DEPTH, S5_GROUPS, S5_STATE), 0.01),
        's5_B_re': nrm(ks[15], (DEPTH, S5_GROUPS, S5_STATE, S5_CH), (2 * S5_CH) ** -0.5),
        's5_B_im': nrm(ks[16], (DEPTH, S5_GROUPS, S5_STATE, S5_CH), (2 * S5_CH) ** -0.5),
        's5_C_re': nrm(ks[17], (DEPTH, S5_GROUPS, S5_CH, S5_STATE), (2 * S5_STATE) ** -0.5),
        's5_C_im': nrm(ks[18], (DEPTH, S5_GROUPS, S5_CH, S5_STATE), (2 * S5_STATE) ** -0.5),
        's5_D': nrm(ks[19], (DEPTH, BRANCH_W), 1.0),
        's5_log_dt': jax.random.uniform(ks[20], (DEPTH, S5_GROUPS), f32, math.log(1e-3), math.log(1e-1)),
        's5_w_glu': nrm(ks[21], (DEPTH, BRANCH_W, BRANCH_W), BRANCH_W ** -0.5),
        'hgrn_lb_logits': nrm(ks[22], (DEPTH, HGRN_HEADS * HGRN_DK), 1.0),
        'mlstm_b_i': nrm(ks[23], (DEPTH, MLSTM_HEADS), 0.1),
        'mlstm_b_f': jnp.linspace(3.0, 6.0, MLSTM_HEADS, dtype=f32)[None, :] + nrm(jax.random.fold_in(ks[23], 1), (DEPTH, MLSTM_HEADS), 0.1),
    }

def reference(x_prompt, x_sample, state_s5_re, state_s5_im, state_hgrn, state_mlstm_C, state_mlstm_n,
              state_mlstm_m, state_ret, norm_w, w_in, w_out, final_norm_w, s5_lambda_re, s5_lambda_im,
              s5_B_re, s5_B_im, s5_C_re, s5_C_im, s5_D, s5_log_dt, s5_w_glu, hgrn_lb_logits,
              mlstm_b_i, mlstm_b_f):
    f32 = jnp.float32
    params = (norm_w, w_in, w_out, final_norm_w, s5_lambda_re, s5_lambda_im, s5_B_re, s5_B_im,
              s5_C_re, s5_C_im, s5_D, s5_log_dt, s5_w_glu, hgrn_lb_logits, mlstm_b_i, mlstm_b_f)
    bp, lp = x_prompt.shape[0], x_prompt.shape[1]
    zero_states = (
        jnp.zeros((DEPTH, bp, S5_GROUPS, S5_STATE), f32),
        jnp.zeros((DEPTH, bp, S5_GROUPS, S5_STATE), f32),
        jnp.zeros((DEPTH, bp, HGRN_HEADS, HGRN_DK, HGRN_DV), f32),
        jnp.zeros((DEPTH, bp, MLSTM_HEADS, MLSTM_DH, MLSTM_DH), f32),
        jnp.zeros((DEPTH, bp, MLSTM_HEADS, MLSTM_DH), f32),
        jnp.zeros((DEPTH, bp, MLSTM_HEADS), f32),
        jnp.zeros((DEPTH, bp, RET_HEADS, RET_DK, RET_DV), f32),
    )
    pos_prompt = jnp.arange(lp, dtype=jnp.int32)
    pos_sample = PAST_LEN + jnp.arange(x_sample.shape[1], dtype=jnp.int32)
    y_prompt, (p_s5_re, p_s5_im, p_hgrn, p_mlstm_C, p_mlstm_n, p_mlstm_m, p_ret) = trunk(
        x_prompt, pos_prompt, zero_states, params)
    sample_states = (state_s5_re, state_s5_im, state_hgrn, state_mlstm_C, state_mlstm_n, state_mlstm_m, state_ret)
    y_sample, (d_s5_re, d_s5_im, d_hgrn, d_mlstm_C, d_mlstm_n, d_mlstm_m, d_ret) = trunk(
        x_sample, pos_sample, sample_states, params)
    return (y_prompt, y_sample,
            p_s5_re, p_s5_im, p_hgrn, p_mlstm_C, p_mlstm_n, p_mlstm_m, p_ret,
            d_s5_re, d_s5_im, d_hgrn, d_mlstm_C, d_mlstm_n, d_mlstm_m, d_ret)


_drawn_inputs = setup_inputs


def setup_inputs(seed=0):
    import zlib

    import numpy as np

    out = dict(_drawn_inputs(seed))
    spreads = {}
    factors = {}
    for name, (base, spread) in spreads.items():
        noise = np.random.default_rng([zlib.crc32(name.encode()), seed]).standard_normal(out[name].shape)
        drawn = base * np.exp(spread * noise) if base else spread * noise
        out[name] = jnp.asarray(drawn.astype(out[name].dtype))
    for name, factor in factors.items():
        out[name] = (out[name] * factor).astype(out[name].dtype)
    return out
```

```python
from contextlib import ExitStack

import numpy as np

import concourse.bass as bass
from concourse import mybir

F32 = mybir.dt.float32
F32R = mybir.dt.float32r
U8 = mybir.dt.uint8
ALU = mybir.AluOpType
ACT = mybir.ActivationFunctionType
AX = mybir.AxisListType.X

P = 128
D = 1024
KT = D // P
SEQ, DEPTH, NB, DSEQ = 1024, 2, 8, 4
PAST = 8192
HALF = SEQ // 2
TS = NB * DSEQ
W = HALF + TS
WP = HALF + P
CH = 128
NCH = HALF // CH
WC = 264
D_IN = 3592
EPS = 1e-6

BLOCKS = [
    ("hg_q", 512, 256, "ch", "av"), ("hg_f", 768, 256, "ch", "a"),
    ("hg_i", 1024, 256, "tok", "a"), ("hg_g", 1280, 256, "tok", "av"),
    ("ml_q", 1536, 256, "ch", "a"), ("ml_k", 1792, 256, "ch", "a"),
    ("ml_v", 2048, 256, "tok", "a"), ("ml_o", 2304, 256, "tok", "a"),
    ("ml_ifg", 2560, 264, "tok", "av"),
    ("rt_qk", 2824, 256, "ch", "v"), ("rt_v", 3080, 256, "tok", "a"), ("rt_g", 3336, 256, "tok", "av"),
    ("s5_x", 0, 256, "ch", "a"), ("s5_g", 256, 256, "ch", "av"),
]
BLOCK = {b[0]: b for b in BLOCKS}


class Signal:

    def __init__(self, nc, ctx, name, keys, unit=1):
        self.sem = ctx.enter_context(nc.semaphore(name))
        self.name, self.unit, self.fired, self.keys = name, unit, set(), list(keys)
        self.value = {k: unit * (i + 1) for i, k in enumerate(self.keys)}

    def inc(self, key):
        assert key in self.value and key not in self.fired, (self.name, key)
        self.fired.add(key)
        return self.sem, self.unit

    def at(self, key):
        return self.sem, self.value[key]


class Chain:

    def __init__(self, nc, ctx, name):
        self.sem, self.n = ctx.enter_context(nc.semaphore(name)), 0

    def inc(self):
        self.n += 1
        return self.sem, 1

    def now(self):
        return self.sem, self.n


class Bank:

    def __init__(self, nc, ctx, name, uses, tensor):
        self.t = tensor
        self.full = Signal(nc, ctx, name + "_full", uses)
        self.free = Signal(nc, ctx, name + "_free", uses)

    def claim(self, pe, key):
        i = self.full.keys.index(key)
        if i:
            pe.wait_ge(*self.free.at(self.full.keys[i - 1]))


def make_plan(parts):
    plan = []
    for n in range(2 * DEPTH):
        plan.append(("norm", n))
        if n == 0 and "s5" in parts:
            plan += [("s5set", l) for l in range(DEPTH)]
        for br in ("hg", "ml", "rt", "s5"):
            if br not in parts:
                continue
            plan += [("proj", n, b[0]) for b in BLOCKS if b[0][:2] == br]
            if br in ("hg", "ml"):
                plan.append((br + "pre", n))
            if br == "s5":
                plan.append(("s5", n))

            else:
                plan += [(br, n, c) for c in range(NCH + n % 2)]
        plan.append(("out", n))
    plan.append(("final",))
    return plan


def pieces_of(plan):
    out = []
    for s in plan:
        if s[0] == "proj":
            n, name = s[1], s[2]
            half = n % 2
            kinds = ([(j, m) for j in range(2) for m in range(1 + half)] if BLOCK[name][3] == "ch"
                     else [(t,) for t in range(NCH + half)])
            out += [(n, name) + k for k in kinds]
    return out


LEVELS = [64, 32, 16, 8, 4, 2, 1]
NL = len(LEVELS)
SLEV = [2, 1]
CONST = {}


def constants():
    p = np.arange(P)[:, None]
    t = np.arange(P)[None, :]
    same = (np.arange(TS)[:, None] // DSEQ == np.arange(TS)[None, :] // DSEQ)
    tri = np.arange(TS)[None, :] >= np.arange(TS)[:, None]
    first = np.ones(W, np.float32)
    first[0:HALF:CH] = 0
    first[HALF:W:DSEQ] = 0
    parts = {
        "ident": np.eye(P),
        "reset": np.broadcast_to(first, (P, W)),
        "causal": t >= p,
        "cneg": np.where(t >= p, 0.0, -1e30),
        "causal_s": same & tri,
        "cneg_s": np.where(same & tri, 0.0, -1e30),
        "selj": np.stack([(np.arange(4)[:, None] == 2 * j + (np.arange(P) >= 64)[None, :]) for j in range(2)], 1).reshape(4, -1),
        "headsel": np.arange(P)[:, None] // 64 == np.arange(2)[None, :],
        "halfpi": np.full((P, 1), np.pi / 2),
        "gam": (1 - 2.0 ** (-5.0 - p // 32)) ** np.array([[CH, DSEQ]]),
        "bmask": np.arange(TS)[:, None] // DSEQ == np.arange(NB)[None, :],
    }
    at, cols = 0, []
    for k, a in parts.items():
        a = np.asarray(a, np.float32)
        full = np.zeros((P, a.shape[1]), np.float32)
        full[:a.shape[0]] = a
        CONST[k] = (at, a.shape[0], a.shape[1])
        at += a.shape[1]
        cols.append(full)
    masks = np.zeros((P, NL * 64 + 2 * 16 + P), np.float32)
    for i, w in enumerate(LEVELS):
        u = np.arange(64)
        blk = u // w
        masks[:, i * 64:(i + 1) * 64] = (p // (2 * w) == blk) & (p % (2 * w) < w)
    for i, w in enumerate(SLEV):
        u = np.arange(16)
        masks[:TS, NL * 64 + i * 16:NL * 64 + (i + 1) * 16] = ((p // (2 * w) == u // w) & (p % (2 * w) < w))[:TS]
    masks[:, NL * 64 + 32:] = np.eye(P)
    rot = np.zeros((2, P, 4, W), np.float32)
    inv = (np.float32(10000.0) ** (-np.arange(16, dtype=np.float32) / np.float32(16)))
    i = np.arange(P) % 32
    gamma = 1 - 2.0 ** (-5.0 - np.arange(P) // 32)
    for half in range(2):
        pos = np.concatenate([np.arange(HALF) + HALF * half, PAST + np.arange(TS) % DSEQ]).astype(np.float32)
        loc = np.concatenate([np.arange(HALF) % CH, np.arange(TS) % DSEQ]) + 1
        ang = (pos[None, :] * inv[i % 16][:, None]).astype(np.float32).astype(np.float64)
        c, s = np.cos(ang), np.where(i < 16, -1, 1)[:, None] * np.sin(ang)
        up, down = gamma[:, None] ** loc[None, :], gamma[:, None] ** -loc[None, :].astype(float) * 32 ** -0.5
        rot[half] = np.stack([c * up, s * up, c * down, s * down], 1)
    return np.concatenate(cols, 1), masks, rot.reshape(2, P, 4 * W)


constants()


def trunk_kernel(nc, inp, out, parts=("hg", "ml", "rt", "s5")):
    plan = make_plan(parts)
    ctx = ExitStack()
    with ctx:
        def sb(name, shape, dt=F32):
            return ctx.enter_context(nc.sbuf_tensor(name, shape, dt))

        def signal(name, keys, unit=1):
            return Signal(nc, ctx, name, keys, unit)

        def tiles_of(n):
            return range(NCH + n % 2)

        def chunk_len(c):
            return CH if c < NCH else TS

        def cols(c):
            return slice(c * CH, c * CH + chunk_len(c))

        def outs_of(n):
            return [(n, b, t) for b in range(4) for t in tiles_of(n)]

        norm_tiles = [(s[1], t) for s in plan if s[0] == "norm" for t in tiles_of(s[1])]
        final_tiles = [("final", t) for t in range(2 * NCH + 1)]
        all_tiles = norm_tiles + final_tiles
        tslot = {k: i % 2 for i, k in enumerate(all_tiles)}
        in_blocks = [s[1:] for s in plan if s[0] == "proj"]
        pieces = pieces_of(plan)
        out_pieces = [k for s in plan if s[0] == "out" for k in outs_of(s[1])]
        w_loads, proj_uses = [], []
        for s in plan:
            if s[0] == "norm":
                proj_uses += [("norm", s[1], t, g) for t in tiles_of(s[1]) for g in range(2)]
            elif s[0] == "proj":
                w_loads.append(s[1:])
                proj_uses += [k for k in pieces if k[:2] == s[1:]]
            elif s[0] == "out":
                w_loads += [(s[1], "wo", b) for b in range(4)]
                proj_uses += outs_of(s[1])
        bank_of = {k: i % 3 for i, k in enumerate(proj_uses)}
        wslot = {k: i % 2 for i, k in enumerate(w_loads)}
        hslot = {k: i % 2 for i, k in enumerate(in_blocks)}
        oslot = {k: i % 3 for i, k in enumerate(out_pieces)}
        last_piece = {b: [k for k in pieces if k[:2] == b][-1] for b in in_blocks}
        mixes = [s[0:1] + s[1:] for s in plan if s[0] in ("hg", "ml", "rt")]
        pres = [s for s in plan if s[0] in ("hgpre", "mlpre")]
        mix_tile = {"s5": 0, "hg": 2, "ml": 4, "rt": 6}
        score_keys, upd_keys, aux_keys = [], [], []
        for s in plan:
            if s[0] == "s5set":
                score_keys += [s + (i,) for i in range(4)]
                aux_keys.append(s + ("C",))
            if s[0] == "s5":
                score_keys += [s + (i,) for i in range(3)]
                if s[1] % 2:
                    upd_keys += [s + (i,) for i in ("w", "y", "glu")]
                    aux_keys.append(s + ("y",))
            if s[0] == "mlpre":
                score_keys.append(s + (0,))
                upd_keys += [s + ("s",)] * (s[1] % 2)
            elif s in mixes:
                sample = s[2] == NCH
                score_keys += [s + (j,) for j in range(1 if s[0] == "rt" else 2)] + [s + ("su",)] * sample
                upd_keys += [s + ("inter",), ] * sample + ([s + ("n",)] * (s[0] == "ml") if sample else [s + ("U",)])
                aux_keys += [s + ("turn",), s + ("mixed",)]
        samples = [m for m in mixes if m[2] == NCH]

        psum = ctx.enter_context(nc.psum_tensor("psum", [P, 8, 512], F32))
        PB = [Bank(nc, ctx, f"proj{i}", [k for k in proj_uses if bank_of[k] == i], psum[:, i, :]) for i in range(3)]
        scores = Bank(nc, ctx, "scores", score_keys, psum[:, 3:5, :])
        outb = Bank(nc, ctx, "outb", mixes, psum[:, 5, :])
        aux = Bank(nc, ctx, "aux", aux_keys, psum[:, 6, :])
        upd = Bank(nc, ctx, "upd", upd_keys, psum[:, 7, :])

        const = sb("const", [P, inp["c_packed"].shape[1]])
        cm = sb("cm", [P, inp["c_masks"].shape[1]], U8)

        def C(name):
            at, rows, width = CONST[name]
            return const[0:rows, at:at + width]

        ident = C("ident")
        hhi = sb("hhi", [P, KT, W], F32R)
        hlo = sb("hlo", [P, KT, W], F32R)
        wraw = sb("wraw", [P, 2, KT, WC])
        whi = sb("whi", [P, 2, KT, WC], F32R)
        wlo = sb("wlo", [P, 2, KT, WC], F32R)
        mixT = sb("mixT", [P, 8, W])
        xo = sb("xo", [P, 3, 256])
        th = sb("th", [P, 2, 512])
        ssq = sb("ssq", [P, 2])
        rstd = sb("rstd", [P, 2])
        epow = sb("epow", [P, 4])
        stats = sb("stats", [P, 4, 6])
        mv = sb("mv", [P, 4, 2])
        rs = sb("rs", [P, 4])
        ST = sb("ST", [P, 4, CH])
        STs = sb("STs", [TS, 4, TS])
        kT = sb("kT", [P, 256])
        y = sb("y", [P, 4, 64])
        ex = sb("ex", [P, 512])
        oT = sb("oT", [65, 4, TS])
        small = sb("small", [P, 64])
        sst = sb("sst", [P, 2, NB, 65])
        S_hg = sb("S_hg", [P, 2, 64])
        S_ml = sb("S_ml", [P, 2, 65])
        S_rt = sb("S_rt", [P, 64])
        lb = sb("lb", [P, 8])
        gb = sb("gb", [4, 8])
        m0 = sb("m0", [4, NB])
        mp = sb("mp", [4, NCH])

        class Carve:
            def __init__(self, name, size):
                self.t, self.at, self.size, self.name = sb(name, [P, size]), 0, size, name

            def take(self, *shape, rows=P):
                n = int(np.prod(shape))
                v = self.t[0:rows, self.at:self.at + n]
                self.at += n
                assert self.at <= self.size, (self.name, self.at)
                if len(shape) > 1:
                    names = "abcd"[:len(shape)]
                    v = v.rearrange(f"p ({' '.join(names)}) -> p {' '.join(names)}", **dict(zip(names[1:], shape[1:])))
                return v

        R1, R2 = Carve("r1", 8896), Carve("r2", 10200)
        xt, normw = R1.take(2, D), R1.take(D)
        cm_wide = R1.take(inp["c_masks"].shape[1])
        R1.at = 0
        hq, hk, hcum = R1.take(2, W), R1.take(2, W), R1.take(2, W)
        hv, hgate = R1.take(5, 256), R1.take(5, 256)
        at = R1.at
        E, QD = R1.take(10, 2, CH), R1.take(2, 2, CH)
        R1.at = at
        hf, hu = R1.take(2, W), R1.take(2, W)
        R1.at = 0
        rq, rk = R1.take(4, W), R1.take(W)
        rv, rgate = R1.take(5, 256), R1.take(5, 256)
        rtab, rtmp = R1.take(4, W), R1.take(2, HALF)
        mq, mk = R2.take(4, W), R2.take(2, W)
        mvv, mo, mgate = R2.take(5, 4, 65), R2.take(5, 256), R2.take(5, 256)
        ifc = R2.take(5, 8)
        rows = R2.take(5, W, rows=4)
        G_, SP_, M_, WK_, A_ = range(5)

        R2.at = 0
        cB, cBb, cCn, cCT = R2.take(2, 8, 16), R2.take(2, 8, 16), R2.take(2, 2, P), R2.take(2, 8, 16)
        cV, cW = R2.take(2, 8, 9, 16), R2.take(2, 8, 8, 16)
        cE = R2.take(2, 8, 64)
        at = R2.at
        ct = [R2.take(8 * 9 * 16) for _ in range(2)]
        R2.at = at
        cWT = R2.take(8, 2, P)
        cK = cW.rearrange("p r q s c -> p (r q s c)")[0:16, :].rearrange("p (g x) -> p g x", g=16)
        R2.at = 0
        ux, U = R2.take(2, W), R2.take(16, 72)
        sG = R2.take(2, 8, 64)
        at = R2.at
        sX, sE = R2.take(2, 8, 65), R2.take(2, 8, 64)
        R2.at = at
        yT = R2.take(2, W)
        R2.at = at + 8 * 65 * 2 + 1024
        sMx = R2.take(16 * P)
        sWT, sT = sMx.rearrange("p (q r x) -> p q r x", q=8, r=2), sMx.rearrange("p (g x) -> p g x", g=16)
        at = R2.at
        sV = R2.take(2, 8, P)
        R2.at = at
        stmp = [R2.take(8, 64) for _ in range(2)]
        R2.at = at
        yg = R2.take(2, W)
        R2.at = at + 2048
        wglu = R2.take(2, 256)
        sX0 = R2.take(2, 8, NB)
        sXf = R2.take(2, 8, NB)
        Yall = sG.rearrange("p r q b -> p (r q b)")
        Ys = sb("Ys", [64, 16, NB])
        gt = U.rearrange("p g b -> p (g b)")[:, 0:2 * W].rearrange("p (j w) -> p j w", j=2)
        s5c = sb("s5c", [P, DEPTH, 3, 8])
        s5v = sb("s5v", [P, 26, 16])
        s5i = sb("s5i", [P, 16], mybir.dt.int32)
        s5x = sb("s5x", [P, 2, 8])
        s5d = sb("s5d", [P, DEPTH, 2])
        s5p = sb("s5p", [P, 2, 16, 9])
        Tm = nc.dram_tensor("Tm", (DEPTH, 16, P, P), F32, kind="Internal").ap()
        WTm = nc.dram_tensor("WTm", (DEPTH, P, 16 * P), F32, kind="Internal").ap()
        VTm = nc.dram_tensor("VTm", (DEPTH, P, 2, 8, P), F32, kind="Internal").ap()
        Em = nc.dram_tensor("Em", (DEPTH, P, 1024), F32, kind="Internal").ap()
        ud = nc.dram_tensor("ud", (256, W), F32, kind="Internal").ap()
        yd = nc.dram_tensor("yd", (256, W), F32, kind="Internal").ap()

        gate_of = {"hg": hgate, "rt": rgate, "ml": mgate}
        x1 = nc.dram_tensor("x1", (SEQ + TS, D), F32, kind="Internal").ap()
        x2 = nc.dram_tensor("x2", (SEQ + TS, D), F32, kind="Internal").ap()

        def x_rows(x, n, t):
            return x[n % 2 * HALF + t * P:n % 2 * HALF + (t + 1) * P, :] if t < NCH else x[SEQ:SEQ + TS, :]

        def x_src(n, t):
            if n >= 2:
                return x_rows(x1, n, t)
            return x_rows(inp["x_prompt"][0], n, t) if t < NCH else inp["x_sample"].rearrange("b s d -> (b s) d")

        const_in = signal("const_in", range(9), 16)
        nw_in = signal("nw_in", [s[1] for s in plan if s[0] == "norm"] + ["final"], 16)
        xt_in = [signal(f"xt_in{s}", [k for k in all_tiles if tslot[k] == s], 16) for s in range(2)]
        ssq_done = signal("ssq_done", all_tiles)
        rstd_done = signal("rstd_done", all_tiles)
        h_done = signal("h_done", all_tiles)
        hhi_done = signal("hhi_done", [k + (g,) for k in norm_tiles for g in range(2)])
        y_out = [signal(f"y_out{s}", [k for k in final_tiles if tslot[k] == s], 16) for s in range(2)]
        wr_in = [signal(f"wr_in{s}", [k for k in w_loads if wslot[k] == s], 16) for s in range(2)]
        whi_done = signal("whi_done", in_blocks)
        wlo_done = signal("wlo_done", in_blocks)
        th_keys = [k for k in pieces if BLOCK[k[1]][4] == "av"]
        th_done = signal("th_done", th_keys)
        xo_in = [signal(f"xo_in{s}", [k for k in out_pieces if oslot[k] == s], 16) for s in range(3)]
        xo_sum = signal("xo_sum", out_pieces)
        xo_out = [signal(f"xo_out{s}", [k for k in out_pieces if oslot[k] == s], 16) for s in range(3)]
        rot_done = signal("rot_done", range(2 * DEPTH))
        ml_clear = signal("ml_clear", range(2 * DEPTH))
        tab_in = signal("tab_in", range(2 * DEPTH), 16)
        pool_done = Chain(nc, ctx, "pool_done")
        act_done = Chain(nc, ctx, "act_done")
        dve_done = Chain(nc, ctx, "dve_done")
        pool_setup = signal("pool_setup", ["all"])
        lb_exp = signal("lb_exp", ["in"])
        lb_done = signal("lb_done", ["diff", "all"])
        pre_act = signal("pre_act", [s + (i,) for s in pres for i in range(1 if s[0] == "mlpre" else 2 + s[1] // 2)])
        pre_dve = signal("pre_dve", [s + (i,) for s in pres for i in range(1 if s[0] == "mlpre" else 1 + s[1] // 2)])
        hg_mixes = [m for m in mixes if m[0] == "hg"]
        ml_mixes = [m for m in mixes if m[0] == "ml"]
        hg_diff = signal("hg_diff", hg_mixes)
        hg_exp = signal("hg_exp", hg_mixes)
        hg_prod = signal("hg_prod", hg_mixes)
        ex_add = signal("ex_add", ml_mixes)
        ex_exp = signal("ex_exp", ml_mixes)
        st_done = signal("st_done", mixes)
        mv_done = signal("mv_done", mixes)
        rs_done = signal("rs_done", mixes)
        y_done = signal("y_done", mixes)
        vexp_done = signal("vexp_done", [m + (h,) for m in samples for h in range(4)])
        vexp_used = signal("vexp_used", [m + (h,) for m in samples for h in range(4)])
        ss_parts = {"hg": 4, "ml": 8, "rt": 4}
        m_in = signal("m_in", range(DEPTH), 16)
        m_out = signal("m_out", [(l, i) for l in range(DEPTH) for i in range(2)], 16)
        ss_in = signal("ss_in", [m + (i,) for m in samples for i in range(ss_parts[m[0]])], 16)
        ss_new = signal("ss_new", samples)
        ss_out = signal("ss_out", [m + (i,) for m in samples for i in range(ss_parts[m[0]])], 16)
        last_prompt = [m for m in mixes if m[1] % 2 and m[2] == NCH - 1]
        ps_parts = {"hg": 4, "ml": 8, "rt": 1}
        ps_out = signal("ps_out", [m + (i,) for m in last_prompt for i in range(ps_parts[m[0]])], 16)
        state_zero = signal("state_zero", [(l, "hg") for l in range(DEPTH)])

        s5n = [s for s in plan if s[0] == "s5"]
        s5sets = [s for s in plan if s[0] == "s5set"]
        set_in = signal("set_in", [s + (i,) for s in s5sets for i in range(6)], 16)
        vec_in = signal("vec_in", range(9), 16)
        vec_act = signal("vec_act", ["sin"])
        vec_dve = signal("vec_dve", ["phase", "all"])
        set_dve = signal("set_dve", [s + (i,) for s in s5sets for i in ("E", "V", "W")])
        set_out = signal("set_out", [s + (i,) for s in s5sets for i in range(18)], 16)
        set_k = signal("set_k", s5sets)
        s5_in = {i: signal(f"s5_in_{i}", s5n, 16) for i in ("E", "W", "G", "T", "V", "Y")}
        s5_u = signal("s5_u", [s + (i,) for s in s5n for i in range(8 + 4 * (s[1] % 2))], 16)
        s5_us = signal("s5_us", s5n, 16)
        s5_xi = signal("s5_xi", [s + (i, b) for s in s5n if s[1] % 2 for i in range(2) for b in range(NB)], 16)
        s5_y = signal("s5_y", [s + (i,) for s in s5n for i in range(8 + 4 * (s[1] % 2))], 16)
        s5_clear = signal("s5_clear", s5n)
        s5_rot = signal("s5_rot", s5n)
        s5_lin = signal("s5_lin", s5n)
        s5_act = signal("s5_act", [s + (i,) for s in s5n for i in ("sq", "tanh")])
        s5_dve = signal("s5_dve", [s + (i,) for s in s5n for i in ("skip", "cube", "gelu", "mixed")])
        s5_out = signal("s5_out", [s + (i, b) for s in s5n if s[1] % 2 for i in range(2) for b in ["p", *range(NB)]], 16)

        def piece_psum(key):
            if BLOCK[key[1]][3] == "ch":
                width, c0 = (HALF, 0) if key[3] == 0 else (TS, HALF)
                return PB[bank_of[key]].t[:, 0:width], c0, width
            lo, hi = (0, P) if key[2] < NCH else (P - TS, P)
            return PB[bank_of[key]].t[lo:hi, 0:BLOCK[key[1]][2]], key[2], hi - lo

        def before(keys, key, back=1):
            i = keys.index(key)
            return keys[i - back] if i >= back else None

        def levels(c):
            return LEVELS if c < NCH else SLEV

        def split(ap, w):
            return ap.rearrange("p (n g w) -> p n g w", g=2, w=w)

        ctx.enter_context(nc.allow_non_contiguous_dma(reason="a few small rows of parameters and states"))
        block = ctx.enter_context(nc.Block())

        @block.sync
        def _(sp):
            sp.dma_start(const[:, :], inp["c_packed"]).then_inc(*const_in.inc(0))
            sp.dma_start(cm_wide, inp["c_masks"]).then_inc(*const_in.inc(1))
            sp.dma_start(lb[:, 0:4].rearrange("p (l j) -> p l j", l=2),
                         inp["hgrn_lb_logits"].rearrange("l (j p) -> p l j", p=P)).then_inc(*const_in.inc(2))
            sp.dma_start(gb[:, 0:2], inp["mlstm_b_i"].rearrange("l h -> h l")).then_inc(*const_in.inc(3))
            sp.dma_start(gb[:, 2:4], inp["mlstm_b_f"].rearrange("l h -> h l")).then_inc(*const_in.inc(4))

            loads = list(w_loads)

            def load_weights():
                k = loads.pop(0)
                prev = before(w_loads, k, 2)
                if prev is not None:
                    if prev[1] == "wo":
                        sp.wait_ge(*PB[bank_of[(prev[0], prev[2], tiles_of(prev[0])[-1])]].full.at((prev[0], prev[2], tiles_of(prev[0])[-1])))
                    else:
                        sp.wait_ge(*whi_done.at(prev))
                        sp.wait_ge(*wlo_done.at(prev))
                l = k[0] // 2
                if k[1] == "wo":
                    src, width = inp["w_out"][l][:, k[2] * 256:(k[2] + 1) * 256], 256
                else:
                    _, c0, width, _, _ = BLOCK[k[1]]
                    src = inp["w_in"][l][:, c0:c0 + width]
                sp.dma_start(wraw[:, wslot[k], :, 0:width], src.rearrange("(k p) c -> p k c", p=P)
                             ).then_inc(*wr_in[wslot[k]].inc(k))

            def load_until(i):
                while loads and len(w_loads) - len(loads) <= i:
                    load_weights()

            def load_x(k):
                n, t = k
                if k in final_tiles:
                    src = x_rows(x2, 1, NCH) if t == 2 * NCH else x_rows(x2, t // NCH, t % NCH)
                else:
                    src = x_src(n, t)
                prev = before(all_tiles, k, 2)
                if prev is not None:
                    if prev in final_tiles:
                        sp.wait_ge(*y_out[tslot[prev]].at(prev))
                    else:
                        sp.wait_ge(*PB[bank_of[("norm",) + prev + (1,)]].full.at(("norm",) + prev + (1,)))
                sp.dma_start(xt[0:P if t != (NCH if n != "final" else 2 * NCH) else TS, tslot[k], :], src).then_inc(*xt_in[tslot[k]].inc(k))

            def stored(n):
                for s in range(3):
                    ks = [k for k in out_pieces if k[0] <= n and oslot[k] == s]
                    sp.wait_ge(*xo_out[s].at(ks[-1]))

            def norm_weights(n):
                src = inp["final_norm_w"] if n == "final" else inp["norm_w"][n // 2]
                sp.dma_start(normw[:, :], src.rearrange("(o d) -> o d", o=1).broadcast_to([P, D])).then_inc(*nw_in.inc(n))

            if s5n:
                v3 = lambda i: s5v[:, i, :].rearrange("p (l q) -> p l q", l=DEPTH)
                for l in range(DEPTH):
                    sp.dma_start(v3(0)[:, l], inp["s5_lambda_re"][l].rearrange("(q a) p -> (a p) q", a=2)).then_inc(*vec_in.inc(4 * l))
                    sp.dma_start(v3(1)[:, l], inp["s5_lambda_im"][l].rearrange("(q a) p -> (a p) q", a=2)).then_inc(*vec_in.inc(4 * l + 1))
                    for a in range(2):
                        sp.dma_start(v3(2)[64 * a:64 * a + 64, l], inp["s5_log_dt"][l].rearrange("(o q a) -> a o q", a=2, o=1)[a].broadcast_to([64, 8])
                                     ).then_inc(*vec_in.inc(4 * l + 2 + a))
                sp.dma_start(s5d[:, :, :], inp["s5_D"].rearrange("l (j p) -> p l j", p=P)).then_inc(*vec_in.inc(8))

            def permuted(ap, t):
                a = ap.rearrange("(g c) w -> c g w", c=16)
                return a[:, :, t * 64:(t + 1) * 64] if t < 8 else a[:, :, HALF + (t - 8) * NB:HALF + (t - 7) * NB]

            for s in plan:
                if s[0] == "s5set":
                    l = s[1]
                    if l:
                        sp.wait_ge(*set_out.at(s5sets[0] + (17,)))
                    for ri, nm in enumerate(("re", "im")):
                        sp.dma_start(cB[:, ri], inp["s5_B_" + nm][l].rearrange("(q a) p c -> (a p) q c", a=2)).then_inc(*set_in.inc(s + (ri,)))
                        for d in range(2):
                            sp.dma_start(cCn[:, ri, :, 64 * d:64 * d + 64], inp["s5_C_" + nm][l].rearrange("(f g) c p -> (g c) f p", f=2)
                                         ).then_inc(*set_in.inc(s + (2 + 2 * ri + d,)))
                    sp.wait_ge(*set_dve.at(s + ("E",)))
                    sp.dma_start(Em[l], cE.rearrange("p r q b -> p (r q b)")).then_inc(*set_out.inc(s + (0,)))
                    sp.wait_ge(*set_dve.at(s + ("V",)))
                    sp.dma_start(VTm[l].rearrange("p r q x -> p (r q) x"),
                                 cV.rearrange("p r q j c -> p (r q) (j c)")[:, :, 16:144]).then_inc(*set_out.inc(s + (1,)))
                    sp.wait_ge(*scores.free.at(s + (1,)))
                    sp.dma_start(WTm[l], cWT.rearrange("p q r x -> p (q r x)")).then_inc(*set_out.inc(s + (2,)))
                    sp.wait_ge(*scores.free.at(s + (3,)))
                    for t in range(8):
                        T_rows = Tm[l][:, 16 * t:16 * t + 16, :].rearrange("g c x -> c g x")
                        sp.dma_start(T_rows[:, :, 16 * t:], cK[:, :, 0:P - 16 * t]).then_inc(*set_out.inc(s + (3 + t,)))
                        if t:
                            z = mixT[0:16, :, :].rearrange("p k w -> p (k w)")[:, 0:16 * 16 * t].rearrange("p (g x) -> p g x", g=16)
                            sp.dma_start(T_rows[:, :, 0:16 * t], z).then_inc(*set_out.inc(s + (10 + t,)))
                elif s[0] == "s5":
                    n, l = s[1], s[1] // 2
                    odd = n % 2
                    nt = 8 + 4 * odd
                    Wn = HALF + TS * odd
                    if s == s5n[0]:
                        sp.wait_ge(*set_out.at(s5sets[-1] + (17,)))
                    mls = [m for m in mixes if m[0] == "ml" and m[1] == n]
                    if mls:
                        sp.wait_ge(*y_done.at(mls[-1]))
                        sp.wait_ge(*aux.full.at(mls[-1] + ("mixed",)))
                        if odd:
                            sp.wait_ge(*m_out.at((l, 1)))
                    sp.dma_start(sE.rearrange("p r q b -> p (r q b)"), Em[l]).then_inc(*s5_in["E"].inc(s))
                    sp.dma_start(sMx, WTm[l]).then_inc(*s5_in["W"].inc(s))
                    for k in [k for k in pieces if k[:2] == (n, "s5_x")]:
                        sp.wait_ge(*PB[bank_of[k]].free.at(k))
                    sp.dma_start(ud[:, 0:Wn].rearrange("(j p) w -> p j w", p=P), ux[:, :, 0:Wn]).then_inc(*s5_us.inc(s))
                    sp.wait_ge(*s5_us.at(s))
                    sp.wait_ge(*s5_clear.at(s))
                    for t in range(nt):
                        dst = U[16 * t:16 * t + 16, :, 0:64] if t < 8 else U[16 * (t - 4):16 * (t - 3), :, 64:72]
                        sp.dma_start(dst, permuted(ud, t)).then_inc(*s5_u.inc(s + (t,)))
                    if odd:
                        for ri, nm in enumerate(("re", "im")):
                            for b in range(NB):
                                v = inp["state_s5_" + nm][l, b].rearrange("(q a) p -> (a p) q", a=2)
                                sp.dma_start(sX0[:, ri, :, b], v).then_inc(*s5_xi.inc(s + (ri, b)))
                    sp.dma_start(wglu, inp["s5_w_glu"][l].rearrange("(k p) c -> p k c", p=P)).then_inc(*s5_in["G"].inc(s))
                    sp.wait_ge(*scores.full.at(s + (0,)))
                    if odd:
                        sp.wait_ge(*upd.full.at(s + ("w",)))
                    sp.dma_start(sT, Tm[l].rearrange("g s x -> s g x")).then_inc(*s5_in["T"].inc(s))
                    sp.wait_ge(*s5_rot.at(s))
                    sp.dma_start(sV, VTm[l]).then_inc(*s5_in["V"].inc(s))
                    sp.wait_ge(*scores.free.at(s + (1,)))
                    if odd:
                        sp.wait_ge(*aux.free.at(s + ("y",)))
                    for t in range(nt):
                        src = (Yall[16 * t:16 * t + 16, :].rearrange("p (g b) -> p g b", g=16) if t < 8
                               else Ys[16 * (t - 8):16 * (t - 7), :, :])
                        sp.dma_start(permuted(yd, t), src).then_inc(*s5_y.inc(s + (t,)))
                    sp.wait_ge(*s5_y.at(s + (nt - 1,)))
                    sp.dma_start(yT[:, :, 0:Wn], yd[:, 0:Wn].rearrange("(j p) w -> p j w", p=P)).then_inc(*s5_in["Y"].inc(s))
                    if odd:
                        for ri, nm in enumerate(("re", "im")):
                            sp.dma_start(out["p_s5_" + nm][l, 0].rearrange("(q a) p -> (a p) q", a=2), s5x[:, ri, :]).then_inc(*s5_out.inc(s + (ri, "p")))
                            for b in range(NB):
                                sp.dma_start(out["d_s5_" + nm][l, b].rearrange("(q a) p -> (a p) q", a=2), sXf[:, ri, :, b]).then_inc(*s5_out.inc(s + (ri, b)))
                elif s[0] == "norm":
                    n = s[1]
                    if n >= 1:
                        ks = [m for m in mixes if m[1] < n and m[0] != "ml"]
                        if ks:
                            sp.wait_ge(*y_done.at(ks[-1]))
                            sp.wait_ge(*upd.free.at([k for k in upd_keys if k[:3] == ks[-1]][-1]))
                    if n >= 2:
                        stored(n - 2)
                    norm_weights(n)
                    for t in tiles_of(n):
                        load_x((n, t))
                        if t == 1:
                            load_until([k[0] for k in w_loads].index(n) + 1)
                elif s[0] == "proj":
                    n = s[1]
                    load_until(w_loads.index(s[1:]) + 2)
                    if s[2] == "rt_qk":
                        m = [m for m in hg_mixes if m[1] == n]
                        if m:
                            sp.wait_ge(*y_done.at(m[-1]))
                        else:
                            sp.wait_ge(*PB[bank_of[("norm", n, tiles_of(n)[-1], 1)]].full.at(("norm", n, tiles_of(n)[-1], 1)))
                        sp.dma_start(rtab, inp["c_rot"][n % 2].rearrange("p (k w) -> p k w", k=4)).then_inc(*tab_in.inc(n))
                elif s[0] == "mlpre" and s[1] % 2:
                    l = s[1] // 2
                    if l:
                        sp.wait_ge(*pre_dve.at(("mlpre", s[1] - 2, 0)))
                    sp.dma_start(m0[:, :], inp["state_mlstm_m"][l].rearrange("b h -> h b")).then_inc(*m_in.inc(l))
                    sp.wait_ge(*pre_dve.at(s + (0,)))
                    sp.dma_start(out["d_mlstm_m"][l].rearrange("b h -> h b"),
                                 rows[:, M_, HALF + DSEQ - 1:W:DSEQ]).then_inc(*m_out.inc((l, 0)))
                    sp.dma_start(out["p_mlstm_m"][l].rearrange("b h -> h b"), rows[:, M_, HALF - 1:HALF]).then_inc(*m_out.inc((l, 1)))
                elif s in samples:
                    l = s[1] // 2
                    i = samples.index(s)
                    if i:
                        prev = samples[i - 1]
                        sp.wait_ge(*ss_out.at(prev + (ss_parts[prev[0]] - 1,)))

                    def moves():
                        if s[0] == "rt":
                            for h in range(4):
                                yield sst[32 * h:32 * h + 32, 0, :, 0:64], inp["state_ret"][l, :, h].rearrange("b k v -> k b v"), out["d_ret"][l, :, h].rearrange("b k v -> k b v")
                        else:
                            name, oname = ("state_hgrn", "d_hgrn") if s[0] == "hg" else ("state_mlstm_C", "d_mlstm_C")
                            for h in range(4):
                                v = sst[h % 2 * 64:h % 2 * 64 + 64, h // 2, :, 0:64]
                                yield v, inp[name][l, :, h].rearrange("b k v -> k b v"), out[oname][l, :, h].rearrange("b k v -> k b v")
                            if s[0] == "ml":
                                for h in range(4):
                                    v = sst[h % 2 * 64:h % 2 * 64 + 64, h // 2, :, 64:65]
                                    r = lambda a: a[l, :, h, :].rearrange("b (k o) -> k b o", o=1)
                                    yield v, r(inp["state_mlstm_n"]), r(out["d_mlstm_n"])
                    k = 0
                    for view, src, dst in moves():
                        sp.dma_start(view, src).then_inc(*ss_in.inc(s + (k,)))
                        k += 1
                    sp.wait_ge(*ss_new.at(s))
                    k = 0
                    for view, src, dst in moves():
                        sp.dma_start(dst, view).then_inc(*ss_out.inc(s + (k,)))
                        k += 1
                elif s in last_prompt:
                    l = s[1] // 2
                    sp.wait_ge(*upd.free.at(s + ("U",)))
                    if s[0] == "hg":
                        for h in range(4):
                            sp.dma_start(out["p_hgrn"][l, 0, h], S_hg[h % 2 * 64:h % 2 * 64 + 64, h // 2, :]).then_inc(*ps_out.inc(s + (h,)))
                    elif s[0] == "rt":
                        sp.dma_start(out["p_ret"][l, 0].rearrange("h k v -> (h k) v"), S_rt[:, :]).then_inc(*ps_out.inc(s + (0,)))
                    else:
                        for h in range(4):
                            v = S_ml[h % 2 * 64:h % 2 * 64 + 64, h // 2, :]
                            sp.dma_start(out["p_mlstm_C"][l, 0, h], v[:, 0:64]).then_inc(*ps_out.inc(s + (2 * h,)))
                            sp.dma_start(out["p_mlstm_n"][l, 0, h].rearrange("(k o) -> k o", o=1), v[:, 64:65]).then_inc(*ps_out.inc(s + (2 * h + 1,)))
                elif s[0] == "out":
                    n = s[1]
                    for i, k in enumerate(outs_of(n)):
                        if k[2] == tiles_of(n)[0] and k[1] > 0 or i == 0:
                            if k[1] < 3:
                                load_until(w_loads.index((n, "wo", k[1])) + 1)
                        slot, prev = oslot[k], before(out_pieces, k, 3)
                        if prev is not None:
                            sp.wait_ge(*xo_out[slot].at(prev))
                        c = slice(k[1] * 256, (k[1] + 1) * 256)
                        sp.dma_start(xo[0:chunk_len(k[2]), slot, :], x_src(n, k[2])[:, c]).then_inc(*xo_in[slot].inc(k))
                        ks = outs_of(n)
                        for kk in ([ks[i - 2]] if i >= 2 else []) + (ks[-2:] if i == len(ks) - 1 else []):
                            sp.wait_ge(*xo_sum.at(kk))
                            sp.dma_start(x_rows(x1 if n < 2 else x2, n, kk[2])[:, kk[1] * 256:(kk[1] + 1) * 256],
                                         xo[0:chunk_len(kk[2]), oslot[kk], :]).then_inc(*xo_out[oslot[kk]].inc(kk))
                elif s[0] == "final":
                    stored(2 * DEPTH - 1)
                    norm_weights("final")
                    for k in final_tiles:
                        load_x(k)
                        for kk in ([final_tiles[k[1] - 1]] if k[1] else []) + ([k] if k == final_tiles[-1] else []):
                            t = kk[1]
                            sp.wait_ge(*h_done.at(kk))
                            dst = (out["y_sample"].rearrange("b s d -> (b s) d") if t == 2 * NCH
                                   else out["y_prompt"][0, t * P:(t + 1) * P, :])
                            sp.dma_start(dst, xt[0:TS if t == 2 * NCH else P, tslot[kk], :]).then_inc(*y_out[tslot[kk]].inc(kk))
            for sgl in [*y_out, ss_out, ps_out, m_out, s5_out]:
                if sgl.fired:
                    sp.wait_ge(*sgl.at(sgl.keys[-1]))

        @block.gpsimd
        def _(pool):
            for v, x in ((epow[:, :], -0.5), (ST[:, :, :], 0.0), (STs[:, :, :], 0.0), (ssq[:, :], 0.0), (mixT[:, :, :], 0.0)):
                nc.gpsimd.memset(v, x).then_inc(*pool_done.inc())
            pool.wait_ge(*pool_done.now())
            nc.gpsimd.memset(small[:, :], 0.0).then_inc(*pool_setup.inc("all"))

            blocks = list(in_blocks)

            def split_low():
                b = blocks.pop(0)
                prev = before(in_blocks, b, 2)
                if prev is not None:
                    pool.wait_ge(*PB[bank_of[last_piece[prev]]].full.at(last_piece[prev]))
                pool.wait_ge(*whi_done.at(b))
                width = BLOCK[b[1]][2]
                nc.gpsimd.tensor_tensor(wlo[:, hslot[b], :, 0:width], wraw[:, wslot[b], :, 0:width],
                                        whi[:, hslot[b], :, 0:width].bitcast(F32), ALU.subtract).then_inc(*wlo_done.inc(b))

            def power(k):
                s = tslot[k]
                pool.wait_ge(*ssq_done.at(k))
                nc.gpsimd.tensor_scalar(rstd[:, s:s + 1], ssq[:, s:s + 1], 1.0 / D, EPS, ALU.mult, ALU.add).then_inc(*pool_done.inc())
                pool.wait_ge(*pool_done.now())
                nc.gpsimd.tensor_tensor(rstd[:, s:s + 1], rstd[:, s:s + 1], epow[:, 0:1], ALU.pow).then_inc(*rstd_done.inc(k))

            for s in plan:
                if s[0] == "norm":
                    for t in tiles_of(s[1]):
                        power((s[1], t))
                    split_low()
                elif s[0] == "proj":
                    if blocks and blocks[0][0] == s[1]:
                        split_low()
                elif s[0] == "s5":
                    n = s[1]
                    if s == s5n[0]:
                        pool.wait_ge(*set_out.at(s5sets[-1] + (17,)))
                    k = last_piece[(n, "s5_x")]
                    pool.wait_ge(*PB[bank_of[k]].full.at(k))
                    mls = [m for m in mixes if m[0] == "ml" and m[1] == n]
                    if mls:
                        pool.wait_ge(*y_done.at(mls[-1]))
                        pool.wait_ge(*aux.full.at(mls[-1] + ("mixed",)))
                    nc.gpsimd.memset(U[0:64, :, 64:72], 0.0).then_inc(*s5_clear.inc(s))
                elif s in mixes:
                    T = chunk_len(s[2])
                    pool.wait_ge(*mv_done.at(s))
                    nc.gpsimd.tensor_scalar(rs[0:T, :], mv[0:T, :, 1], EPS if s[0] == "rt" else 4 * EPS, 4.0,
                                            ALU.add, ALU.mult).then_inc(*pool_done.inc())
                    pool.wait_ge(*pool_done.now())
                    nc.gpsimd.tensor_tensor(rs[0:T, :], rs[0:T, :], epow[0:T, :], ALU.pow).then_inc(*rs_done.inc(s))
                elif s[0] == "final":
                    for k in final_tiles:
                        power(k)

        @block.scalar
        def _(act):
            act.wait_ge(*pool_setup.at("all"))
            act.wait_ge(*const_in.at(4))
            blocks = list(in_blocks)

            def split_high():
                b = blocks.pop(0)
                prev = before(in_blocks, b, 2)
                if prev is not None:
                    act.wait_ge(*PB[bank_of[last_piece[prev]]].full.at(last_piece[prev]))
                act.wait_ge(*wr_in[wslot[b]].at(b))
                width = BLOCK[b[1]][2]
                nc.scalar.activation(whi[:, hslot[b], :, 0:width], wraw[:, wslot[b], :, 0:width], ACT.Copy).then_inc(*whi_done.inc(b))

            def square_sum(k):
                act.wait_ge(*xt_in[tslot[k]].at(k))
                prev = before(all_tiles, k, 2)
                if prev is not None:
                    act.wait_ge(*rstd_done.at(prev))
                r = P if k[1] != (NCH if k[0] != "final" else 2 * NCH) else TS
                if before(all_tiles, k):
                    act.wait_ge(*ssq_done.at(before(all_tiles, k)))
                nc.scalar.activation(th[0:r, :, :].rearrange("p a b -> p (a b)"), xt[0:r, tslot[k], :], ACT.Square,
                                     accum_out=ssq[0:r, tslot[k]:tslot[k] + 1]).then_inc(*ssq_done.inc(k))

            act.wait_ge(*lb_done.at("diff"))
            nc.scalar.activation(lb[:, 4:6], lb[:, 4:6], ACT.Exp).then_inc(*act_done.inc())
            act.wait_ge(*act_done.now())
            nc.scalar.activation(lb[:, 6:8], lb[:, 6:8], ACT.Exp).then_inc(*lb_exp.inc("in"))

            def take_piece(k):
                n, name = k[:2]
                bank = PB[bank_of[k]]
                ps, at, ln = piece_psum(k)
                kind = BLOCK[name][4]
                if kind == "v":
                    return
                if name == "s5_x" and k == [q for q in pieces if q[:2] == k[:2]][0]:
                    mls = [m for m in mixes if m[0] == "ml" and m[1] == n]
                    if n % 2 and mls:
                        act.wait_ge(*m_out.at((n // 2, 1)))
                    if not n:
                        act.wait_ge(*set_out.at(s5sets[-1] + (17,)))
                act.wait_ge(*bank.full.at(k))
                if kind == "av":
                    i = th_keys.index(k)
                    if i >= 2:
                        act.wait_ge(*PB[bank_of[th_keys[i - 2]]].free.at(th_keys[i - 2]))
                    v = th[:, i % 2, 0:ln]
                    if name == "ml_ifg":
                        nc.scalar.activation(ifc[0:ln, at, :], ps[:, 0:8], ACT.Copy).then_inc(*act_done.inc())
                        ps = ps[:, 8:264]
                    if BLOCK[name][3] == "tok":
                        v = th[0:ln, i % 2, 0:256]
                    nc.scalar.activation(v, ps, ACT.Tanh, scale=0.5).then_inc(*th_done.inc(k))
                    return
                done = bank.free.inc(k)
                if name == "hg_f":
                    nc.scalar.activation(hf[:, k[2], at:at + ln], ps, ACT.Copy).then_inc(*done)
                elif name == "ml_q":
                    act.wait_ge(*ml_clear.at(n))
                    for par in range(2):
                        r = slice(par * 64, par * 64 + 64)
                        nc.scalar.activation(mq[r, 2 * k[2] + par, at:at + ln], ps[r, :], ACT.Copy).then_inc(
                            *(done if par else act_done.inc()))
                elif name == "ml_k":
                    nc.scalar.activation(mk[:, k[2], at:at + ln], ps, ACT.Copy, scale=0.125).then_inc(*done)
                elif name == "ml_v":
                    nc.scalar.activation(mvv[0:ln, at, :, 0:64], ps.rearrange("p (h v) -> p h v", h=4), ACT.Copy).then_inc(*done)
                elif name == "ml_o":
                    nc.scalar.activation(mo[0:ln, at, :], ps, ACT.Tanh, scale=0.5).then_inc(*done)
                elif name == "s5_x":
                    tau = 8 if ln == HALF else DSEQ
                    nc.scalar.activation(ux[:, k[2], at:at + ln].rearrange("p (t b) -> p t b", t=tau), ps.rearrange("p (b t) -> p t b", t=tau),
                                         ACT.Copy).then_inc(*done)
                elif name in ("hg_i", "rt_v"):
                    nc.scalar.activation((hv if name == "hg_i" else rv)[0:ln, at, :], ps, ACT.Copy).then_inc(*done)

            for s in plan:
                if s[0] == "norm":
                    n = s[1]
                    if th_keys and n:
                        ks = [k for k in th_keys if k[0] < n]
                        act.wait_ge(*PB[bank_of[ks[-1]]].free.at(ks[-1]))
                        if len(ks) > 1:
                            act.wait_ge(*PB[bank_of[ks[-2]]].free.at(ks[-2]))
                    ts = list(tiles_of(n))
                    square_sum((n, 0))
                    for t in ts:
                        if t + 1 in ts:
                            square_sum((n, t + 1))
                        r = chunk_len(t)
                        for g in range(2):
                            u = ("norm", n, t, g)
                            act.wait_ge(*PB[bank_of[u]].full.at(u))
                            nc.scalar.activation(hhi[:, 4 * g:4 * g + 4, t * P:t * P + r],
                                                 PB[bank_of[u]].t.rearrange("p (k c) -> p k c", k=4)[:, :, 0:r],
                                                 ACT.Copy).then_inc(*hhi_done.inc((n, t, g)))
                    split_high()
                elif s[0] == "proj":
                    if blocks and blocks[0][0] == s[1]:
                        split_high()
                    for k in pieces:
                        if k[:2] == s[1:]:
                            take_piece(k)
                elif s[0] == "s5set":
                    l = s[1]
                    if not l:
                        act.wait_ge(*vec_dve.at("phase"))
                        ph, sn, cs = (s5v[:, 14 + 2 * i:16 + 2 * i, :] for i in range(3))
                        nc.scalar.activation(sn, ph, ACT.Sin, scale=0.5).then_inc(*act_done.inc())
                        nc.scalar.activation(ph, ph, ACT.Abs).then_inc(*act_done.inc())
                        act.wait_ge(*act_done.now())
                        nc.scalar.activation(cs, ph, ACT.Sin, scale=-0.5, bias=C("halfpi")).then_inc(*vec_act.inc("sin"))
                    act.wait_ge(*aux.full.at(s + ("C",)))
                    for ri in range(2):
                        for f in range(2):
                            for a in range(2):
                                src = aux.t[64 * a:64 * a + 64, (2 * ri + f) * P:(2 * ri + f + 1) * P].rearrange("p (q a c) -> p q a c", q=4, a=2)[:, :, a, :]
                                fin = ri == f == a == 1
                                nc.scalar.activation(cCT[64 * a:64 * a + 64, ri, 4 * f:4 * f + 4, :], src, ACT.Copy).then_inc(
                                    *(aux.free.inc(s + ("C",)) if fin else act_done.inc()))
                    for ri in range(2):
                        act.wait_ge(*scores.full.at(s + (ri,)))
                        for b in range(2):
                            nc.scalar.activation(cWT[:, 4 * b:4 * b + 4, ri, :], scores.t[:, b, :].rearrange("p (q x) -> p q x", q=4), ACT.Copy).then_inc(
                                *(scores.free.inc(s + (ri,)) if b else act_done.inc()))
                    for r in range(2):
                        act.wait_ge(*scores.full.at(s + (2 + r,)))
                        for a in range(2):
                            dst = cK.rearrange("p (q a) x -> p q a x", a=2)[:, 4 * r:4 * r + 4, a, :]
                            nc.scalar.activation(dst, scores.t[0:16, a, :].rearrange("p (q x) -> p q x", q=4), ACT.Copy).then_inc(
                                *(scores.free.inc(s + (2 + r,)) if a else act_done.inc()))
                elif s[0] == "s5":
                    n = s[1]
                    odd = n % 2
                    Wn = HALF + TS * odd
                    k = s + (1,)
                    act.wait_ge(*scores.full.at(k))
                    if odd:
                        act.wait_ge(*aux.full.at(s + ("y",)))
                    Yv = Yall.rearrange("p (q a b) -> p q a b", q=8, a=2)
                    Ysv = Ys.rearrange("p (q a) b -> p q a b", a=2)
                    for a in range(2):
                        nc.scalar.activation(Yv[:, :, a, :], scores.t[:, a, :].rearrange("p (q b) -> p q b", q=8), ACT.Copy).then_inc(
                            *(scores.free.inc(k) if a else act_done.inc()))
                    if odd:
                        act.wait_ge(*upd.full.at(s + ("y",)))
                        nc.scalar.activation(Ysv[:, :, 0, :], upd.t[0:64, 0:8 * NB].rearrange("p (q b) -> p q b", q=8), ACT.Copy).then_inc(*upd.free.inc(s + ("y",)))
                        nc.scalar.activation(Ysv[:, :, 1, :], aux.t[0:64, 0:8 * NB].rearrange("p (q b) -> p q b", q=8), ACT.Copy).then_inc(*aux.free.inc(s + ("y",)))
                    act.wait_ge(*s5_dve.at(s + ("skip",)))
                    nc.scalar.activation(gt[:, :, 0:Wn], yT[:, :, 0:Wn], ACT.Square).then_inc(*s5_act.inc(s + ("sq",)))
                    act.wait_ge(*s5_dve.at(s + ("cube",)))
                    nc.scalar.activation(gt[:, :, 0:Wn], gt[:, :, 0:Wn], ACT.Tanh, scale=(2 / np.pi) ** 0.5).then_inc(*s5_act.inc(s + ("tanh",)))
                    k = s + (2,)
                    act.wait_ge(*scores.full.at(k))
                    for j in range(2):
                        nc.scalar.activation(gt[:, j, 0:HALF], scores.t[:, j, :], ACT.Tanh, scale=0.25).then_inc(
                            *(scores.free.inc(k) if j else act_done.inc()))
                    if odd:
                        k = s + ("glu",)
                        act.wait_ge(*upd.full.at(k))
                        nc.scalar.activation(gt[:, :, HALF:W], upd.t[:, 0:2 * TS].rearrange("p (j w) -> p j w", j=2), ACT.Tanh, scale=0.25).then_inc(*upd.free.inc(k))
                elif s[0] == "hgpre":
                    n, Wn = s[1], HALF + TS * (s[1] % 2)
                    act.wait_ge(*act_done.now())
                    f, u, cum, kk = hf[:, :, 0:Wn], hu[:, :, 0:Wn], hcum[:, :, 0:Wn], hk[:, :, 0:Wn]
                    lastf = last_piece[(n, "hg_f")]
                    act.wait_ge(*PB[bank_of[lastf]].free.at(lastf))
                    lf2 = [k for k in pieces if k[:2] == (n, "hg_f")]
                    for k in lf2:
                        act.wait_ge(*PB[bank_of[k]].free.at(k))
                    nc.scalar.activation(u, f, ACT.Abs).then_inc(*act_done.inc())
                    act.wait_ge(*act_done.now())
                    nc.scalar.activation(u, u, ACT.Exp, scale=-1.0).then_inc(*act_done.inc())
                    act.wait_ge(*act_done.now())
                    nc.scalar.activation(u, u, ACT.Ln, bias=1.0).then_inc(*pre_act.inc(s + (0,)))
                    act.wait_ge(*pre_dve.at(s + (0,)))
                    if n // 2:
                        nc.scalar.activation(u, cum, ACT.Exp).then_inc(*act_done.inc())
                    nc.scalar.activation(kk, f, ACT.Exp).then_inc(*pre_act.inc(s + (1,)))
                    if n // 2:
                        act.wait_ge(*pre_dve.at(s + (1,)))
                        nc.scalar.activation(cum, u, ACT.Ln).then_inc(*pre_act.inc(s + (2,)))
                elif s[0] == "mlpre":
                    n, l = s[1], s[1] // 2
                    act.wait_ge(*scores.full.at(s + (0,)))
                    nc.scalar.activation(rows[:, G_, 0:HALF], scores.t[0:4, 0, :], ACT.Identity, bias=gb[:, l:l + 1]).then_inc(*act_done.inc())
                    nc.scalar.activation(rows[:, SP_, 0:HALF], scores.t[0:4, 1, :], ACT.Identity, bias=gb[:, 2 + l:3 + l]).then_inc(*scores.free.inc(s + (0,)))
                    act.wait_ge(*scores.free.at(s + (0,)))
                    Wn = HALF
                    if n % 2:
                        Wn = W
                        act.wait_ge(*upd.full.at(s + ("s",)))
                        nc.scalar.activation(rows[:, G_, HALF:W], upd.t[0:4, 0:TS], ACT.Identity, bias=gb[:, l:l + 1]).then_inc(*act_done.inc())
                        nc.scalar.activation(rows[:, SP_, HALF:W], upd.t[0:4, TS:2 * TS], ACT.Identity, bias=gb[:, 2 + l:3 + l]).then_inc(*upd.free.inc(s + ("s",)))
                        act.wait_ge(*upd.free.at(s + ("s",)))
                    act.wait_ge(*act_done.now())
                    m = rows[:, M_, 0:Wn]
                    nc.scalar.activation(m, rows[:, SP_, 0:Wn], ACT.Abs).then_inc(*act_done.inc())
                    act.wait_ge(*act_done.now())
                    nc.scalar.activation(m, m, ACT.Exp, scale=-1.0).then_inc(*act_done.inc())
                    act.wait_ge(*act_done.now())
                    nc.scalar.activation(m, m, ACT.Ln, bias=1.0).then_inc(*pre_act.inc(s + (0,)))
                elif s in mixes:
                    br, n, c = s
                    T = chunk_len(c)
                    if br == "hg":
                        act.wait_ge(*hg_diff.at(s))
                        for v in ([E[:, 0:8]] if c < NCH else [E[:, 0:2], E[:, 7:8]]):
                            v = v[:, :, :, 0:T]
                            for j in range(2):
                                nc.scalar.activation(v[:, :, j], v[:, :, j], ACT.Abs).then_inc(*act_done.inc())
                            act.wait_ge(*act_done.now())
                            for j in range(2):
                                nc.scalar.activation(v[:, :, j], v[:, :, j], ACT.Exp, scale=-1.0).then_inc(*act_done.inc())
                        nc.scalar.activation(E[:, 8, :, 0:T], hcum[:, :, cols(c)], ACT.Exp).then_inc(*hg_exp.inc(s))
                    turn, tk = aux.t, s + ("turn",)
                    if before(mixes, s):
                        act.wait_ge(*y_done.at(before(mixes, s)))
                    act.wait_ge(*aux.full.at(tk))
                    if br == "ml":
                        nb = 1 if c < NCH else NB
                        g, sp_, em, wk, cs = (small[:, 4 * i:4 * i + 4] for i in range(5))
                        cs = small[:, 16:16 + 2 * nb]
                        nc.scalar.activation(small[0:T, 0:4], turn[0:T, 256:260], ACT.Copy).then_inc(*act_done.inc())
                        nc.scalar.activation(small[0:T, 4:8], turn[0:T, 260:264], ACT.Exp).then_inc(*act_done.inc())
                        nc.scalar.activation(small[0:T, 8:12], turn[0:T, 264:268], ACT.Exp, scale=-1.0).then_inc(*act_done.inc())
                        nc.scalar.activation(small[0:T, 12:16], turn[0:T, 268:272], ACT.Exp).then_inc(*act_done.inc())
                        nc.scalar.activation(cs, turn[:, 272:272 + 2 * nb], ACT.Exp).then_inc(*act_done.inc())
                        act.wait_ge(*act_done.now())
                        for h in range(4):
                            nc.scalar.activation(kT[0:T, h * 64:h * 64 + 64], turn[0:T, h * 64:h * 64 + 64], ACT.Copy,
                                                 scale=small[0:T, 12 + h:13 + h]).then_inc(*(aux.free.inc(tk) if h == 3 else act_done.inc()))
                        act.wait_ge(*ex_add.at(s))
                        for h in range(4):
                            v = ex[0:T, h * T:h * T + T]
                            nc.scalar.activation(v, v, ACT.Exp, bias=small[0:T, h:h + 1]).then_inc(*(ex_exp.inc(s) if h == 3 else act_done.inc()))
                    elif br == "hg":
                        nc.scalar.activation(small[0:T, 0:4], turn[0:T, 256:260], ACT.Copy).then_inc(*act_done.inc())
                        nc.scalar.activation(kT[0:T, :], turn[0:T, 0:256], ACT.Copy).then_inc(*aux.free.inc(tk))
                    else:
                        nc.scalar.activation(kT[0:T, 0:128], turn[0:T, 0:128], ACT.Copy).then_inc(*aux.free.inc(tk))
                    if c == NCH:
                        act.wait_ge(*upd.full.at(s + ("inter",)))
                        r = 65 if br == "ml" else 64
                        nc.scalar.activation(oT[0:r, :, :], upd.t[0:r, 0:128].rearrange("p (h t) -> p h t", h=4), ACT.Copy).then_inc(*upd.free.inc(s + ("inter",)))
                    mk_ = s + ("mixed",)
                    act.wait_ge(*aux.full.at(mk_))
                    nc.scalar.activation(mixT[:, mix_tile[br]:mix_tile[br] + 2, cols(c)],
                                         aux.t[:, 0:256].rearrange("p (j t) -> p j t", j=2)[:, :, 0:T], ACT.Copy).then_inc(*aux.free.inc(mk_))
                elif s[0] == "final":
                    for k in final_tiles:
                        square_sum(k)

        @block.vector
        def _(dve):
            keep_phase = []

            def settle():
                dve.wait_ge(*dve_done.now())

            dve.wait_ge(*const_in.at(4))
            mx = small[:, 32:34]
            dve.wait_ge(*pool_setup.at("all"))
            nc.vector.tensor_copy(cm[:, :], cm_wide).then_inc(*dve_done.inc())
            nc.vector.tensor_tensor(mx, lb[:, 0:2], lb[:, 2:4], ALU.max).then_inc(*dve_done.inc())
            settle()
            nc.vector.tensor_tensor(lb[:, 4:6], lb[:, 0:2], mx, ALU.subtract).then_inc(*dve_done.inc())
            nc.vector.tensor_tensor(lb[:, 6:8], lb[:, 2:4], mx, ALU.subtract).then_inc(*lb_done.inc("diff"))
            dve.wait_ge(*lb_exp.at("in"))
            nc.vector.tensor_tensor(mx, lb[:, 4:6], lb[:, 6:8], ALU.add).then_inc(*dve_done.inc())
            settle()
            nc.vector.reciprocal(mx, mx).then_inc(*dve_done.inc())
            settle()
            nc.vector.tensor_tensor(lb[:, 0:2], lb[:, 6:8], mx, ALU.mult).then_inc(*dve_done.inc())
            nc.vector.tensor_tensor(lb[:, 2:4], lb[:, 4:6], mx, ALU.mult).then_inc(*lb_done.inc("all"))
            dve.wait_ge(*lb_done.at("all"))

            def scale_rows(k):
                sl = tslot[k]
                r = P if k[1] != (NCH if k[0] != "final" else 2 * NCH) else TS
                dve.wait_ge(*rstd_done.at(k))
                nc.vector.scalar_tensor_tensor(xt[0:r, sl, :], xt[0:r, sl, :], rstd[0:r, sl:sl + 1], normw[0:r, :],
                                               ALU.mult, ALU.mult).then_inc(*h_done.inc(k))

            def take_piece(k):
                n, name = k[:2]
                bank = PB[bank_of[k]]
                ps, at, ln = piece_psum(k)
                kind = BLOCK[name][4]
                if kind == "a":
                    return
                if kind == "av":
                    dve.wait_ge(*th_done.at(k))
                    i = th_keys.index(k) % 2
                    if name in ("hg_q", "s5_g"):
                        v, dst = th[:, i, 0:ln], (hq if name == "hg_q" else mixT)[:, k[2], at:at + ln]
                    else:
                        v, dst = th[0:ln, i, 0:256], gate_of[name[:2]][0:ln, at, :]
                    if name == "ml_ifg":
                        ps = ps[:, 8:264]
                    nc.vector.scalar_tensor_tensor(dst, v, 1.0, ps, ALU.add, ALU.mult).then_inc(*bank.free.inc(k))
                    return
                dve.wait_ge(*bank.full.at(k))
                dve.wait_ge(*tab_in.at(n))
                q = k[2] == 0
                a, b = rtmp[:, 0, 0:ln], rtmp[:, 1, 0:ln]
                if dve_done.n:
                    settle()
                nc.vector.stream_shuffle(a, ps, [(i + 16) % 32 for i in range(32)]).then_inc(*dve_done.inc())
                nc.vector.tensor_tensor(b, ps, rtab[:, 0 if q else 2, at:at + ln], ALU.mult).then_inc(*bank.free.inc(k))
                settle()
                nc.vector.tensor_tensor(a, a, rtab[:, 1 if q else 3, at:at + ln], ALU.mult).then_inc(*dve_done.inc())
                settle()
                dve.wait_ge(*bank.free.at(k))
                if q:
                    for h in range(4):
                        r = slice(32 * h, 32 * h + 32)
                        nc.vector.tensor_tensor(rq[r, h, at:at + ln], a[r, :], b[r, :], ALU.add).then_inc(*dve_done.inc())
                else:
                    nc.vector.tensor_tensor(rk[:, at:at + ln], a, b, ALU.add).then_inc(*dve_done.inc())
                if k == last_piece[k[:2]]:
                    settle()
                    nc.vector.memset(small[0:1, 63:64], 0.0).then_inc(*rot_done.inc(n))

            for s in plan:
                if s[0] == "norm":
                    dve.wait_ge(*nw_in.at(s[1]))
                    for t in tiles_of(s[1]):
                        scale_rows((s[1], t))
                        r = chunk_len(t)
                        for g in range(2):
                            u = ("norm", s[1], t, g)
                            bank = PB[bank_of[u]]
                            dve.wait_ge(*hhi_done.at((s[1], t, g)))
                            c = slice(t * P, t * P + r)
                            nc.vector.tensor_tensor(hlo[:, 4 * g:4 * g + 4, c], bank.t.rearrange("p (k c) -> p k c", k=4)[:, :, 0:r],
                                                    hhi[:, 4 * g:4 * g + 4, c].bitcast(F32), ALU.subtract).then_inc(*bank.free.inc(u))
                elif s[0] == "proj":
                    if s[2] == "ml_q":
                        if s[1]:
                            dve.wait_ge(*y_done.at([m for m in mixes if m[1] < s[1] and m[0] == "ml"][-1]))
                        elif s5n:
                            dve.wait_ge(*set_out.at(s5sets[-1] + (17,)))
                        nc.vector.memset(mq, 0.0).then_inc(*dve_done.inc())
                        nc.vector.memset(mvv[:, :, :, 64:65], 1.0).then_inc(*ml_clear.inc(s[1]))
                    if s[2] == "rt_qk":
                        nc.vector.memset(rq, 0.0).then_inc(*dve_done.inc())
                        settle()
                    for k in pieces:
                        if k[:2] == s[1:]:
                            take_piece(k)
                elif s[0] == "s5set":
                    l = s[1]

                    def tt(o, a, b, op):
                        nc.vector.tensor_tensor(o, a, b, op).then_inc(*dve_done.inc())

                    def cmul(o, a, b, t, u, conj=False, neg=False):
                        tt(t, a[0], b[0], ALU.mult)
                        tt(u, a[1], b[1], ALU.mult)
                        settle()
                        tt(o[0], t, u, ALU.subtract)
                        settle()
                        tt(t, a[0], b[1], ALU.mult)
                        tt(u, a[1], b[0], ALU.mult)
                        settle()
                        if neg:
                            nc.vector.scalar_tensor_tensor(o[1], t, -1.0, u, ALU.mult, ALU.subtract).then_inc(*dve_done.inc())
                        else:
                            tt(o[1], t, u, ALU.add)
                        settle()

                    LR, LI, DT, T2, T3, UR, UI, DEN, FR, FI, RR = (s5v[:, i, :] for i in range(11))
                    XX, PH2, SN2, CS2, E2, Q2, Z2 = (s5v[:, 12 + 2 * i:14 + 2 * i, :] for i in range(7))

                    def ts(o, a, x, y, op0, op1=None):
                        (nc.vector.tensor_scalar(o, a, x, y, op0, op1) if op1 is not None else nc.vector.tensor_scalar(o, a, x, None, op0)).then_inc(*dve_done.inc())
                        settle()

                    if not l:
                        dve.wait_ge(*vec_in.at(8))
                        ts(T2, DT, 1 / np.log(2), 12582912.0, ALU.mult, ALU.add)
                        ts(T2, T2, -12582912.0, -126.0, ALU.add, ALU.max)
                        ts(T2, T2, 127.0, None, ALU.min)
                        for part in (0.693359375, np.log(2) - 0.693359375):
                            nc.vector.scalar_tensor_tensor(DT, T2, -part, DT, ALU.mult, ALU.add).then_inc(*dve_done.inc())
                            settle()
                        ts(T3, DT, 1 / 7, 1.0, ALU.mult, ALU.add)
                        for k in (6, 5, 4, 3, 2, 1):
                            nc.vector.scalar_tensor_tensor(T3, T3, 1 / k, DT, ALU.mult, ALU.mult).then_inc(*dve_done.inc())
                            settle()
                            ts(T3, T3, 1.0, None, ALU.add)
                        ts(s5i[:, :], T2, 127.0, float(1 << 23), ALU.add, ALU.mult)
                        tt(DT, T3, s5i[:, :].bitcast(F32), ALU.mult)
                        settle()
                        tt(XX[:, 0], LR, DT, ALU.mult)
                        tt(PH2[:, 0], LI, DT, ALU.mult)
                        settle()

                        def less_turns(ph):
                            ts(T2, ph, 1 / (2 * np.pi), 12582912.0, ALU.mult, ALU.add)
                            ts(T2, T2, -12582912.0, None, ALU.add)
                            for part in (6.28125, 2 * np.pi - 6.28125):
                                nc.vector.scalar_tensor_tensor(ph, T2, -part, ph, ALU.mult, ALU.add).then_inc(*dve_done.inc())
                                settle()

                        less_turns(PH2[:, 0])
                        ts(PH2[:, 1], PH2[:, 0], 8.0, None, ALU.mult)
                        less_turns(PH2[:, 1])
                        ts(XX[:, 1], XX[:, 0], 8.0, None, ALU.mult)
                        nc.vector.memset(small[0:1, 57:58], 0.0).then_inc(*vec_dve.inc("phase"))
                        ts(XX, XX, 1 / 128, None, ALU.mult)
                        ts(E2, XX, 1 / 5, 1.0, ALU.mult, ALU.add)
                        for k in (4, 3, 2):
                            nc.vector.scalar_tensor_tensor(E2, E2, 1 / k, XX, ALU.mult, ALU.mult).then_inc(*dve_done.inc())
                            settle()
                            ts(E2, E2, 1.0, None, ALU.add)
                        tt(E2, E2, XX, ALU.mult)
                        settle()
                        for _ in range(7):
                            nc.vector.scalar_tensor_tensor(XX, E2, 2.0, E2, ALU.add, ALU.mult).then_inc(*dve_done.inc())
                            settle()
                            E2, XX = XX, E2
                        dve.wait_ge(*vec_act.at("sin"))
                        nc.vector.scalar_tensor_tensor(Q2, SN2, -2.0, SN2, ALU.mult, ALU.mult).then_inc(*dve_done.inc())
                        nc.vector.scalar_tensor_tensor(Z2, SN2, 2.0, CS2, ALU.mult, ALU.mult).then_inc(*dve_done.inc())
                        settle()
                        ts(PH2, Q2, 1.0, None, ALU.add)
                        nc.vector.scalar_tensor_tensor(UI, E2[:, 0], 1.0, Z2[:, 0], ALU.add, ALU.mult).then_inc(*dve_done.inc())
                        tt(UR, E2[:, 0], PH2[:, 0], ALU.mult)
                        settle()
                        tt(UR, UR, Q2[:, 0], ALU.add)
                        settle()
                        tt(T2, LR, LR, ALU.mult)
                        settle()
                        tt(T3, LI, LI, ALU.mult)
                        settle()
                        tt(DEN, T2, T3, ALU.add)
                        settle()
                        nc.vector.reciprocal(DEN, DEN).then_inc(*dve_done.inc())
                        tt(T2, UR, LR, ALU.mult)
                        settle()
                        tt(T3, UI, LI, ALU.mult)
                        settle()
                        tt(FR, T2, T3, ALU.add)
                        settle()
                        tt(T2, UI, LR, ALU.mult)
                        settle()
                        tt(T3, UR, LI, ALU.mult)
                        settle()
                        tt(FI, T2, T3, ALU.subtract)
                        settle()
                        tt(FR, FR, DEN, ALU.mult)
                        settle()
                        tt(FI, FI, DEN, ALU.mult)
                        settle()
                        ts(RR, E2[:, 1], 1.0, None, ALU.add)
                        s5_phase = (PH2[:, 1], Z2[:, 1])
                        pw = lambda i, lo, hi: s5p[:, i, :, lo:hi]
                        nc.vector.memset(s5p[:, 0, :, 0], 1.0).then_inc(*dve_done.inc())
                        nc.vector.memset(s5p[:, 1, :, 0], 0.0).then_inc(*dve_done.inc())
                        ts(s5p[:, 0, :, 1], UR, 1.0, None, ALU.add)
                        nc.vector.tensor_copy(s5p[:, 1, :, 1], UI).then_inc(*dve_done.inc())
                        settle()
                        for k in (1, 2, 4):
                            t, u = (x[:, 0:16 * k].rearrange("p (s k) -> p s k", k=k) for x in ct)
                            cmul((pw(0, k + 1, 2 * k + 1), pw(1, k + 1, 2 * k + 1)), (pw(0, 1, k + 1), pw(1, 1, k + 1)),
                                 tuple(pw(i, k, k + 1).broadcast_to([P, 16, k]) for i in range(2)), t, u)
                        for ll in range(DEPTH):
                            for i in range(2):
                                nc.vector.tensor_copy(s5c[:, ll, i, :], s5p[:, i, 8 * ll:8 * ll + 8, 4]).then_inc(*dve_done.inc())
                            nc.vector.tensor_copy(s5c[:, ll, 2, :], RR[:, 8 * ll:8 * ll + 8]).then_inc(*dve_done.inc())
                        settle()
                        keep_phase[:] = [s5_phase, (FR, FI)]
                    (zr, zi), (fr, fi) = keep_phase
                    ly = slice(8 * l, 8 * l + 8)
                    if l:
                        dve.wait_ge(*set_out.at(s5sets[0] + (17,)))
                    nc.vector.tensor_copy(cE[:, 0, :, 0], zr[:, ly]).then_inc(*dve_done.inc())
                    nc.vector.tensor_scalar(cE[:, 1, :, 0], zi[:, ly], -1.0, None, ALU.mult).then_inc(*dve_done.inc())
                    settle()
                    for k in (1, 2, 4, 8, 16, 32):
                        t, u = (x[:, 0:8 * k].rearrange("p (s k) -> p s k", k=k) for x in ct)
                        cmul((cE[:, 0, :, k:2 * k], cE[:, 1, :, k:2 * k]), (cE[:, 0, :, 0:k], cE[:, 1, :, 0:k]),
                             tuple(cE[:, i, :, k - 1:k].broadcast_to([P, 8, k]) for i in range(2)), t, u)
                    t, u = (x[:, 0:512].rearrange("p (s k) -> p s k", k=64) for x in ct)
                    tt(t, cE[:, 0], cE[:, 0], ALU.mult)
                    tt(u, cE[:, 1], cE[:, 1], ALU.mult)
                    settle()
                    tt(t, t, u, ALU.add)
                    settle()
                    ts(t, t, -0.5, 1.5, ALU.mult, ALU.add)
                    tt(cE[:, 0], cE[:, 0], t, ALU.mult)
                    tt(cE[:, 1], cE[:, 1], t, ALU.mult)
                    settle()
                    nc.vector.memset(small[0:1, 57:58], 0.0).then_inc(*set_dve.inc(s + ("E",)))
                    dve.wait_ge(*set_in.at(s + (5,)))
                    t, u = (x[:, 0:128].rearrange("p (q c) -> p q c", c=16) for x in ct)
                    o1 = lambda v, w: v.rearrange("p (q o) -> p q o", o=1).broadcast_to([P, 8, w])
                    cmul((cBb[:, 0], cBb[:, 1]), (o1(fr[:, ly], 16), o1(fi[:, ly], 16)), (cB[:, 0], cB[:, 1]), t, u)
                    dve.wait_ge(*aux.free.at(s + ("C",)))
                    pj = lambda i, lo, hi: s5p[:, i, ly, lo:hi].rearrange("p q (j o) -> p q j o", o=1).broadcast_to([P, 8, hi - lo, 16])
                    cc_ = lambda v, k: v.rearrange("p q (o c) -> p q o c", o=1).broadcast_to([P, 8, k, 16])
                    t, u = (x[:, :].rearrange("p (q j c) -> p q j c", j=9, c=16) for x in ct)
                    cmul((cV[:, 0], cV[:, 1]), (pj(0, 0, 9), pj(1, 0, 9)), (cc_(cCT[:, 0], 9), cc_(cCT[:, 1], 9)), t, u, neg=True)
                    nc.vector.memset(small[0:1, 57:58], 0.0).then_inc(*set_dve.inc(s + ("V",)))
                    for s_ in range(8):
                        t, u = (x[:, 128 * s_:128 * s_ + 128].rearrange("p (q c) -> p q c", c=16) for x in ct)
                        pj1 = lambda i: s5p[:, i, ly, 7 - s_:8 - s_].broadcast_to([P, 8, 16])
                        cmul((cW[:, 0, :, s_, :], cW[:, 1, :, s_, :]), (pj1(0), pj1(1)), (cBb[:, 0], cBb[:, 1]), t, u)
                    nc.vector.memset(small[0:1, 57:58], 0.0).then_inc(*set_dve.inc(s + ("W",)))
                elif s[0] == "s5":
                    n, l = s[1], s[1] // 2
                    odd = n % 2
                    Wn = HALF + TS * odd

                    def tt(o, a, b, op, inc=None):
                        nc.vector.tensor_tensor(o, a, b, op).then_inc(*(inc or dve_done.inc()))

                    if not odd:
                        if n:
                            dve.wait_ge(*s5_out.at(("s5", n - 1, 1, NB - 1)))
                        nc.vector.memset(s5x[:, :, :], 0.0).then_inc(*dve_done.inc())
                    wr, wi = (scores.t[:, i, :].rearrange("p (q b) -> p q b", q=8) for i in range(2))
                    Er, Ei = sE[:, 0], sE[:, 1]
                    t, u = stmp
                    dve.wait_ge(*s5_in["E"].at(s))
                    dve.wait_ge(*scores.full.at(s + (0,)))
                    tt(t, Er, wr, ALU.mult)
                    tt(u, Ei, wi, ALU.mult)
                    settle()
                    tt(sG[:, 0], t, u, ALU.subtract)
                    settle()
                    tt(t, Er, wi, ALU.mult)
                    tt(u, Ei, wr, ALU.mult, scores.free.inc(s + (0,)))
                    settle()
                    dve.wait_ge(*scores.free.at(s + (0,)))
                    tt(sG[:, 1], t, u, ALU.add)
                    settle()
                    for i in range(2):
                        for q in range(8):
                            nc.vector.tensor_tensor_scan(sG[:, i, q, :], s5c[:, l, 2, q:q + 1].broadcast_to([P, 64]), sG[:, i, q, :],
                                                         s5x[:, i, q:q + 1], ALU.mult, ALU.add).then_inc(*dve_done.inc())
                    nc.vector.tensor_copy(sX[:, :, :, 0], s5x[:, :, :]).then_inc(*dve_done.inc())
                    settle()
                    tt(t, Er, sG[:, 0], ALU.mult)
                    tt(u, Ei, sG[:, 1], ALU.mult)
                    settle()
                    tt(sX[:, 0, :, 1:65], t, u, ALU.add)
                    settle()
                    tt(t, Er, sG[:, 1], ALU.mult)
                    tt(u, Ei, sG[:, 0], ALU.mult)
                    settle()
                    tt(sX[:, 1, :, 1:65], t, u, ALU.subtract)
                    settle()
                    nc.vector.tensor_copy(s5x[:, :, :], sX[:, :, :, 64]).then_inc(*dve_done.inc())
                    if odd:
                        dve.wait_ge(*s5_xi.at(s + (1, NB - 1)))
                        dve.wait_ge(*upd.full.at(s + ("w",)))
                        A = [s5c[:, l, i, :].rearrange("p (q o) -> p q o", o=1).broadcast_to([P, 8, NB]) for i in range(2)]
                        t8, u8 = (x[:, :, 0:NB] for x in stmp)
                        ws = upd.t[:, 0:16 * NB].rearrange("p (r q b) -> p r q b", r=2, q=8)
                        for i, op in ((0, ALU.subtract), (1, ALU.add)):
                            settle()
                            tt(t8, A[0], sX0[:, i], ALU.mult)
                            tt(u8, A[1], sX0[:, 1 - i], ALU.mult)
                            settle()
                            tt(sXf[:, i], t8, u8, op)
                        settle()
                        tt(sXf, sXf, ws, ALU.add, upd.free.inc(s + ("w",)))
                        dve.wait_ge(*upd.free.at(s + ("w",)))
                    settle()
                    nc.vector.memset(small[0:1, 57:58], 0.0).then_inc(*s5_rot.inc(s))
                    dve.wait_ge(*s5_in["Y"].at(s))
                    for j in range(2):
                        nc.vector.scalar_tensor_tensor(yT[:, j, 0:Wn], ux[:, j, 0:Wn], s5d[:, l, j:j + 1], yT[:, j, 0:Wn], ALU.mult, ALU.add).then_inc(
                            *(s5_dve.inc(s + ("skip",)) if j else dve_done.inc()))
                    dve.wait_ge(*s5_act.at(s + ("sq",)))
                    g, yy = gt[:, :, 0:Wn], yT[:, :, 0:Wn]
                    nc.vector.tensor_scalar(g, g, 0.044715, 1.0, ALU.mult, ALU.add).then_inc(*dve_done.inc())
                    settle()
                    dve.wait_ge(*s5_dve.at(s + ("skip",)))
                    tt(g, g, yy, ALU.mult, s5_dve.inc(s + ("cube",)))
                    dve.wait_ge(*s5_act.at(s + ("tanh",)))
                    for j in range(2):
                        nc.vector.scalar_tensor_tensor(yg[:, j, 0:Wn], gt[:, j, 0:Wn], 1.0, yT[:, j, 0:Wn], ALU.add, ALU.mult).then_inc(
                            *(s5_dve.inc(s + ("gelu",)) if j else dve_done.inc()))
                    dve.wait_ge(*scores.free.at(s + (2,)))
                    if odd:
                        dve.wait_ge(*upd.free.at(s + ("glu",)))
                    settle()
                    for j in range(2):
                        nc.vector.scalar_tensor_tensor(yT[:, j, 0:Wn], gt[:, j, 0:Wn], 1.0, yg[:, j, 0:Wn], ALU.add, ALU.mult).then_inc(*dve_done.inc())
                    settle()
                    for lo, hi, tau in ((0, HALF, 8), (HALF, W, DSEQ))[:1 + odd]:
                        for j in range(2):
                            m = mixT[:, j, lo:hi].rearrange("p (b t) -> p t b", t=tau)
                            nc.vector.scalar_tensor_tensor(m, yT[:, j, lo:hi].rearrange("p (t b) -> p t b", t=tau), 0.125, m, ALU.mult, ALU.mult).then_inc(*dve_done.inc())
                    settle()
                    nc.vector.memset(small[0:1, 57:58], 0.0).then_inc(*s5_dve.inc(s + ("mixed",)))
                elif s[0] == "hgpre":
                    n, Wn = s[1], HALF + TS * (s[1] % 2)
                    f, u, cum, kk = hf[:, :, 0:Wn], hu[:, :, 0:Wn], hcum[:, :, 0:Wn], hk[:, :, 0:Wn]
                    dve.wait_ge(*pre_act.at(s + (0,)))
                    for j in range(2):
                        nc.vector.scalar_tensor_tensor(cum[:, j], f[:, j], 0.0, u[:, j], ALU.min, ALU.subtract).then_inc(*dve_done.inc())
                    settle()
                    nc.vector.tensor_tensor(f, cum, f, ALU.subtract).then_inc(*pre_dve.inc(s + (0,)))
                    dve.wait_ge(*pre_act.at(s + (1,)))
                    if n // 2:
                        for j in range(2):
                            nc.vector.tensor_scalar(u[:, j], u[:, j], lb[:, 2 + j:3 + j], lb[:, j:j + 1], ALU.mult, ALU.add).then_inc(*dve_done.inc())
                            nc.vector.tensor_scalar(kk[:, j], kk[:, j], lb[:, 2 + j:3 + j], None, ALU.mult).then_inc(*dve_done.inc())
                        settle()
                        nc.vector.tensor_scalar(u, u, 2.0 ** -60, None, ALU.max).then_inc(*pre_dve.inc(s + (1,)))
                        dve.wait_ge(*pre_act.at(s + (2,)))
                    for j in range(2):
                        nc.vector.tensor_tensor_scan(cum[:, j], C("reset")[:, 0:Wn], cum[:, j], 0.0, ALU.mult, ALU.add).then_inc(*dve_done.inc())
                    settle()
                    if n % 2 == 0:
                        if n:
                            dve.wait_ge(*ps_out.at([m for m in last_prompt if m[0] == "hg" and m[1] < n][-1] + (3,)))
                        nc.vector.memset(S_hg[:, :, :], 0.0).then_inc(*state_zero.inc((n // 2, "hg")))
                        dve.wait_ge(*state_zero.at((n // 2, "hg")))
                elif s[0] == "mlpre":
                    n, l = s[1], s[1] // 2
                    Wn = W if n % 2 else HALF
                    dve.wait_ge(*pre_act.at(s + (0,)))
                    lf, cum, m, g, a = (rows[:, i, 0:Wn] for i in (SP_, WK_, M_, G_, A_))
                    nc.vector.scalar_tensor_tensor(lf, lf, 0.0, m, ALU.min, ALU.subtract).then_inc(*dve_done.inc())
                    if n % 2 == 0:
                        if n:
                            dve.wait_ge(*ps_out.at([q for q in last_prompt if q[0] == "ml" and q[1] < n][-1] + (7,)))
                            dve.wait_ge(*m_out.at((l - 1, 1)))
                        nc.vector.memset(S_ml[:, :, :], 0.0).then_inc(*dve_done.inc())
                        nc.vector.memset(gb[:, 4:5], 0.0).then_inc(*dve_done.inc())
                    settle()
                    nc.vector.tensor_copy(a, g).then_inc(*dve_done.inc())
                    nc.vector.tensor_tensor_scan(cum, C("reset")[0:4, 0:Wn], lf, 0.0, ALU.mult, ALU.add).then_inc(*dve_done.inc())
                    settle()
                    first = slice(HALF, W, DSEQ)
                    if n % 2:
                        dve.wait_ge(*m_in.at(l))
                        nc.vector.tensor_tensor(rows[:, M_, 0:NB], rows[:, SP_, first], m0[:, :], ALU.add).then_inc(*dve_done.inc())
                        settle()
                        nc.vector.tensor_tensor(rows[:, A_, first], rows[:, M_, 0:NB], rows[:, G_, first], ALU.max).then_inc(*dve_done.inc())
                        nc.vector.memset(rows[:, SP_, first], -1e30).then_inc(*dve_done.inc())
                        settle()
                    nc.vector.tensor_copy(mp[:, 0:1], gb[:, 4:5]).then_inc(*dve_done.inc())
                    nc.vector.tensor_tensor_scan(m, lf, a, gb[:, 4:5], ALU.add, ALU.max).then_inc(*dve_done.inc())
                    settle()
                    nc.vector.tensor_tensor(g, g, cum, ALU.subtract).then_inc(*dve_done.inc())
                    nc.vector.tensor_tensor(a, cum, m, ALU.subtract).then_inc(*dve_done.inc())
                    nc.vector.tensor_copy(mp[:, 1:NCH], rows[:, M_, CH - 1:HALF - 1:CH]).then_inc(*dve_done.inc())
                    nc.vector.tensor_copy(gb[:, 4:5], rows[:, M_, HALF - 1:HALF]).then_inc(*dve_done.inc())
                    settle()

                    def per_chunk(slot, lo, hi, w):
                        return rows[:, slot, lo:hi].rearrange("p (c w) -> p c w", w=w)

                    for lo, hi, w, prev in ((0, HALF, CH, mp), (HALF, W, DSEQ, m0))[:1 + n % 2]:
                        k = (hi - lo) // w
                        nc.vector.tensor_tensor(per_chunk(SP_, lo, hi, w), per_chunk(A_, lo, hi, w),
                                                prev[:, :].rearrange("p (c o) -> p c o", o=1).broadcast_to([4, k, w]), ALU.add).then_inc(*dve_done.inc())
                        nc.vector.tensor_tensor(per_chunk(WK_, lo, hi, w), per_chunk(G_, lo, hi, w),
                                                per_chunk(A_, lo, hi, w)[:, :, w - 1:w].broadcast_to([4, k, w]), ALU.add).then_inc(*dve_done.inc())
                    settle()
                    nc.vector.memset(small[0:4, 62:63], 0.0).then_inc(*pre_dve.inc(s + (0,)))
                elif s in mixes:
                    br, n, c = s
                    T, cc = chunk_len(c), cols(c)
                    nb = 1 if c < NCH else NB
                    prev = before(mixes, s)
                    stt = ST if c < NCH else STs
                    dv = 65 if br == "ml" else 64
                    v_all = {"hg": hv, "rt": rv}.get(br)
                    if prev:
                        dve.wait_ge(*outb.full.at(prev))
                    if br == "hg":
                        for i, w in enumerate(levels(c)):
                            for j in range(2):
                                x = hcum[:, j, cc].rearrange("p (n w) -> p n w", w=2 * w)
                                mid = x[:, :, w - 1:w].broadcast_to([P, T // (2 * w), 2 * w])
                                nc.vector.tensor_tensor(E[:, i, j, 0:T].rearrange("p (n w) -> p n w", w=2 * w), x, mid, ALU.subtract).then_inc(*dve_done.inc())
                        L = CH if c < NCH else DSEQ
                        for j in range(2):
                            x = hcum[:, j, cc].rearrange("p (n w) -> p n w", w=L)
                            nc.vector.tensor_tensor(E[:, 7, j, 0:T].rearrange("p (n w) -> p n w", w=L), x,
                                                    x[:, :, L - 1:L].broadcast_to([P, T // L, L]), ALU.subtract).then_inc(*(hg_diff.inc(s) if j else dve_done.inc()))
                        nc.vector.tensor_tensor(E[:, 9, :, 0:T], hq[:, :, cc], hk[:, :, cc], ALU.mult).then_inc(*dve_done.inc())
                        if c in (0, NCH):
                            nc.vector.memset(QD, 0.0).then_inc(*dve_done.inc())
                        settle()
                        dve.wait_ge(*hg_exp.at(s))
                        for i, w in enumerate(levels(c)):
                            for j in range(2):
                                e = split(E[:, i, j, 0:T], w)
                                nc.vector.tensor_tensor(e[:, :, 1], e[:, :, 1], split(hq[:, j, cc], w)[:, :, 1], ALU.mult).then_inc(*dve_done.inc())
                                nc.vector.tensor_tensor(e[:, :, 0], e[:, :, 0], split(hk[:, j, cc], w)[:, :, 0], ALU.mult).then_inc(*dve_done.inc())
                        nc.vector.tensor_tensor(E[:, 7, :, 0:T], E[:, 7, :, 0:T], hk[:, :, cc], ALU.mult).then_inc(*dve_done.inc())
                        for par in range(2):
                            r = slice(par * 64, par * 64 + 64)
                            nc.vector.tensor_tensor(QD[r, :, par, 0:T], E[r, 8, :, 0:T], hq[r, :, cc], ALU.mult).then_inc(*dve_done.inc())
                        settle()
                        nc.vector.memset(small[0:1, 61:62], 0.0).then_inc(*hg_prod.inc(s))
                        for j in range(2):
                            dve.wait_ge(*scores.full.at(s + (j,)))
                            ls = levels(c)
                            u = T // 2
                            base = 0 if c < NCH else NL * 64
                            for i, w in enumerate(ls):
                                if i:
                                    settle()
                                for par in range(2):
                                    o = split(stt[0:T, 2 * j + par, 0:T], w)[:, :, 1]
                                    mask = cm[0:T, base + i * u:base + (i + 1) * u].rearrange("p (n w) -> p n w", w=w)
                                    dat = scores.t[0:T, par, i * u:(i + 1) * u].rearrange("p (n w) -> p n w", w=w)
                                    nc.vector.copy_predicated(o, mask, dat).then_inc(
                                        *(scores.free.inc(s + (j,)) if i == len(ls) - 1 and par else dve_done.inc()))
                            dve.wait_ge(*scores.free.at(s + (j,)))
                        dve.wait_ge(*aux.free.at(s + ("turn",)))
                        settle()
                        for h in range(4):
                            nc.vector.copy_predicated(stt[0:T, h, 0:T], cm[0:T, NL * 64 + 32:NL * 64 + 32 + T],
                                                      small[0:T, h:h + 1].broadcast_to([T, T])).then_inc(*(st_done.inc(s) if h == 3 else dve_done.inc()))
                    elif br == "rt":
                        dve.wait_ge(*scores.full.at(s + (0,)))
                        mask = (C("causal") if c < NCH else C("causal_s")).rearrange("p (o t) -> p o t", o=1).broadcast_to([T, 4, T])
                        nc.vector.tensor_tensor(stt[0:T, :, 0:T], scores.t[0:T, 0, 0:4 * T].rearrange("p (h t) -> p h t", h=4), mask,
                                                ALU.mult).then_inc(*scores.free.inc(s + (0,)))
                        dve.wait_ge(*scores.free.at(s + (0,)))
                        nc.vector.memset(small[0:1, 60:61], 0.0).then_inc(*st_done.inc(s))
                    else:
                        dve.wait_ge(*scores.full.at(s + (0,)))
                        mask = (C("cneg") if c < NCH else C("cneg_s")).rearrange("p (o t) -> p o t", o=1).broadcast_to([T, 4, T])
                        e4 = ex[0:T, 0:4 * T].rearrange("p (h t) -> p h t", h=4)
                        nc.vector.tensor_tensor(e4, scores.t[0:T, 1, 0:4 * T].rearrange("p (h t) -> p h t", h=4), mask, ALU.add).then_inc(*ex_add.inc(s))
                        dve.wait_ge(*ex_exp.at(s))
                        nc.vector.tensor_tensor(stt[0:T, :, 0:T], e4, scores.t[0:T, 0, 0:4 * T].rearrange("p (h t) -> p h t", h=4),
                                                ALU.mult).then_inc(*scores.free.inc(s + (0,)))
                        dve.wait_ge(*scores.free.at(s + (0,)))
                        nc.vector.memset(small[0:1, 60:61], 0.0).then_inc(*st_done.inc(s))

                    dve.wait_ge(*outb.full.at(s))
                    if prev:
                        dve.wait_ge(*aux.full.at(prev + ("mixed",)))
                    yf = y[0:T, :, :]
                    gate = gate_of[br][0:T, c, :].rearrange("p (h v) -> p h v", h=4)
                    if br == "ml":
                        num = ex[0:T, 0:260].rearrange("p (h v) -> p h v", h=4)
                        dve.wait_ge(*scores.full.at(s + (1,)))
                        dve.wait_ge(*aux.free.at(s + ("turn",)))
                        nc.vector.tensor_tensor(num, scores.t[0:T, 0, 0:260].rearrange("p (h v) -> p h v", h=4),
                                                small[0:T, 4:8].rearrange("p (h o) -> p h o", o=1).broadcast_to([T, 4, 65]), ALU.mult).then_inc(*scores.free.inc(s + (1,)))
                        dve.wait_ge(*scores.free.at(s + (1,)))
                        nc.vector.tensor_tensor(num, num, outb.t[0:T, 0:260].rearrange("p (h v) -> p h v", h=4), ALU.add).then_inc(*outb.free.inc(s))
                        dve.wait_ge(*outb.free.at(s))
                        den = small[0:T, 32:36]
                        nc.vector.scalar_tensor_tensor(den, ex[0:T, 64:260:65], -1.0, ex[0:T, 64:260:65], ALU.mult, ALU.max).then_inc(*dve_done.inc())
                        nc.vector.scalar_tensor_tensor(yf.rearrange("p h v -> p (h v)").rearrange("p (h v) -> p h v", h=4), mo[0:T, c, :].rearrange("p (h v) -> p h v", h=4), 1.0, num[:, :, 0:64], ALU.add, ALU.mult).then_inc(*dve_done.inc())
                        settle()
                        nc.vector.tensor_tensor(den, den, small[0:T, 8:12], ALU.max).then_inc(*dve_done.inc())
                        settle()
                        nc.vector.reciprocal(den, den).then_inc(*dve_done.inc())
                        settle()
                        nc.vector.tensor_tensor(yf, yf, den.rearrange("p (h o) -> p h o", o=1).broadcast_to([T, 4, 64]), ALU.mult).then_inc(*dve_done.inc())
                        settle()
                        src = yf
                    else:
                        src = outb.t[0:T, 0:256].rearrange("p (h v) -> p h v", h=4)
                    for h in range(4):
                        nc.vector.bn_stats(stats[0:T, h, :], src[:, h, :]).then_inc(*dve_done.inc())
                    settle()
                    for h in range(4):
                        nc.vector.bn_aggr(mv[0:T, h, :], stats[0:T, h, :]).then_inc(*(mv_done.inc(s) if h == 3 else dve_done.inc()))
                    settle()
                    dve.wait_ge(*mv_done.at(s))
                    for h in range(4):
                        nc.vector.scalar_tensor_tensor(yf[:, h, :], src[:, h, :], mv[0:T, h, 0:1], gate[:, h, :], ALU.subtract, ALU.mult).then_inc(
                            *(outb.free.inc(s) if h == 3 and br != "ml" else dve_done.inc()))
                    if nb == 1:
                        dve.wait_ge(*upd.full.at(s + ("U",)))
                        if br == "rt":
                            nc.vector.tensor_tensor(S_rt[:, :], S_rt[:, :], upd.t[:, 0:64], ALU.add).then_inc(*dve_done.inc())
                            settle()
                            nc.vector.tensor_scalar(S_rt[:, :], S_rt[:, :], C("gam")[:, 0:1], None, ALU.mult).then_inc(*upd.free.inc(s + ("U",)))
                        else:
                            S = S_hg if br == "hg" else S_ml
                            for j in range(2):
                                dec = E[:, 8, j, T - 1:T] if br == "hg" else small[:, 16 + j:17 + j]
                                nc.vector.scalar_tensor_tensor(S[:, j, :], S[:, j, :], dec, upd.t[:, j * dv:(j + 1) * dv], ALU.mult, ALU.add).then_inc(
                                    *(upd.free.inc(s + ("U",)) if j else dve_done.inc()))
                        dve.wait_ge(*upd.free.at(s + ("U",)))
                    else:
                        for h in range(4):
                            if h or samples.index(s):
                                i = samples.index(s)
                                dve.wait_ge(*vexp_used.at(s + (h - 1,) if h else samples[i - 1] + (3,)))
                            vs = (v_all[0:TS, c, h * 64:h * 64 + 64] if v_all is not None else mvv[0:TS, c, h, 0:64])
                            nc.vector.tensor_tensor(ex[0:TS, :].rearrange("p (b v) -> p b v", b=NB),
                                                    vs.rearrange("p (o v) -> p o v", o=1).broadcast_to([TS, NB, 64]),
                                                    C("bmask").rearrange("p (b o) -> p b o", o=1).broadcast_to([TS, NB, 64]), ALU.mult).then_inc(*vexp_done.inc(s + (h,)))
                        dve.wait_ge(*scores.full.at(s + ("su",)))
                        for j in range(1 if br == "rt" else 2):
                            sv = sst[:, j, :, 0:dv]
                            if br == "rt":
                                pass
                            else:
                                dec = (E[:, 8, j, DSEQ - 1:TS:DSEQ] if br == "hg" else small[:, 16 + NB * j:16 + NB * j + NB])
                                nc.vector.tensor_tensor(sv, sv, dec.rearrange("p (b o) -> p b o", o=1).broadcast_to([P, NB, dv]), ALU.mult).then_inc(*dve_done.inc())
                                settle()
                            nc.vector.tensor_tensor(sst[:, j, :, 0:64], sst[:, j, :, 0:64], scores.t[:, j, :].rearrange("p (b v) -> p b v", b=NB), ALU.add).then_inc(
                                *(scores.free.inc(s + ("su",)) if j or br == "rt" else dve_done.inc()))
                            if br == "rt":
                                dve.wait_ge(*scores.free.at(s + ("su",)))
                                nc.vector.tensor_scalar(sst[:, j, :, 0:64], sst[:, j, :, 0:64], C("gam")[:, 1:2], None, ALU.mult).then_inc(*dve_done.inc())
                        if br == "ml":
                            dve.wait_ge(*upd.full.at(s + ("n",)))
                            dve.wait_ge(*scores.free.at(s + ("su",)))
                            nc.vector.tensor_tensor(sst[:, :, :, 64], sst[:, :, :, 64], upd.t[:, 0:2 * NB].rearrange("p (j b) -> p j b", j=2), ALU.add).then_inc(*upd.free.inc(s + ("n",)))
                            dve.wait_ge(*upd.free.at(s + ("n",)))
                        settle()
                        dve.wait_ge(*scores.free.at(s + ("su",)))
                        nc.vector.memset(small[0:1, 59:60], 0.0).then_inc(*ss_new.inc(s))
                    settle()
                    if br != "ml":
                        dve.wait_ge(*outb.free.at(s))
                    dve.wait_ge(*rs_done.at(s))
                    nc.vector.tensor_tensor(yf, yf, rs[0:T, :].rearrange("p (h o) -> p h o", o=1).broadcast_to([T, 4, 64]), ALU.mult).then_inc(*y_done.inc(s))
                elif s[0] == "out":
                    for k in outs_of(s[1]):
                        r, sl = chunk_len(k[2]), oslot[k]
                        bank = PB[bank_of[k]]
                        dve.wait_ge(*xo_in[sl].at(k))
                        dve.wait_ge(*bank.full.at(k))
                        nc.vector.tensor_tensor(xo[0:r, sl, :], xo[0:r, sl, :], bank.t[0:r, 0:256], ALU.add).then_inc(*bank.free.inc(k))
                        dve.wait_ge(*bank.free.at(k))
                        nc.vector.memset(small[0:1, 58:59], 0.0).then_inc(*xo_sum.inc(k))
                elif s[0] == "final":
                    dve.wait_ge(*nw_in.at("final"))
                    for k in final_tiles:
                        scale_rows(k)
                if s[0] == "proj" and s[2] == "rt_qk" and s[1] % 2 == 0:
                    if s[1]:
                        dve.wait_ge(*ps_out.at([q for q in last_prompt if q[0] == "rt" and q[1] < s[1]][-1] + (0,)))
                    nc.vector.memset(S_rt[:, :], 0.0).then_inc(*dve_done.inc())
                    settle()

        @block.tensor
        def _(pe):
            pe.wait_ge(*const_in.at(4))
            pe.wait_ge(*pool_setup.at("all"))
            for s in plan:
                if s[0] == "norm":
                    for t in tiles_of(s[1]):
                        r = chunk_len(t)
                        pe.wait_ge(*h_done.at((s[1], t)))
                        for g in range(2):
                            u = ("norm", s[1], t, g)
                            bank = PB[bank_of[u]]
                            bank.claim(pe, u)
                            for k in range(4):
                                mm = nc.tensor.transpose(bank.t[:, k * P:k * P + r], xt[0:r, tslot[(s[1], t)], (4 * g + k) * P:(4 * g + k + 1) * P],
                                                         ident[0:r, 0:r])
                            mm.then_inc(*bank.full.inc(u))
                elif s[0] == "proj":
                    b, n = s[1:], s[1]
                    pe.wait_ge(*whi_done.at(b))
                    pe.wait_ge(*wlo_done.at(b))
                    sl = hslot[b]
                    for k in pieces:
                        if k[:2] != b:
                            continue
                        bank = PB[bank_of[k]]
                        bank.claim(pe, k)
                        if k == [q for q in pieces if q[:2] == b][0]:
                            for t in tiles_of(n):
                                for g in range(2):
                                    u = ("norm", n, t, g)
                                    pe.wait_ge(*PB[bank_of[u]].free.at(u))
                        for kt in range(KT):
                            for x, w in ((hhi, whi), (hhi, wlo), (hlo, whi)):
                                first, last = kt == 0 and w is whi and x is hhi, kt == KT - 1 and x is hlo
                                if BLOCK[b[1]][3] == "ch":
                                    c = slice(0, HALF) if k[3] == 0 else slice(HALF, W)
                                    mm = nc.tensor.matmul(bank.t[:, 0:c.stop - c.start], w[:, sl, kt, k[2] * P:(k[2] + 1) * P], x[:, kt, c],
                                                          start=first, stop=last)
                                else:
                                    c = slice(k[2] * P, k[2] * P + P) if k[2] < NCH else slice(W - P, W)
                                    width = BLOCK[b[1]][2]
                                    mm = nc.tensor.matmul(bank.t[:, 0:width], x[:, kt, c], w[:, sl, kt, 0:width], start=first, stop=last)
                        mm.then_inc(*bank.full.inc(k))
                elif s[0] == "s5set":
                    k = s + ("C",)
                    aux.claim(pe, k)
                    pe.wait_ge(*set_in.at(s + (5,)))
                    for ri in range(2):
                        for f in range(2):
                            mm = nc.tensor.transpose(aux.t[:, (2 * ri + f) * P:(2 * ri + f + 1) * P], cCn[:, ri, f, :], ident)
                    mm.then_inc(*aux.full.inc(k))
                    pe.wait_ge(*set_dve.at(s + ("W",)))
                    for ri in range(2):
                        scores.claim(pe, s + (ri,))
                        for q in range(8):
                            mm = nc.tensor.transpose(scores.t[:, q // 4, q % 4 * P:(q % 4 + 1) * P], cW[:, ri, q].rearrange("p s c -> p (s c)"), ident)
                        mm.then_inc(*scores.full.inc(s + (ri,)))
                    for r in range(2):
                        scores.claim(pe, s + (2 + r,))
                        for a in range(2):
                            h = slice(64 * a, 64 * a + 64)
                            for q in range(4):
                                for ri in range(2):
                                    mm = nc.tensor.matmul(scores.t[0:16, a, q * P:(q + 1) * P], cBb[h, ri, 4 * r + q, :],
                                                          cV[h, ri, 4 * r + q, 0:8].rearrange("p j c -> p (j c)"), start=ri == 0, stop=ri == 1)
                        mm.then_inc(*scores.full.inc(s + (2 + r,)))
                elif s[0] == "s5":
                    n = s[1]
                    odd = n % 2
                    pe.wait_ge(*s5_in["W"].at(s))
                    pe.wait_ge(*s5_u.at(s + (7 + 4 * odd,)))
                    scores.claim(pe, s + (0,))
                    for ri in range(2):
                        for q in range(8):
                            for a in range(2):
                                mm = nc.tensor.matmul(scores.t[64 * a:64 * a + 64, ri, q * 64:(q + 1) * 64], sWT[:, q, ri, 64 * a:64 * a + 64],
                                                      U[:, 2 * q + a, 0:64], start=True, stop=True)
                    mm.then_inc(*scores.full.inc(s + (0,)))
                    if odd:
                        upd.claim(pe, s + ("w",))
                        for ri in range(2):
                            for q in range(8):
                                for a in range(2):
                                    mm = nc.tensor.matmul(upd.t[64 * a:64 * a + 64, (8 * ri + q) * NB:(8 * ri + q + 1) * NB], sWT[:, q, ri, 64 * a:64 * a + 64],
                                                          U[:, 2 * q + a, 64:72], start=True, stop=True)
                        mm.then_inc(*upd.full.inc(s + ("w",)))
                    pe.wait_ge(*s5_in["T"].at(s))
                    pe.wait_ge(*s5_in["V"].at(s))
                    pe.wait_ge(*s5_rot.at(s))
                    scores.claim(pe, s + (1,))
                    for a in range(2):
                        h = slice(64 * a, 64 * a + 64)
                        for q in range(8):
                            o = scores.t[:, a, q * 64:(q + 1) * 64]
                            nc.tensor.matmul(o, sT[:, 2 * q + a, :], U[:, 2 * q + a, 0:64], start=True, stop=False)
                            nc.tensor.matmul(o, sV[h, 0, q, :], sX[h, 0, q, 0:64], start=False, stop=False)
                            mm = nc.tensor.matmul(o, sV[h, 1, q, :], sX[h, 1, q, 0:64], start=False, stop=True)
                    mm.then_inc(*scores.full.inc(s + (1,)))
                    if odd:
                        for a, bank in enumerate((upd, aux)):
                            bank.claim(pe, s + ("y",))
                            h = slice(64 * a, 64 * a + 64)
                            for q in range(8):
                                o = bank.t[0:64, q * NB:(q + 1) * NB]
                                nc.tensor.matmul(o, sT[:, 2 * q + a, 64:128], U[:, 2 * q + a, 64:72], start=True, stop=False)
                                nc.tensor.matmul(o, sV[h, 0, q, 0:64], sX0[h, 0, q, :], start=False, stop=False)
                                mm = nc.tensor.matmul(o, sV[h, 1, q, 0:64], sX0[h, 1, q, :], start=False, stop=True)
                            mm.then_inc(*bank.full.inc(s + ("y",)))
                    pe.wait_ge(*s5_in["G"].at(s))
                    pe.wait_ge(*s5_dve.at(s + ("gelu",)))
                    scores.claim(pe, s + (2,))
                    for j in range(2):
                        for kt in range(2):
                            mm = nc.tensor.matmul(scores.t[:, j, :], wglu[:, kt, j * P:(j + 1) * P], yg[:, kt, 0:HALF], start=kt == 0, stop=kt == 1)
                    mm.then_inc(*scores.full.inc(s + (2,)))
                    if odd:
                        upd.claim(pe, s + ("glu",))
                        for j in range(2):
                            for kt in range(2):
                                mm = nc.tensor.matmul(upd.t[:, j * TS:(j + 1) * TS], wglu[:, kt, j * P:(j + 1) * P], yg[:, kt, HALF:W], start=kt == 0, stop=kt == 1)
                        mm.then_inc(*upd.full.inc(s + ("glu",)))
                elif s[0] == "mlpre":
                    n = s[1]
                    scores.claim(pe, s + (0,))
                    for k in [k for k in pieces if k[:2] == (n, "ml_ifg")]:
                        pe.wait_ge(*PB[bank_of[k]].free.at(k))
                    for t in range(NCH):
                        for i in range(2):
                            mm = nc.tensor.transpose(scores.t[0:4, i, t * P:(t + 1) * P], ifc[:, t, 4 * i:4 * i + 4], ident)
                    mm.then_inc(*scores.full.inc(s + (0,)))
                    if n % 2:
                        upd.claim(pe, s + ("s",))
                        for i in range(2):
                            mm = nc.tensor.transpose(upd.t[0:4, TS * i:TS * i + TS], ifc[0:TS, NCH, 4 * i:4 * i + 4], ident[0:TS, 0:TS])
                        mm.then_inc(*upd.full.inc(s + ("s",)))
                elif s in mixes:
                    br, n, c = s
                    T, cc = chunk_len(c), cols(c)
                    sample = c == NCH
                    stt = ST if c < NCH else STs
                    dv = 65 if br == "ml" else 64
                    if br == "hg":
                        pe.wait_ge(*hg_prod.at(s))
                    elif br == "rt":
                        pe.wait_ge(*rot_done.at(n))
                    else:
                        pe.wait_ge(*pre_dve.at(("mlpre", n, 0)))
                    if c in (0, NCH):
                        for k in [k for k in pieces if k[0] == n and k[1] in ("hg_i", "rt_v", "ml_v", "ml_k", "ml_q") and k[1][:2] == br]:
                            pe.wait_ge(*PB[bank_of[k]].free.at(k))

                    def v(h):
                        if br == "ml":
                            return mvv[0:T, c, h, :]
                        return (hv if br == "hg" else rv)[0:T, c, h * 64:h * 64 + 64]

                    def q(h):
                        if br == "hg":
                            return QD[:, h // 2, h % 2, 0:T]
                        return (rq if br == "rt" else mq)[:, h, cc]

                    def state(h, b=None):
                        j = 0 if br == "rt" else h // 2
                        if b is not None:
                            return sst[:, j, b, 0:dv]
                        return S_rt[:, :] if br == "rt" else (S_hg if br == "hg" else S_ml)[:, j, :]

                    def score_bank(j):
                        scores.claim(pe, s + (j,))
                        if br == "hg":
                            u = T // 2
                            for par in range(2):
                                r = slice(par * 64, par * 64 + 64)
                                for i, w in enumerate(levels(c)):
                                    mm = nc.tensor.matmul(scores.t[0:T, par, i * u:(i + 1) * u], E[r, i, j, 0:T],
                                                          split(E[r, i, j, 0:T], w)[:, :, 1], start=True, stop=True)
                        elif br == "rt":
                            mm = nc.tensor.matmul(scores.t[0:T, 0, 0:4 * T].rearrange("p (h t) -> p h t", h=4), rk[:, cc], rq[:, :, cc], start=True, stop=True)
                        else:
                            for i in range(2):
                                nc.tensor.matmul(scores.t[0:T, 0, i * 2 * T:(i + 1) * 2 * T].rearrange("p (h t) -> p h t", h=2),
                                                 mk[:, i, cc], mq[:, 2 * i:2 * i + 2, cc], start=True, stop=True)
                            for h in range(4):
                                mm = nc.tensor.matmul(scores.t[0:T, 1, h * T:(h + 1) * T], ident[0:4, h:h + 1].broadcast_to([4, T]),
                                                      rows[:, A_, cc], start=True, stop=True)
                        mm.then_inc(*scores.full.inc(s + (j,)))

                    tk = s + ("turn",)
                    aux.claim(pe, tk)
                    if br == "rt":
                        mm = nc.tensor.transpose(aux.t[0:T, 0:P], rk[:, cc], ident)
                    else:
                        for j in range(2):
                            src = E[:, 7, j, 0:T] if br == "hg" else mk[:, j, cc]
                            mm = nc.tensor.transpose(aux.t[0:T, j * P:(j + 1) * P], src, ident)
                    if br == "hg":
                        for j in range(2):
                            mm = nc.tensor.matmul(aux.t[0:T, 256 + 2 * j:258 + 2 * j], E[:, 9, j, 0:T], C("headsel"), start=True, stop=True)
                    if br == "ml":
                        for i, slot in enumerate((G_, SP_, M_, WK_)):
                            nc.tensor.transpose(aux.t[0:T, 256 + 4 * i:260 + 4 * i], rows[:, slot, cc], ident[0:4, 0:4])
                        nb = NB if sample else 1
                        for j in range(2):
                            lhs = C("selj")[:, j * P:(j + 1) * P]
                            last = rows[:, SP_, HALF + DSEQ - 1:W:DSEQ] if sample else rows[:, SP_, cc.stop - 1:cc.stop]
                            mm = nc.tensor.matmul(aux.t[:, 272 + nb * j:272 + nb * (j + 1)], lhs, last, start=True, stop=True)
                    mm.then_inc(*aux.full.inc(tk))
                    score_bank(0)
                    if br == "hg":
                        score_bank(1)
                    if sample:
                        ik = s + ("inter",)
                        upd.claim(pe, ik)
                        pe.wait_ge(*ss_in.at(s + (ss_parts[br] - 1,)))
                        for h in range(4):
                            for b in range(NB):
                                mm = nc.tensor.matmul(upd.t[0:dv, h * TS + DSEQ * b:h * TS + DSEQ * (b + 1)], state(h, b),
                                                      q(h)[:, DSEQ * b:DSEQ * (b + 1)], start=True, stop=True)
                        mm.then_inc(*upd.full.inc(ik))
                        pe.wait_ge(*upd.free.at(ik))
                    elif [k for k in upd_keys if k[:3] == s or k[:3] != s and upd_keys.index(k) < upd_keys.index(s + ("U",))][:-1]:
                        pe.wait_ge(*upd.free.at(before(upd_keys, s + ("U",))))
                    pe.wait_ge(*st_done.at(s))
                    outb.claim(pe, s)
                    for h in range(4):
                        o = outb.t[0:T, h * dv:(h + 1) * dv]
                        if br != "ml":
                            if sample:
                                nc.tensor.matmul(o, oT[0:dv, h, :], ident[0:dv, 0:dv], start=True, stop=False)
                            else:
                                nc.tensor.matmul(o, q(h), state(h), start=True, stop=False)
                        mm = nc.tensor.matmul(o, stt[0:T, h, 0:T], v(h), start=br == "ml", stop=True)
                    mm.then_inc(*outb.full.inc(s))
                    if br == "ml":
                        ak = s + (1,)
                        scores.claim(pe, ak)
                        for h in range(4):
                            o = scores.t[0:T, 0, h * dv:(h + 1) * dv]
                            if sample:
                                mm = nc.tensor.matmul(o, oT[0:dv, h, :], ident[0:dv, 0:dv], start=True, stop=True)
                            else:
                                mm = nc.tensor.matmul(o, q(h), state(h), start=True, stop=True)
                        mm.then_inc(*scores.full.inc(ak))
                    pe.wait_ge(*aux.free.at(tk))
                    dk = 32 if br == "rt" else 64
                    if not sample:
                        uk = s + ("U",)
                        upd.claim(pe, uk)
                        for h in range(4):
                            p0 = 32 * h if br == "rt" else h % 2 * 64
                            c0 = 0 if br == "rt" else h // 2 * dv
                            mm = nc.tensor.matmul(upd.t[p0:p0 + dk, c0:c0 + dv], kT[0:T, h * dk:(h + 1) * dk], v(h), start=True, stop=True)
                        mm.then_inc(*upd.full.inc(uk))
                    else:
                        if br == "ml":
                            nk = s + ("n",)
                            upd.claim(pe, nk)
                            for h in range(4):
                                p0 = h % 2 * 64
                                mm = nc.tensor.matmul(upd.t[p0:p0 + 64, h // 2 * NB:(h // 2 + 1) * NB], kT[0:T, h * 64:h * 64 + 64], C("bmask"), start=True, stop=True)
                            mm.then_inc(*upd.full.inc(nk))
                        sk = s + ("su",)
                        scores.claim(pe, sk)
                        for h in range(4):
                            p0 = 32 * h if br == "rt" else h % 2 * 64
                            pe.wait_ge(*vexp_done.at(s + (h,)))
                            nc.tensor.matmul(scores.t[p0:p0 + dk, 0 if br == "rt" else h // 2, :], kT[0:T, h * dk:(h + 1) * dk], ex[0:T, :],
                                             start=True, stop=True).then_inc(*vexp_used.inc(s + (h,)))
                        pe.wait_ge(*vexp_used.at(s + (3,)))
                        nc.tensor.matmul(aux.t[0:1, 500:501], ident[:, 0:1], ident[:, 0:1], start=True, stop=True).then_inc(*scores.full.inc(sk))
                    pe.wait_ge(*y_done.at(s))
                    xk = s + ("mixed",)
                    aux.claim(pe, xk)
                    for j in range(2):
                        mm = nc.tensor.transpose(aux.t[:, j * P:j * P + T], y[0:T, 2 * j:2 * j + 2, :], ident[0:T, 0:T])
                    mm.then_inc(*aux.full.inc(xk))
                elif s[0] == "out":
                    n = s[1]
                    if s5n:
                        pe.wait_ge(*s5_dve.at(("s5", n, "mixed")))
                    done = [k for k in aux_keys if k[0] != "s5set" and k[1] <= n]
                    if done:
                        pe.wait_ge(*aux.free.at(done[-1]))
                    for k in outs_of(n):
                        b = (n, "wo", k[1])
                        if k[2] == 0:
                            pe.wait_ge(*wr_in[wslot[b]].at(b))
                        bank = PB[bank_of[k]]
                        bank.claim(pe, k)
                        r = chunk_len(k[2])
                        for kt in range(8):
                            mm = nc.tensor.matmul(bank.t[0:r, 0:256], mixT[:, kt, k[2] * P:k[2] * P + r], wraw[:, wslot[b], kt, 0:256],
                                                  start=kt == 0, stop=kt == 7)
                        mm.then_inc(*bank.full.inc(k))


OUTPUTS = {
    "y_prompt": (1, SEQ, D), "y_sample": (NB, DSEQ, D),
    "p_s5_re": (DEPTH, 1, 16, 64), "p_s5_im": (DEPTH, 1, 16, 64), "p_hgrn": (DEPTH, 1, 4, 64, 64),
    "p_mlstm_C": (DEPTH, 1, 4, 64, 64), "p_mlstm_n": (DEPTH, 1, 4, 64), "p_mlstm_m": (DEPTH, 1, 4),
    "p_ret": (DEPTH, 1, 4, 32, 64),
    "d_s5_re": (DEPTH, NB, 16, 64), "d_s5_im": (DEPTH, NB, 16, 64), "d_hgrn": (DEPTH, NB, 4, 64, 64),
    "d_mlstm_C": (DEPTH, NB, 4, 64, 64), "d_mlstm_n": (DEPTH, NB, 4, 64), "d_mlstm_m": (DEPTH, NB, 4),
    "d_ret": (DEPTH, NB, 4, 32, 64),
}


def kernel(**inputs):
    import concourse.bacc as bacc
    from concourse.bass_utils import run_bass_kernel_spmd

    nc = bacc.Bacc("TRN2", target_bir_lowering=False, num_devices=1)
    packed, masks, rot = constants()
    arrays = {"c_packed": packed, "c_masks": masks, "c_rot": rot}
    arrays.update({k: np.ascontiguousarray(v) for k, v in inputs.items()})
    inp = {k: nc.dram_tensor("in_" + k, a.shape, mybir.dt.from_np(a.dtype), kind="ExternalInput").ap() for k, a in arrays.items()}
    out = {k: nc.dram_tensor("out_" + k, shape, F32, kind="ExternalOutput").ap() for k, shape in OUTPUTS.items()}
    trunk_kernel(nc, inp, out)
    r = run_bass_kernel_spmd(nc, [{"in_" + k: a for k, a in arrays.items()}], core_ids=[0])
    return tuple(r.results[0]["out_" + k] for k in OUTPUTS)
```

```python
from contextlib import ExitStack

import numpy as np

import concourse.bass as bass
from concourse import mybir

F32 = mybir.dt.float32
F32R = mybir.dt.float32r
U8 = mybir.dt.uint8
ALU = mybir.AluOpType
ACT = mybir.ActivationFunctionType
AX = mybir.AxisListType.X

P = 128
D = 1024
KT = D // P
SEQ, DEPTH, NB, DSEQ = 1024, 2, 8, 4
PAST = 8192
HALF = SEQ // 2
TS = NB * DSEQ
W = HALF + TS
WP = HALF + P
CH = 128
NCH = HALF // CH
WC = 264
D_IN = 3592
EPS = 1e-6

BLOCKS = [
    ("hg_f", 768, 256, "ch", "a"), ("hg_i", 1024, 256, "tok", "a"),
    ("hg_q", 512, 256, "ch", "av"), ("hg_g", 1280, 256, "tok", "av"),
    ("ml_ifg", 2560, 264, "tok", "av"),
    ("ml_q", 1536, 256, "ch", "a"), ("ml_k", 1792, 256, "ch", "a"),
    ("ml_v", 2048, 256, "tok", "a"), ("ml_o", 2304, 256, "tok", "a"),
    ("rt_qk", 2824, 256, "ch", "v"), ("rt_v", 3080, 256, "tok", "a"), ("rt_g", 3336, 256, "tok", "av"),
    ("s5_x", 0, 256, "ch", "a"), ("s5_g", 256, 256, "ch", "av"),
]
BLOCK = {b[0]: b for b in BLOCKS}


class Signal:

    def __init__(self, nc, ctx, name, keys, unit=1):
        self.sem = ctx.enter_context(nc.semaphore(name))
        self.name, self.unit, self.fired, self.keys = name, unit, set(), list(keys)
        self.value = {k: unit * (i + 1) for i, k in enumerate(self.keys)}

    def inc(self, key):
        assert key in self.value and key not in self.fired, (self.name, key)
        self.fired.add(key)
        return self.sem, self.unit

    def at(self, key):
        return self.sem, self.value[key]


class Chain:

    def __init__(self, nc, ctx, name):
        self.sem, self.n = ctx.enter_context(nc.semaphore(name)), 0

    def inc(self):
        self.n += 1
        return self.sem, 1

    def now(self):
        return self.sem, self.n


class Bank:

    def __init__(self, nc, ctx, name, uses, tensor):
        self.t = tensor
        self.full = Signal(nc, ctx, name + "_full", uses)
        self.free = Signal(nc, ctx, name + "_free", uses)

    def claim(self, pe, key):
        i = self.full.keys.index(key)
        if i:
            pe.wait_ge(*self.free.at(self.full.keys[i - 1]))


def pieces_of_block(n, name):
    odd = n % 2
    kinds = ([(j, m) for j in range(2) for m in range(1 + odd)] if BLOCK[name][3] == "ch"
             else [(t,) for t in range(NCH + odd)])
    return [(n, name) + k for k in kinds]


def weave(a, b):
    def groups(steps):
        out = []
        for x in steps:
            if out and (x[1] in ("A0", "A1", "u", "store") or x[1] is None or isinstance(x[1], tuple) and x[1][0] == "take"):
                out[-1].append(x)
            else:
                out.append([x])
        return out

    a, b = groups(a), groups(b)
    out, i, j = [], 0, 0
    while i < len(a) or j < len(b):
        if j >= len(b) or (i < len(a) and i * len(b) <= j * len(a)):
            out += a[i]
            i += 1
        else:
            out += b[j]
            j += 1
    return out


def make_plan(parts):
    passes = range(2 * DEPTH)

    def project(n, br, after=None):
        out, late = [], []
        for b in BLOCKS:
            if b[0][:2] == br and br in parts:
                ks = pieces_of_block(n, b[0])
                for k in ks:
                    out += [(("proj", n, b[0]), ("mm", k))] + late
                    late = [(("proj", n, b[0]), ("take", k))]
                late += (after or {}).get(b[0], [])
        return out + late

    def mix(n, br):
        if br not in parts:
            return []
        cs, out = range(NCH + n % 2), []
        if br == "hg":
            out += [((br, n, 0), "A0"), ((br, n, 0), "A1")]
        for c in cs:
            out.append(((br, n, c), "B0"))
            if br == "hg":
                out.append(((br, n, c), "B1"))
                if c + 1 in cs:
                    out.append(((br, n, c + 1), "A0"))
            if c:
                out.append(((br, n, c - 1), "D"))
            out.append(((br, n, c), "C"))
            if br == "hg" and c + 1 in cs:
                out.append(((br, n, c + 1), "A1"))
        return out + [((br, n, cs[-1]), "D")]

    def norm(n):
        return [(("norm", n), t) for t in range(NCH + n % 2)]

    def outs(n):
        return [(("out", n), (n, b, t)) for b in range(4) for t in range(NCH + n % 2)]

    def s5set(l):
        return [(("s5set", l), x) for x in ("c", "v", "w", "s")] if "s5" in parts else []

    def s5(n, stages):
        return [(("s5", n), x) for x in stages] if "s5" in parts else []

    plan = norm(0) + weave(project(0, "hg", {"hg_f": [(("hgpre", 0), None)]}), s5set(0)[:2]) + s5set(0)[2:]
    head = mix(0, "hg")
    for n in passes:
        plan += weave(head, project(n, "ml", {"ml_ifg": [(("mlpre", n), None)]}))
        plan += [(("mlpre", n), "store")] if "ml" in parts else []
        plan += weave(mix(n, "ml"), project(n, "rt"))
        half = project(n, "s5", {"s5_x": s5(n, "u")})
        if n + 1 in passes:
            plan += weave(mix(n, "rt"), half + norm(n + 1))
            plan += weave(s5(n, "wysgz"), project(n + 1, "hg", {"hg_f": [(("hgpre", n + 1), None)]}))
            head = mix(n + 1, "hg")
            k = head.index((("hg", n + 1, 0), "D")) if head else 0
            sets = s5set(1) if n == 0 else []
            plan += weave(outs(n), head[:2] + sets[:1] + head[2:k] + sets[1:])
            head = head[k:]
        else:
            last, o = [(("final",), t) for t in range(2 * NCH + 1)], outs(n)
            k = 3 * (NCH + 1)
            tail = o[k:k + 2]
            for t in range(NCH + 1):
                tail += o[k + 2 + t:k + 3 + t] + last[NCH + t:NCH + t + 1]
            plan += weave(mix(n, "rt"), half + s5(n, "wys")) + s5(n, "gz") + weave(o[:k], last[:NCH]) + tail
    return plan


LEVELS = [64, 32, 16, 8, 4, 2, 1]
NL = len(LEVELS)
SLEV = [2, 1]
CONST = {}


def constants():
    p = np.arange(P)[:, None]
    t = np.arange(P)[None, :]
    same = (np.arange(TS)[:, None] // DSEQ == np.arange(TS)[None, :] // DSEQ)
    tri = np.arange(TS)[None, :] >= np.arange(TS)[:, None]
    first = np.ones(W, np.float32)
    first[0:HALF:CH] = 0
    first[HALF:W:DSEQ] = 0
    parts = {
        "ident": np.eye(P),
        "reset": np.broadcast_to(first, (P, W)),
        "causal": t >= p,
        "cneg": np.where(t >= p, 0.0, -1e30),
        "causal_s": same & tri,
        "cneg_s": np.where(same & tri, 0.0, -1e30),
        "selj": np.stack([(np.arange(4)[:, None] == 2 * j + (np.arange(P) >= 64)[None, :]) for j in range(2)], 1).reshape(4, -1),
        "headsel": np.arange(P)[:, None] // 64 == np.arange(2)[None, :],
        "halfpi": np.full((P, 1), np.pi / 2),
        "gam": (1 - 2.0 ** (-5.0 - p // 32)) ** np.array([[CH, DSEQ]]),
        "bmask": np.arange(TS)[:, None] // DSEQ == np.arange(NB)[None, :],
    }
    at, cols = 0, []
    for k, a in parts.items():
        a = np.asarray(a, np.float32)
        full = np.zeros((P, a.shape[1]), np.float32)
        full[:a.shape[0]] = a
        CONST[k] = (at, a.shape[0], a.shape[1])
        at += a.shape[1]
        cols.append(full)
    masks = np.zeros((P, NL * 64 + 2 * 16 + P), np.float32)
    for i, w in enumerate(LEVELS):
        u = np.arange(64)
        blk = u // w
        masks[:, i * 64:(i + 1) * 64] = (p // (2 * w) == blk) & (p % (2 * w) < w)
    for i, w in enumerate(SLEV):
        u = np.arange(16)
        masks[:TS, NL * 64 + i * 16:NL * 64 + (i + 1) * 16] = ((p // (2 * w) == u // w) & (p % (2 * w) < w))[:TS]
    masks[:, NL * 64 + 32:] = np.eye(P)
    rot = np.zeros((2, P, 4, W), np.float32)
    inv = (np.float32(10000.0) ** (-np.arange(16, dtype=np.float32) / np.float32(16)))
    i = np.arange(P) % 32
    gamma = 1 - 2.0 ** (-5.0 - np.arange(P) // 32)
    for half in range(2):
        pos = np.concatenate([np.arange(HALF) + HALF * half, PAST + np.arange(TS) % DSEQ]).astype(np.float32)
        loc = np.concatenate([np.arange(HALF) % CH, np.arange(TS) % DSEQ]) + 1
        ang = (pos[None, :] * inv[i % 16][:, None]).astype(np.float32).astype(np.float64)
        c, s = np.cos(ang), np.where(i < 16, -1, 1)[:, None] * np.sin(ang)
        up, down = gamma[:, None] ** loc[None, :], gamma[:, None] ** -loc[None, :].astype(float) * 32 ** -0.5
        rot[half] = np.stack([c * up, s * up, c * down, s * down], 1)
    return np.concatenate(cols, 1), masks, rot.reshape(2, P, 4 * W)


constants()


def trunk_kernel(nc, inp, out, parts=("hg", "ml", "rt", "s5")):
    plan = make_plan(parts)
    ctx = ExitStack()
    with ctx:
        def sb(name, shape, dt=F32):
            return ctx.enter_context(nc.sbuf_tensor(name, shape, dt))

        def signal(name, keys, unit=1):
            return Signal(nc, ctx, name, keys, unit)

        def tiles_of(n):
            return range(NCH + n % 2)

        def chunk_len(c):
            return CH if c < NCH else TS

        def cols(c):
            return slice(c * CH, c * CH + chunk_len(c))

        def outs_of(n):
            return [(n, b, t) for b in range(4) for t in tiles_of(n)]

        steps = list(dict.fromkeys(s for s, _ in plan))
        norm_tiles = [(s[1], t) for s in steps if s[0] == "norm" for t in tiles_of(s[1])]
        final_tiles = [("final", t) for t in range(2 * NCH + 1)]
        all_tiles = norm_tiles + final_tiles
        tslot = {k: i % 2 for i, k in enumerate(all_tiles)}
        in_blocks = [s[1:] for s in steps if s[0] == "proj"]
        pieces = [part[1] for s, part in plan if s[0] == "proj" and part[0] == "mm"]
        out_pieces = [k for s in steps if s[0] == "out" for k in outs_of(s[1])]
        w_loads, proj_uses = [], []
        for s, part in plan:
            if s[0] == "norm":
                proj_uses += [("norm", s[1], part, g) for g in range(2)]
            elif s[0] == "proj" and part[0] == "mm":
                if part[1] == pieces_of_block(*s[1:])[0]:
                    w_loads.append(s[1:])
                proj_uses.append(part[1])
            elif s[0] == "out":
                if part[2] == 0:
                    w_loads.append((s[1], "wo", part[1]))
                proj_uses.append(part)
        bank_of = {k: i % 3 for i, k in enumerate(proj_uses)}
        wslot = {k: i % 2 for i, k in enumerate(w_loads)}
        hslot = {k: i % 2 for i, k in enumerate(in_blocks)}
        oslot = {k: i % 3 for i, k in enumerate(out_pieces)}
        last_piece = {b: [k for k in pieces if k[:2] == b][-1] for b in in_blocks}
        mixes = [s for s in steps if s[0] in ("hg", "ml", "rt")]
        pres = [s for s in steps if s[0] in ("hgpre", "mlpre")]
        mix_tile = {"s5": 0, "hg": 2, "ml": 4, "rt": 6}
        score_keys, upd_keys, aux_keys = [], [], []
        for s, part in plan:
            odd = s[0] != "final" and s[1] % 2
            if s[0] == "s5set" and part == "c":
                aux_keys.append(s + ("C",))
            elif s[0] == "s5set" and part == "w":
                score_keys += [s + (i,) for i in range(4)]
            elif s[0] == "s5" and part == "w":
                score_keys.append(s + (0,))
                upd_keys += [s + ("w",)] * odd
            elif s[0] == "s5" and part == "y":
                score_keys.append(s + (1,))
                upd_keys += [s + ("y",)] * odd
                aux_keys += [s + ("y",)] * odd
            elif s[0] == "s5" and part == "z":
                score_keys.append(s + (2,))
                upd_keys += [s + ("glu",)] * odd
            elif s[0] == "mlpre" and part is None:
                score_keys.append(s + (0,))
                upd_keys += [s + ("s",)] * odd
            elif s in mixes and part == "B0":
                aux_keys.append(s + ("turn",))
                score_keys.append(s + (0,))
            elif s in mixes and part == "B1":
                score_keys.append(s + (1,))
            elif s in mixes and part == "C":
                sample = s[2] == NCH
                upd_keys += [s + ("inter",)] * sample
                score_keys += [s + (1,)] * (s[0] == "ml") + [s + ("su",)] * sample
                upd_keys += [s + ("n",)] * (s[0] == "ml") if sample else [s + ("U",)]
            elif s in mixes and part == "D":
                aux_keys.append(s + ("mixed",))
        samples = [m for m in mixes if m[2] == NCH]

        psum = ctx.enter_context(nc.psum_tensor("psum", [P, 8, 512], F32))
        PB = [Bank(nc, ctx, f"proj{i}", [k for k in proj_uses if bank_of[k] == i], psum[:, i, :]) for i in range(3)]
        scores = Bank(nc, ctx, "scores", score_keys, psum[:, 3:5, :])
        outb = Bank(nc, ctx, "outb", mixes, psum[:, 5, :])
        aux = Bank(nc, ctx, "aux", aux_keys, psum[:, 6, :])
        upd = Bank(nc, ctx, "upd", upd_keys, psum[:, 7, :])

        const = sb("const", [P, inp["c_packed"].shape[1]])
        cm = sb("cm", [P, inp["c_masks"].shape[1]], U8)

        def C(name):
            at, rows, width = CONST[name]
            return const[0:rows, at:at + width]

        ident = C("ident")
        hhi = sb("hhi", [P, KT, W], F32R)
        hlo = sb("hlo", [P, KT, W], F32R)
        wraw = sb("wraw", [P, 2, KT, WC])
        whi = sb("whi", [P, 2, KT, WC], F32R)
        wlo = sb("wlo", [P, 2, KT, WC], F32R)
        mixT = sb("mixT", [P, 8, W])
        xo = sb("xo", [P, 3, 256])
        th = sb("th", [P, 2, 512])
        ssq = sb("ssq", [P, 2])
        rstd = sb("rstd", [P, 2])
        epow = sb("epow", [P, 4])
        stats = sb("stats", [P, 4, 6])
        mv = sb("mv", [P, 4, 2])
        rs = sb("rs", [P, 4])
        ST = sb("ST", [P, 4, CH])
        STs = sb("STs", [TS, 4, TS])
        kT = sb("kT", [P, 256])
        y = sb("y", [P, 4, 64])
        ex = sb("ex", [P, 512])
        oT = sb("oT", [65, 4, TS])
        small = sb("small", [P, 64])
        sst = sb("sst", [P, 2, NB, 65])
        S_hg = sb("S_hg", [P, 2, 64])
        S_ml = sb("S_ml", [P, 2, 65])
        S_rt = sb("S_rt", [P, 64])
        QE = sb("QE", [P, NL, 2, 64])
        hdec = sb("hdec", [P, 2, NB])
        lb = sb("lb", [P, 8])
        gb = sb("gb", [4, 8])
        m0 = sb("m0", [4, NB])
        mp = sb("mp", [4, NCH])

        class Carve:
            def __init__(self, name, size):
                self.t, self.at, self.size, self.name = sb(name, [P, size]), 0, size, name

            def take(self, *shape, rows=P):
                n = int(np.prod(shape))
                v = self.t[0:rows, self.at:self.at + n]
                self.at += n
                assert self.at <= self.size, (self.name, self.at)
                if len(shape) > 1:
                    names = "abcd"[:len(shape)]
                    v = v.rearrange(f"p ({' '.join(names)}) -> p {' '.join(names)}", **dict(zip(names[1:], shape[1:])))
                return v

        R1, R2 = Carve("r1", 8896), Carve("r2", 10200)
        cm_wide = R1.take(inp["c_masks"].shape[1])
        R1.at = 0
        hq, hk, hcum = R1.take(2, W), R1.take(2, W), R1.take(2, W)
        hv, hgate = R1.take(5, 256), R1.take(5, 256)
        at = R1.at
        E, QD = R1.take(10, 2, CH), R1.take(2, 2, CH)
        R1.at = at
        hf, hu = R1.take(2, W), R1.take(2, W)
        R1.at = 0
        rq, rk = R1.take(4, W), R1.take(W)
        rv, rgate = R1.take(5, 256), R1.take(5, 256)
        at = R1.at
        rtab, rtmp = R1.take(4, W), R1.take(2, HALF)
        R1.at = at
        xt, normw = R1.take(2, D), R1.take(D)
        mq, mk = R2.take(4, W), R2.take(2, W)
        mvv, mo, mgate = R2.take(5, 4, 65), R2.take(5, 256), R2.take(5, 256)
        ifc = R2.take(5, 8)
        rows = R2.take(5, W, rows=4)
        G_, SP_, M_, WK_, A_ = range(5)

        R2.at = 0
        cB, cBb, cCn, cCT = R2.take(2, 8, 16), R2.take(2, 8, 16), R2.take(2, 2, P), R2.take(2, 8, 16)
        cV, cW = R2.take(2, 8, 9, 16), R2.take(2, 8, 8, 16)
        cE = R2.take(2, 8, 64)
        at = R2.at
        ct = [R2.take(8 * 9 * 16) for _ in range(2)]
        R2.at = at
        cWT = R2.take(8, 2, P)
        cK = cW.rearrange("p r q s c -> p (r q s c)")[0:16, :].rearrange("p (g x) -> p g x", g=16)
        R2.at = 0
        ux, U = R2.take(2, W), R2.take(16, 72)
        sG = R2.take(2, 8, 64)
        at = R2.at
        sX, sE = R2.take(2, 8, 65), R2.take(2, 8, 64)
        R2.at = at
        yT = R2.take(2, W)
        R2.at = at + 8 * 65 * 2 + 1024
        sMx = R2.take(16 * P)
        sWT, sT = sMx.rearrange("p (q r x) -> p q r x", q=8, r=2), sMx.rearrange("p (g x) -> p g x", g=16)
        at = R2.at
        sV = R2.take(2, 8, P)
        R2.at = at
        stmp = [R2.take(8, 64) for _ in range(2)]
        R2.at = at
        yg = R2.take(2, W)
        R2.at = at + 2048
        wglu = R2.take(2, 256)
        sX0 = R2.take(2, 8, NB)
        sXf = R2.take(2, 8, NB)
        Yall = sG.rearrange("p r q b -> p (r q b)")
        Ys = sb("Ys", [64, 16, NB])
        gt = U.rearrange("p g b -> p (g b)")[:, 0:2 * W].rearrange("p (j w) -> p j w", j=2)
        s5c = sb("s5c", [P, DEPTH, 3, 8])
        s5v = sb("s5v", [P, 26, 16])
        s5i = sb("s5i", [P, 16], mybir.dt.int32)
        s5x = sb("s5x", [P, 2, 8])
        s5d = sb("s5d", [P, DEPTH, 2])
        s5p = sb("s5p", [P, 2, 16, 9])
        Tm = nc.dram_tensor("Tm", (DEPTH, 16, P, P), F32, kind="Internal").ap()
        WTm = nc.dram_tensor("WTm", (DEPTH, P, 16 * P), F32, kind="Internal").ap()
        VTm = nc.dram_tensor("VTm", (DEPTH, P, 2, 8, P), F32, kind="Internal").ap()
        Em = nc.dram_tensor("Em", (DEPTH, P, 1024), F32, kind="Internal").ap()
        ud = nc.dram_tensor("ud", (256, W), F32, kind="Internal").ap()
        yd = nc.dram_tensor("yd", (256, W), F32, kind="Internal").ap()

        gate_of = {"hg": hgate, "rt": rgate, "ml": mgate}
        x1 = nc.dram_tensor("x1", (SEQ + TS, D), F32, kind="Internal").ap()
        x2 = nc.dram_tensor("x2", (SEQ + TS, D), F32, kind="Internal").ap()

        def x_rows(x, n, t):
            return x[n % 2 * HALF + t * P:n % 2 * HALF + (t + 1) * P, :] if t < NCH else x[SEQ:SEQ + TS, :]

        def x_src(n, t):
            if n >= 2:
                return x_rows(x1, n, t)
            return x_rows(inp["x_prompt"][0], n, t) if t < NCH else inp["x_sample"].rearrange("b s d -> (b s) d")

        const_in = signal("const_in", range(9), 16)
        nw_in = signal("nw_in", [s[1] for s in steps if s[0] == "norm"] + ["final"], 16)
        xt_in = [signal(f"xt_in{s}", [k for k in all_tiles if tslot[k] == s], 16) for s in range(2)]
        ssq_done = signal("ssq_done", all_tiles)
        rstd_done = signal("rstd_done", all_tiles)
        h_done = signal("h_done", all_tiles)
        hhi_done = signal("hhi_done", [k + (g,) for k in norm_tiles for g in range(2)])
        y_out = [signal(f"y_out{s}", [k for k in final_tiles if tslot[k] == s], 16) for s in range(2)]
        wr_in = [signal(f"wr_in{s}", [k for k in w_loads if wslot[k] == s], 16) for s in range(2)]
        whi_done = signal("whi_done", in_blocks)
        wlo_done = signal("wlo_done", in_blocks)
        th_keys = [k for k in pieces if BLOCK[k[1]][4] == "av"]
        th_done = signal("th_done", th_keys)
        xo_in = [signal(f"xo_in{s}", [k for k in out_pieces if oslot[k] == s], 16) for s in range(3)]
        xo_sum = signal("xo_sum", out_pieces)
        xo_out = [signal(f"xo_out{s}", [k for k in out_pieces if oslot[k] == s], 16) for s in range(3)]
        rot_done = signal("rot_done", range(2 * DEPTH))
        ml_clear = signal("ml_clear", range(2 * DEPTH))
        tab_in = signal("tab_in", range(2 * DEPTH), 16)
        pool_done = Chain(nc, ctx, "pool_done")
        act_done = Chain(nc, ctx, "act_done")
        dve_done = Chain(nc, ctx, "dve_done")
        pool_setup = signal("pool_setup", ["all"])
        lb_exp = signal("lb_exp", ["in"])
        lb_done = signal("lb_done", ["diff", "all"])
        pre_act = signal("pre_act", [s + (i,) for s in pres for i in range(1 if s[0] == "mlpre" else 2 + s[1] // 2)])
        pre_dve = signal("pre_dve", [s + (i,) for s in pres for i in range(1 if s[0] == "mlpre" else 1 + s[1] // 2)])
        hg_mixes = [m for m in mixes if m[0] == "hg"]
        ml_mixes = [m for m in mixes if m[0] == "ml"]
        hg_diff = signal("hg_diff", hg_mixes)
        hg_exp = signal("hg_exp", hg_mixes)
        hg_prod = signal("hg_prod", [m + (j,) for m in hg_mixes for j in range(2)])
        ex_add = signal("ex_add", ml_mixes)
        ex_exp = signal("ex_exp", ml_mixes)
        st_done = signal("st_done", mixes)
        mv_done = signal("mv_done", mixes)
        rs_done = signal("rs_done", mixes)
        y_done = signal("y_done", mixes)
        vexp_done = signal("vexp_done", [m + (h,) for m in samples for h in range(4)])
        vexp_used = signal("vexp_used", [m + (h,) for m in samples for h in range(4)])
        ss_parts = {"hg": 4, "ml": 8, "rt": 4}
        m_in = signal("m_in", range(DEPTH), 16)
        m_out = signal("m_out", [(l, i) for l in range(DEPTH) for i in range(2)], 16)
        ss_in = signal("ss_in", [m + (i,) for m in samples for i in range(ss_parts[m[0]])], 16)
        ss_new = signal("ss_new", samples)
        ss_out = signal("ss_out", [m + (i,) for m in samples for i in range(ss_parts[m[0]])], 16)
        last_prompt = [m for m in mixes if m[1] % 2 and m[2] == NCH - 1]
        ps_parts = {"hg": 4, "ml": 8, "rt": 1}
        ps_out = signal("ps_out", [m + (i,) for m in last_prompt for i in range(ps_parts[m[0]])], 16)
        state_zero = signal("state_zero", [(l, "hg") for l in range(DEPTH)])

        s5n = [s for s in steps if s[0] == "s5"]
        s5sets = [s for s in steps if s[0] == "s5set"]
        set_in = signal("set_in", [s + (i,) for s in s5sets for i in range(6)], 16)
        vec_in = signal("vec_in", range(9), 16)
        vec_act = signal("vec_act", ["sin"])
        vec_dve = signal("vec_dve", ["phase", "all"])
        set_dve = signal("set_dve", [s + (i,) for s in s5sets for i in ("E", "V", "W")])
        set_out = signal("set_out", [s + (i,) for s in s5sets for i in range(11)], 16)
        set_zero = signal("set_zero", [(t, l) for t in range(1, 8) for l in range(DEPTH)], 16)
        s5_in = {i: signal(f"s5_in_{i}", s5n, 16) for i in ("E", "W", "G", "T", "V", "Y")}
        s5_u = signal("s5_u", [s + (i,) for s in s5n for i in range(8 + 4 * (s[1] % 2))], 16)
        s5_us = signal("s5_us", s5n, 16)
        s5_xi = signal("s5_xi", [s + (i, b) for s in s5n if s[1] % 2 for i in range(2) for b in range(NB)], 16)
        s5_y = signal("s5_y", [s + (i,) for s in s5n for i in range(8 + 4 * (s[1] % 2))], 16)
        s5_clear = signal("s5_clear", s5n)
        s5_rot = signal("s5_rot", s5n)
        s5_lin = signal("s5_lin", s5n)
        s5_act = signal("s5_act", [s + (i,) for s in s5n for i in ("sq", "tanh")])
        s5_dve = signal("s5_dve", [s + (i,) for s in s5n for i in ("skip", "cube", "gelu", "mixed")])
        s5_out = signal("s5_out", [s + (i, b) for s in s5n if s[1] % 2 for i in range(2) for b in ["p", *range(NB)]], 16)

        def piece_psum(key):
            if BLOCK[key[1]][3] == "ch":
                width = HALF if key[0] % 2 == 0 else W // 2
                c0 = width * key[3]
                return PB[bank_of[key]].t[:, 0:width], c0, width
            lo, hi = (0, P) if key[2] < NCH else (P - TS, P)
            return PB[bank_of[key]].t[lo:hi, 0:BLOCK[key[1]][2]], key[2], hi - lo

        def before(keys, key, back=1):
            i = keys.index(key)
            return keys[i - back] if i >= back else None

        def split_after(s, part):
            if s[0] == "norm":
                return part == 1 and s[1] == 0
            i = None
            if s[0] == "proj" and part == ("mm", pieces_of_block(*s[1:])[0]):
                i = w_loads.index(s[1:]) + 1
            if s[0] == "out" and part[1:] == (3, 1):
                i = w_loads.index((s[1], "wo", 3)) + 1
            return i is not None and i < len(w_loads) and w_loads[i][1] != "wo"

        def levels(c):
            return LEVELS if c < NCH else SLEV

        def split(ap, w):
            return ap.rearrange("p (n g w) -> p n g w", g=2, w=w)

        ctx.enter_context(nc.allow_non_contiguous_dma(reason="a few small rows of parameters and states"))
        block = ctx.enter_context(nc.Block())

        @block.sync
        def _(sp):
            loads = list(w_loads)

            def load_weights():
                k = loads.pop(0)
                prev = before(w_loads, k, 2)
                if prev is not None:
                    if prev[1] == "wo":
                        sp.wait_ge(*PB[bank_of[(prev[0], prev[2], tiles_of(prev[0])[-1])]].full.at((prev[0], prev[2], tiles_of(prev[0])[-1])))
                    else:
                        sp.wait_ge(*whi_done.at(prev))
                        sp.wait_ge(*wlo_done.at(prev))
                l = k[0] // 2
                if k[1] == "wo":
                    src, width = inp["w_out"][l][:, k[2] * 256:(k[2] + 1) * 256], 256
                else:
                    _, c0, width, _, _ = BLOCK[k[1]]
                    src = inp["w_in"][l][:, c0:c0 + width]
                sp.dma_start(wraw[:, wslot[k], :, 0:width], src.rearrange("(k p) c -> p k c", p=P)
                             ).then_inc(*wr_in[wslot[k]].inc(k))

            def load_until(i):
                while loads and len(w_loads) - len(loads) <= i:
                    load_weights()

            def load_x(k):
                n, t = k
                if k in final_tiles:
                    src = x_rows(x2, 1, NCH) if t == 2 * NCH else x_rows(x2, t // NCH, t % NCH)
                else:
                    src = x_src(n, t)
                prev = before(all_tiles, k, 2)
                if prev is not None:
                    if prev in final_tiles:
                        sp.wait_ge(*y_out[tslot[prev]].at(prev))
                    else:
                        sp.wait_ge(*PB[bank_of[("norm",) + prev + (1,)]].full.at(("norm",) + prev + (1,)))
                sp.dma_start(xt[0:P if t != (NCH if n != "final" else 2 * NCH) else TS, tslot[k], :], src).then_inc(*xt_in[tslot[k]].inc(k))

            def stored(n):
                for s in range(3):
                    ks = [k for k in out_pieces if k[0] <= n and oslot[k] == s]
                    sp.wait_ge(*xo_out[s].at(ks[-1]))

            def norm_weights(n):
                src = inp["final_norm_w"] if n == "final" else inp["norm_w"][n // 2]
                sp.dma_start(normw[:, :], src.rearrange("(o d) -> o d", o=1).broadcast_to([P, D])).then_inc(*nw_in.inc(n))

            norm_weights(0)
            load_x((0, 0))
            sp.dma_start(const[:, :], inp["c_packed"]).then_inc(*const_in.inc(0))
            sp.dma_start(cm_wide, inp["c_masks"]).then_inc(*const_in.inc(1))
            sp.dma_start(lb[:, 0:4].rearrange("p (l j) -> p l j", l=2),
                         inp["hgrn_lb_logits"].rearrange("l (j p) -> p l j", p=P)).then_inc(*const_in.inc(2))
            sp.dma_start(gb[:, 0:2], inp["mlstm_b_i"].rearrange("l h -> h l")).then_inc(*const_in.inc(3))
            sp.dma_start(gb[:, 2:4], inp["mlstm_b_f"].rearrange("l h -> h l")).then_inc(*const_in.inc(4))
            load_x((0, 1))
            load_until(1)
            if s5n:
                v3 = lambda i: s5v[:, i, :].rearrange("p (l q) -> p l q", l=DEPTH)
                for l in range(DEPTH):
                    sp.dma_start(v3(0)[:, l], inp["s5_lambda_re"][l].rearrange("(q a) p -> (a p) q", a=2)).then_inc(*vec_in.inc(4 * l))
                    sp.dma_start(v3(1)[:, l], inp["s5_lambda_im"][l].rearrange("(q a) p -> (a p) q", a=2)).then_inc(*vec_in.inc(4 * l + 1))
                    for a in range(2):
                        sp.dma_start(v3(2)[64 * a:64 * a + 64, l], inp["s5_log_dt"][l].rearrange("(o q a) -> a o q", a=2, o=1)[a].broadcast_to([64, 8])
                                     ).then_inc(*vec_in.inc(4 * l + 2 + a))
                sp.dma_start(s5d[:, :, :], inp["s5_D"].rearrange("l (j p) -> p l j", p=P)).then_inc(*vec_in.inc(8))

            def permuted(ap, t):
                a = ap.rearrange("(g c) w -> c g w", c=16)
                return a[:, :, t * 64:(t + 1) * 64] if t < 8 else a[:, :, HALF + (t - 8) * NB:HALF + (t - 7) * NB]

            for s, part in plan:
                if s[0] == "s5set" and part == "c":
                    l = s[1]
                    if l:
                        sp.wait_ge(*s5_dve.at(("s5", 0, "mixed")))
                    for ri, nm in enumerate(("re", "im")):
                        sp.dma_start(cB[:, ri], inp["s5_B_" + nm][l].rearrange("(q a) p c -> (a p) q c", a=2)).then_inc(*set_in.inc(s + (ri,)))
                        for d in range(2):
                            sp.dma_start(cCn[:, ri, :, 64 * d:64 * d + 64], inp["s5_C_" + nm][l].rearrange("(f g) c p -> (g c) f p", f=2)
                                         ).then_inc(*set_in.inc(s + (2 + 2 * ri + d,)))
                    for t in range(1, 8) if l == 0 else ():
                        z = mixT[0:16, :, :].rearrange("p k w -> p (k w)")[:, 0:16 * 16 * t].rearrange("p (g x) -> p g x", g=16)
                        for ll in range(DEPTH):
                            sp.dma_start(Tm[ll][:, 16 * t:16 * t + 16, 0:16 * t].rearrange("g c x -> c g x"), z).then_inc(*set_zero.inc((t, ll)))
                elif s[0] == "s5set" and part == "s":
                    l = s[1]
                    sp.wait_ge(*set_dve.at(s + ("E",)))
                    sp.dma_start(Em[l], cE.rearrange("p r q b -> p (r q b)")).then_inc(*set_out.inc(s + (0,)))
                    sp.wait_ge(*set_dve.at(s + ("V",)))
                    sp.dma_start(VTm[l].rearrange("p r q x -> p (r q) x"),
                                 cV.rearrange("p r q j c -> p (r q) (j c)")[:, :, 16:144]).then_inc(*set_out.inc(s + (1,)))
                    sp.wait_ge(*scores.free.at(s + (1,)))
                    sp.dma_start(WTm[l], cWT.rearrange("p q r x -> p (q r x)")).then_inc(*set_out.inc(s + (2,)))
                    sp.wait_ge(*scores.free.at(s + (3,)))
                    for t in range(8):
                        T_rows = Tm[l][:, 16 * t:16 * t + 16, :].rearrange("g c x -> c g x")
                        sp.dma_start(T_rows[:, :, 16 * t:], cK[:, :, 0:P - 16 * t]).then_inc(*set_out.inc(s + (3 + t,)))
                elif s[0] == "s5" and part == "u":
                    n, l = s[1], s[1] // 2
                    odd = n % 2
                    nt = 8 + 4 * odd
                    Wn = HALF + TS * odd
                    if n % 2 == 0:
                        sp.wait_ge(*set_out.at(("s5set", l, 10)))
                        sp.wait_ge(*set_zero.at(set_zero.keys[-1]))
                    mls = [m for m in mixes if m[0] == "ml" and m[1] == n]
                    if mls:
                        sp.wait_ge(*y_done.at(mls[-1]))
                        sp.wait_ge(*aux.full.at(mls[-1] + ("mixed",)))
                        if odd:
                            sp.wait_ge(*m_out.at((l, 1)))
                    sp.dma_start(sE.rearrange("p r q b -> p (r q b)"), Em[l]).then_inc(*s5_in["E"].inc(s))
                    sp.dma_start(sMx, WTm[l]).then_inc(*s5_in["W"].inc(s))
                    for k in [k for k in pieces if k[:2] == (n, "s5_x")]:
                        sp.wait_ge(*PB[bank_of[k]].free.at(k))
                    sp.dma_start(ud[:, 0:Wn].rearrange("(j p) w -> p j w", p=P), ux[:, :, 0:Wn]).then_inc(*s5_us.inc(s))
                    sp.wait_ge(*s5_us.at(s))
                    sp.wait_ge(*s5_clear.at(s))
                    for t in range(nt):
                        dst = U[16 * t:16 * t + 16, :, 0:64] if t < 8 else U[16 * (t - 4):16 * (t - 3), :, 64:72]
                        sp.dma_start(dst, permuted(ud, t)).then_inc(*s5_u.inc(s + (t,)))
                    if odd:
                        for ri, nm in enumerate(("re", "im")):
                            for b in range(NB):
                                v = inp["state_s5_" + nm][l, b].rearrange("(q a) p -> (a p) q", a=2)
                                sp.dma_start(sX0[:, ri, :, b], v).then_inc(*s5_xi.inc(s + (ri, b)))
                    sp.dma_start(wglu, inp["s5_w_glu"][l].rearrange("(k p) c -> p k c", p=P)).then_inc(*s5_in["G"].inc(s))
                elif s[0] == "s5" and part == "y":
                    n, l = s[1], s[1] // 2
                    sp.wait_ge(*scores.full.at(s + (0,)))
                    if n % 2:
                        sp.wait_ge(*upd.full.at(s + ("w",)))
                    sp.dma_start(sT, Tm[l].rearrange("g s x -> s g x")).then_inc(*s5_in["T"].inc(s))
                    sp.wait_ge(*s5_rot.at(s))
                    sp.dma_start(sV, VTm[l]).then_inc(*s5_in["V"].inc(s))
                elif s[0] == "s5" and part == "s":
                    n, l = s[1], s[1] // 2
                    odd = n % 2
                    nt = 8 + 4 * odd
                    Wn = HALF + TS * odd
                    sp.wait_ge(*scores.free.at(s + (1,)))
                    if odd:
                        sp.wait_ge(*aux.free.at(s + ("y",)))
                    for t in range(nt):
                        src = (Yall[16 * t:16 * t + 16, :].rearrange("p (g b) -> p g b", g=16) if t < 8
                               else Ys[16 * (t - 8):16 * (t - 7), :, :])
                        sp.dma_start(permuted(yd, t), src).then_inc(*s5_y.inc(s + (t,)))
                    sp.wait_ge(*s5_y.at(s + (nt - 1,)))
                    sp.dma_start(yT[:, :, 0:Wn], yd[:, 0:Wn].rearrange("(j p) w -> p j w", p=P)).then_inc(*s5_in["Y"].inc(s))
                    if odd:
                        for ri, nm in enumerate(("re", "im")):
                            sp.dma_start(out["p_s5_" + nm][l, 0].rearrange("(q a) p -> (a p) q", a=2), s5x[:, ri, :]).then_inc(*s5_out.inc(s + (ri, "p")))
                            for b in range(NB):
                                sp.dma_start(out["d_s5_" + nm][l, b].rearrange("(q a) p -> (a p) q", a=2), sXf[:, ri, :, b]).then_inc(*s5_out.inc(s + (ri, b)))
                elif s[0] == "norm":
                    n = s[1]
                    if part == 0:
                        if n >= 1:
                            sp.wait_ge(*rot_done.at(n - 1))
                        if n >= 2:
                            stored(n - 2)
                        if n:
                            norm_weights(n)
                            load_x((n, 0))
                            load_x((n, 1))
                    elif part + 1 in tiles_of(n):
                        load_x((n, part + 1))
                elif s[0] == "proj" and part == ("mm", pieces_of_block(*s[1:])[0]):
                    n = s[1]
                    load_until(w_loads.index(s[1:]) + 2)
                    if s[2] == "ml_ifg" and n % 2:
                        if n // 2:
                            sp.wait_ge(*pre_dve.at(("mlpre", n - 2, 0)))
                        sp.dma_start(m0[:, :], inp["state_mlstm_m"][n // 2].rearrange("b h -> h b")).then_inc(*m_in.inc(n // 2))
                    if s[2] == "rt_qk":
                        m = [m for m in hg_mixes if m[1] == n]
                        if m:
                            sp.wait_ge(*y_done.at(m[-1]))
                        else:
                            sp.wait_ge(*PB[bank_of[("norm", n, tiles_of(n)[-1], 1)]].full.at(("norm", n, tiles_of(n)[-1], 1)))
                        sp.dma_start(rtab, inp["c_rot"][n % 2].rearrange("p (k w) -> p k w", k=4)).then_inc(*tab_in.inc(n))
                elif s[0] == "mlpre" and part == "store" and s[1] % 2:
                    l = s[1] // 2
                    sp.wait_ge(*pre_dve.at(s + (0,)))
                    sp.dma_start(out["d_mlstm_m"][l].rearrange("b h -> h b"),
                                 rows[:, M_, HALF + DSEQ - 1:W:DSEQ]).then_inc(*m_out.inc((l, 0)))
                    sp.dma_start(out["p_mlstm_m"][l].rearrange("b h -> h b"), rows[:, M_, HALF - 1:HALF]).then_inc(*m_out.inc((l, 1)))
                elif s in samples and part in ("B0", "D"):
                    l = s[1] // 2
                    i = samples.index(s)
                    if i and part == "B0":
                        prev = samples[i - 1]
                        sp.wait_ge(*ss_out.at(prev + (ss_parts[prev[0]] - 1,)))

                    def moves():
                        if s[0] == "rt":
                            for h in range(4):
                                yield sst[32 * h:32 * h + 32, 0, :, 0:64], inp["state_ret"][l, :, h].rearrange("b k v -> k b v"), out["d_ret"][l, :, h].rearrange("b k v -> k b v")
                        else:
                            name, oname = ("state_hgrn", "d_hgrn") if s[0] == "hg" else ("state_mlstm_C", "d_mlstm_C")
                            for h in range(4):
                                v = sst[h % 2 * 64:h % 2 * 64 + 64, h // 2, :, 0:64]
                                yield v, inp[name][l, :, h].rearrange("b k v -> k b v"), out[oname][l, :, h].rearrange("b k v -> k b v")
                            if s[0] == "ml":
                                for h in range(4):
                                    v = sst[h % 2 * 64:h % 2 * 64 + 64, h // 2, :, 64:65]
                                    r = lambda a: a[l, :, h, :].rearrange("b (k o) -> k b o", o=1)
                                    yield v, r(inp["state_mlstm_n"]), r(out["d_mlstm_n"])
                    if part == "D":
                        sp.wait_ge(*ss_new.at(s))
                    for k, (view, src, dst) in enumerate(moves()):
                        if part == "B0":
                            sp.dma_start(view, src).then_inc(*ss_in.inc(s + (k,)))
                        else:
                            sp.dma_start(dst, view).then_inc(*ss_out.inc(s + (k,)))
                elif s in last_prompt and part == "D":
                    l = s[1] // 2
                    sp.wait_ge(*upd.free.at(s + ("U",)))
                    if s[0] == "hg":
                        for h in range(4):
                            sp.dma_start(out["p_hgrn"][l, 0, h], S_hg[h % 2 * 64:h % 2 * 64 + 64, h // 2, :]).then_inc(*ps_out.inc(s + (h,)))
                    elif s[0] == "rt":
                        sp.dma_start(out["p_ret"][l, 0].rearrange("h k v -> (h k) v"), S_rt[:, :]).then_inc(*ps_out.inc(s + (0,)))
                    else:
                        for h in range(4):
                            v = S_ml[h % 2 * 64:h % 2 * 64 + 64, h // 2, :]
                            sp.dma_start(out["p_mlstm_C"][l, 0, h], v[:, 0:64]).then_inc(*ps_out.inc(s + (2 * h,)))
                            sp.dma_start(out["p_mlstm_n"][l, 0, h].rearrange("(k o) -> k o", o=1), v[:, 64:65]).then_inc(*ps_out.inc(s + (2 * h + 1,)))
                elif s[0] == "out":
                    n = s[1]
                    ks = outs_of(n)
                    k, i = part, ks.index(part)
                    if k[2] == 0:
                        load_until(w_loads.index((n, "wo", k[1])) + 1)
                    slot, prev = oslot[k], before(out_pieces, k, 3)
                    if prev is not None:
                        sp.wait_ge(*xo_out[slot].at(prev))
                    c = slice(k[1] * 256, (k[1] + 1) * 256)
                    sp.dma_start(xo[0:chunk_len(k[2]), slot, :], x_src(n, k[2])[:, c]).then_inc(*xo_in[slot].inc(k))
                    for kk in ([ks[i - 2]] if i >= 2 else []) + (ks[-2:] if i == len(ks) - 1 else []):
                        sp.wait_ge(*xo_sum.at(kk))
                        sp.dma_start(x_rows(x1 if n < 2 else x2, n, kk[2])[:, kk[1] * 256:(kk[1] + 1) * 256],
                                     xo[0:chunk_len(kk[2]), oslot[kk], :]).then_inc(*xo_out[oslot[kk]].inc(kk))
                elif s[0] == "final":
                    k = ("final", part)
                    if part == 0:
                        stored(2 * DEPTH - 2)
                        norm_weights("final")
                    for b in range(4) if part >= NCH else ():
                        kk = (2 * DEPTH - 1, b, part - NCH)
                        sp.wait_ge(*xo_out[oslot[kk]].at(kk))
                    load_x(k)
                    for t in ([part - 1] if part else []) + ([part] if part == 2 * NCH else []):
                        kk = ("final", t)
                        sp.wait_ge(*h_done.at(kk))
                        dst = (out["y_sample"].rearrange("b s d -> (b s) d") if t == 2 * NCH
                               else out["y_prompt"][0, t * P:(t + 1) * P, :])
                        sp.dma_start(dst, xt[0:TS if t == 2 * NCH else P, tslot[kk], :]).then_inc(*y_out[tslot[kk]].inc(kk))
            for sgl in [*y_out, ss_out, ps_out, m_out, s5_out]:
                if sgl.fired:
                    sp.wait_ge(*sgl.at(sgl.keys[-1]))

        @block.gpsimd
        def _(pool):
            for v, x in ((epow[:, :], -0.5), (ST[:, :, :], 0.0), (STs[:, :, :], 0.0), (ssq[:, :], 0.0), (mixT[:, :, :], 0.0), (QE[:, :, :, :], 0.0)):
                nc.gpsimd.memset(v, x).then_inc(*pool_done.inc())
            pool.wait_ge(*pool_done.now())
            nc.gpsimd.memset(small[:, :], 0.0).then_inc(*pool_setup.inc("all"))

            blocks = list(in_blocks)

            def split_low():
                b = blocks.pop(0)
                prev = before(in_blocks, b, 2)
                if prev is not None:
                    pool.wait_ge(*PB[bank_of[last_piece[prev]]].full.at(last_piece[prev]))
                pool.wait_ge(*whi_done.at(b))
                width = BLOCK[b[1]][2]
                nc.gpsimd.tensor_tensor(wlo[:, hslot[b], :, 0:width], wraw[:, wslot[b], :, 0:width],
                                        whi[:, hslot[b], :, 0:width].bitcast(F32), ALU.subtract).then_inc(*wlo_done.inc(b))

            def power(k):
                s = tslot[k]
                pool.wait_ge(*ssq_done.at(k))
                nc.gpsimd.tensor_scalar(rstd[:, s:s + 1], ssq[:, s:s + 1], 1.0 / D, EPS, ALU.mult, ALU.add).then_inc(*pool_done.inc())
                pool.wait_ge(*pool_done.now())
                nc.gpsimd.tensor_tensor(rstd[:, s:s + 1], rstd[:, s:s + 1], epow[:, 0:1], ALU.pow).then_inc(*rstd_done.inc(k))

            for s, part in plan:
                if s[0] == "norm":
                    if part == 0:
                        power((s[1], 0))
                    if part + 1 in tiles_of(s[1]):
                        power((s[1], part + 1))
                if split_after(s, part):
                    split_low()
                if s[0] == "s5" and part == "u":
                    n = s[1]
                    if s == s5n[0]:
                        pool.wait_ge(*set_out.at(("s5set", 0, 10)))
                        pool.wait_ge(*set_zero.at(set_zero.keys[-1]))
                    k = last_piece[(n, "s5_x")]
                    pool.wait_ge(*PB[bank_of[k]].full.at(k))
                    mls = [m for m in mixes if m[0] == "ml" and m[1] == n]
                    if mls:
                        pool.wait_ge(*y_done.at(mls[-1]))
                        pool.wait_ge(*aux.full.at(mls[-1] + ("mixed",)))
                    nc.gpsimd.memset(U[0:64, :, 64:72], 0.0).then_inc(*s5_clear.inc(s))
                elif s in mixes and part == "C":
                    T = chunk_len(s[2])
                    pool.wait_ge(*mv_done.at(s))
                    nc.gpsimd.tensor_scalar(rs[0:T, :], mv[0:T, :, 1], EPS if s[0] == "rt" else 4 * EPS, 4.0,
                                            ALU.add, ALU.mult).then_inc(*pool_done.inc())
                    pool.wait_ge(*pool_done.now())
                    nc.gpsimd.tensor_tensor(rs[0:T, :], rs[0:T, :], epow[0:T, :], ALU.pow).then_inc(*rs_done.inc(s))
                elif s[0] == "final":
                    power(("final", part))

        @block.scalar
        def _(act):
            act.wait_ge(*pool_setup.at("all"))
            act.wait_ge(*const_in.at(4))
            blocks = list(in_blocks)

            def split_high():
                b = blocks.pop(0)
                prev = before(in_blocks, b, 2)
                if prev is not None:
                    act.wait_ge(*PB[bank_of[last_piece[prev]]].full.at(last_piece[prev]))
                act.wait_ge(*wr_in[wslot[b]].at(b))
                width = BLOCK[b[1]][2]
                nc.scalar.activation(whi[:, hslot[b], :, 0:width], wraw[:, wslot[b], :, 0:width], ACT.Copy).then_inc(*whi_done.inc(b))

            def square_sum(k):
                act.wait_ge(*xt_in[tslot[k]].at(k))
                prev = before(all_tiles, k, 2)
                if prev is not None:
                    act.wait_ge(*rstd_done.at(prev))
                r = P if k[1] != (NCH if k[0] != "final" else 2 * NCH) else TS
                if before(all_tiles, k):
                    act.wait_ge(*ssq_done.at(before(all_tiles, k)))
                nc.scalar.activation(th[0:r, :, :].rearrange("p a b -> p (a b)"), xt[0:r, tslot[k], :], ACT.Square,
                                     accum_out=ssq[0:r, tslot[k]:tslot[k] + 1]).then_inc(*ssq_done.inc(k))

            act.wait_ge(*lb_done.at("diff"))
            nc.scalar.activation(lb[:, 4:6], lb[:, 4:6], ACT.Exp).then_inc(*act_done.inc())
            act.wait_ge(*act_done.now())
            nc.scalar.activation(lb[:, 6:8], lb[:, 6:8], ACT.Exp).then_inc(*lb_exp.inc("in"))

            def take_piece(k):
                n, name = k[:2]
                bank = PB[bank_of[k]]
                ps, at, ln = piece_psum(k)
                kind = BLOCK[name][4]
                if kind == "v":
                    return
                if k == (n, "s5_x", 0, 0):
                    mls = [m for m in mixes if m[0] == "ml" and m[1] == n]
                    if n % 2 and mls:
                        act.wait_ge(*m_out.at((n // 2, 1)))
                    if not n:
                        act.wait_ge(*set_out.at(("s5set", 0, 10)))
                act.wait_ge(*bank.full.at(k))
                if kind == "av":
                    i = th_keys.index(k)
                    if i >= 2:
                        act.wait_ge(*PB[bank_of[th_keys[i - 2]]].free.at(th_keys[i - 2]))
                    v = th[:, i % 2, 0:ln]
                    if name == "ml_ifg":
                        if at == 0:
                            act.wait_ge(*ml_clear.at(n))
                        nc.scalar.activation(ifc[0:ln, at, :], ps[:, 0:8], ACT.Copy).then_inc(*act_done.inc())
                        ps = ps[:, 8:264]
                    if BLOCK[name][3] == "tok":
                        v = th[0:ln, i % 2, 0:256]
                    nc.scalar.activation(v, ps, ACT.Tanh, scale=0.5).then_inc(*th_done.inc(k))
                    return
                done = bank.free.inc(k)
                if name == "hg_f":
                    nc.scalar.activation(hf[:, k[2], at:at + ln], ps, ACT.Copy).then_inc(*done)
                elif name == "ml_q":
                    act.wait_ge(*ml_clear.at(n))
                    for par in range(2):
                        r = slice(par * 64, par * 64 + 64)
                        nc.scalar.activation(mq[r, 2 * k[2] + par, at:at + ln], ps[r, :], ACT.Copy).then_inc(
                            *(done if par else act_done.inc()))
                elif name == "ml_k":
                    nc.scalar.activation(mk[:, k[2], at:at + ln], ps, ACT.Copy, scale=0.125).then_inc(*done)
                elif name == "ml_v":
                    nc.scalar.activation(mvv[0:ln, at, :, 0:64], ps.rearrange("p (h v) -> p h v", h=4), ACT.Copy).then_inc(*done)
                elif name == "ml_o":
                    nc.scalar.activation(mo[0:ln, at, :], ps, ACT.Tanh, scale=0.5).then_inc(*done)
                elif name == "s5_x":
                    hi = min(at + ln, HALF)
                    parts_ = [(at, hi, 8, 0)] + [(HALF, W, DSEQ, HALF)] * (at + ln > HALF)
                    for a, e, tau, base in parts_:
                        size = HALF if base == 0 else TS
                        dst = ux[:, k[2], base:base + size].rearrange("p (t b) -> p t b", t=tau)[:, :, (a - base) // tau:(e - base) // tau]
                        nc.scalar.activation(dst, ps[:, a - at:e - at].rearrange("p (b t) -> p t b", t=tau), ACT.Copy).then_inc(
                            *(done if a == parts_[-1][0] else act_done.inc()))
                elif name in ("hg_i", "rt_v"):
                    nc.scalar.activation((hv if name == "hg_i" else rv)[0:ln, at, :], ps, ACT.Copy).then_inc(*done)

            for s, part in plan:
                if s[0] == "norm":
                    n, t = s[1], part
                    if t == 0:
                        if n:
                            ks = [k for k in th_keys if k[0] < n]
                            for k in ks[-2:]:
                                act.wait_ge(*PB[bank_of[k]].free.at(k))
                        square_sum((n, 0))
                    if t + 1 in tiles_of(n):
                        square_sum((n, t + 1))
                    r = chunk_len(t)
                    for g in range(2):
                        u = ("norm", n, t, g)
                        act.wait_ge(*PB[bank_of[u]].full.at(u))
                        nc.scalar.activation(hhi[:, 4 * g:4 * g + 4, t * P:t * P + r],
                                             PB[bank_of[u]].t.rearrange("p (k c) -> p k c", k=4)[:, :, 0:r],
                                             ACT.Copy).then_inc(*hhi_done.inc((n, t, g)))
                if split_after(s, part):
                    split_high()
                if s[0] == "proj" and part[0] == "take":
                    take_piece(part[1])
                elif s[0] == "s5set" and part == "c":
                    l = s[1]
                    if not l:
                        act.wait_ge(*vec_dve.at("phase"))
                        ph, sn, cs = (s5v[:, 14 + 2 * i:16 + 2 * i, :] for i in range(3))
                        nc.scalar.activation(sn, ph, ACT.Sin, scale=0.5).then_inc(*act_done.inc())
                        nc.scalar.activation(ph, ph, ACT.Abs).then_inc(*act_done.inc())
                        act.wait_ge(*act_done.now())
                        nc.scalar.activation(cs, ph, ACT.Sin, scale=-0.5, bias=C("halfpi")).then_inc(*vec_act.inc("sin"))
                    act.wait_ge(*aux.full.at(s + ("C",)))
                    for ri in range(2):
                        for f in range(2):
                            for a in range(2):
                                src = aux.t[64 * a:64 * a + 64, (2 * ri + f) * P:(2 * ri + f + 1) * P].rearrange("p (q a c) -> p q a c", q=4, a=2)[:, :, a, :]
                                fin = ri == f == a == 1
                                nc.scalar.activation(cCT[64 * a:64 * a + 64, ri, 4 * f:4 * f + 4, :], src, ACT.Copy).then_inc(
                                    *(aux.free.inc(s + ("C",)) if fin else act_done.inc()))
                elif s[0] == "s5set" and part == "w":
                    for ri in range(2):
                        act.wait_ge(*scores.full.at(s + (ri,)))
                        for b in range(2):
                            nc.scalar.activation(cWT[:, 4 * b:4 * b + 4, ri, :], scores.t[:, b, :].rearrange("p (q x) -> p q x", q=4), ACT.Copy).then_inc(
                                *(scores.free.inc(s + (ri,)) if b else act_done.inc()))
                    for r in range(2):
                        act.wait_ge(*scores.full.at(s + (2 + r,)))
                        for a in range(2):
                            dst = cK.rearrange("p (q a) x -> p q a x", a=2)[:, 4 * r:4 * r + 4, a, :]
                            nc.scalar.activation(dst, scores.t[0:16, a, :].rearrange("p (q x) -> p q x", q=4), ACT.Copy).then_inc(
                                *(scores.free.inc(s + (2 + r,)) if a else act_done.inc()))
                elif s[0] == "s5" and part == "y":
                    n = s[1]
                    odd = n % 2
                    k = s + (1,)
                    act.wait_ge(*scores.full.at(k))
                    if odd:
                        act.wait_ge(*aux.full.at(s + ("y",)))
                    Yv = Yall.rearrange("p (q a b) -> p q a b", q=8, a=2)
                    Ysv = Ys.rearrange("p (q a) b -> p q a b", a=2)
                    for a in range(2):
                        nc.scalar.activation(Yv[:, :, a, :], scores.t[:, a, :].rearrange("p (q b) -> p q b", q=8), ACT.Copy).then_inc(
                            *(scores.free.inc(k) if a else act_done.inc()))
                    if odd:
                        act.wait_ge(*upd.full.at(s + ("y",)))
                        nc.scalar.activation(Ysv[:, :, 0, :], upd.t[0:64, 0:8 * NB].rearrange("p (q b) -> p q b", q=8), ACT.Copy).then_inc(*upd.free.inc(s + ("y",)))
                        nc.scalar.activation(Ysv[:, :, 1, :], aux.t[0:64, 0:8 * NB].rearrange("p (q b) -> p q b", q=8), ACT.Copy).then_inc(*aux.free.inc(s + ("y",)))
                elif s[0] == "s5" and part == "g":
                    Wn = HALF + TS * (s[1] % 2)
                    act.wait_ge(*s5_dve.at(s + ("skip",)))
                    nc.scalar.activation(gt[:, :, 0:Wn], yT[:, :, 0:Wn], ACT.Square).then_inc(*s5_act.inc(s + ("sq",)))
                    act.wait_ge(*s5_dve.at(s + ("cube",)))
                    nc.scalar.activation(gt[:, :, 0:Wn], gt[:, :, 0:Wn], ACT.Tanh, scale=(2 / np.pi) ** 0.5).then_inc(*s5_act.inc(s + ("tanh",)))
                elif s[0] == "s5" and part == "z":
                    odd = s[1] % 2
                    k = s + (2,)
                    act.wait_ge(*scores.full.at(k))
                    for j in range(2):
                        nc.scalar.activation(gt[:, j, 0:HALF], scores.t[:, j, :], ACT.Tanh, scale=0.25).then_inc(
                            *(scores.free.inc(k) if j else act_done.inc()))
                    if odd:
                        k = s + ("glu",)
                        act.wait_ge(*upd.full.at(k))
                        nc.scalar.activation(gt[:, :, HALF:W], upd.t[:, 0:2 * TS].rearrange("p (j w) -> p j w", j=2), ACT.Tanh, scale=0.25).then_inc(*upd.free.inc(k))
                elif s[0] == "hgpre":
                    n, Wn = s[1], HALF + TS * (s[1] % 2)
                    act.wait_ge(*act_done.now())
                    f, u, cum, kk = hf[:, :, 0:Wn], hu[:, :, 0:Wn], hcum[:, :, 0:Wn], hk[:, :, 0:Wn]
                    lastf = last_piece[(n, "hg_f")]
                    act.wait_ge(*PB[bank_of[lastf]].free.at(lastf))
                    lf2 = [k for k in pieces if k[:2] == (n, "hg_f")]
                    for k in lf2:
                        act.wait_ge(*PB[bank_of[k]].free.at(k))
                    nc.scalar.activation(u, f, ACT.Abs).then_inc(*act_done.inc())
                    act.wait_ge(*act_done.now())
                    nc.scalar.activation(u, u, ACT.Exp, scale=-1.0).then_inc(*act_done.inc())
                    act.wait_ge(*act_done.now())
                    nc.scalar.activation(u, u, ACT.Ln, bias=1.0).then_inc(*pre_act.inc(s + (0,)))
                    act.wait_ge(*pre_dve.at(s + (0,)))
                    if n // 2:
                        nc.scalar.activation(u, cum, ACT.Exp).then_inc(*act_done.inc())
                    nc.scalar.activation(kk, f, ACT.Exp).then_inc(*pre_act.inc(s + (1,)))
                    if n // 2:
                        act.wait_ge(*pre_dve.at(s + (1,)))
                        nc.scalar.activation(cum, u, ACT.Ln).then_inc(*pre_act.inc(s + (2,)))
                elif s[0] == "mlpre" and part is None:
                    n, l = s[1], s[1] // 2
                    act.wait_ge(*scores.full.at(s + (0,)))
                    nc.scalar.activation(rows[:, G_, 0:HALF], scores.t[0:4, 0, :], ACT.Identity, bias=gb[:, l:l + 1]).then_inc(*act_done.inc())
                    nc.scalar.activation(rows[:, SP_, 0:HALF], scores.t[0:4, 1, :], ACT.Identity, bias=gb[:, 2 + l:3 + l]).then_inc(*scores.free.inc(s + (0,)))
                    act.wait_ge(*scores.free.at(s + (0,)))
                    Wn = HALF
                    if n % 2:
                        Wn = W
                        act.wait_ge(*upd.full.at(s + ("s",)))
                        nc.scalar.activation(rows[:, G_, HALF:W], upd.t[0:4, 0:TS], ACT.Identity, bias=gb[:, l:l + 1]).then_inc(*act_done.inc())
                        nc.scalar.activation(rows[:, SP_, HALF:W], upd.t[0:4, TS:2 * TS], ACT.Identity, bias=gb[:, 2 + l:3 + l]).then_inc(*upd.free.inc(s + ("s",)))
                        act.wait_ge(*upd.free.at(s + ("s",)))
                    act.wait_ge(*act_done.now())
                    m = rows[:, M_, 0:Wn]
                    nc.scalar.activation(m, rows[:, SP_, 0:Wn], ACT.Abs).then_inc(*act_done.inc())
                    act.wait_ge(*act_done.now())
                    nc.scalar.activation(m, m, ACT.Exp, scale=-1.0).then_inc(*act_done.inc())
                    act.wait_ge(*act_done.now())
                    nc.scalar.activation(m, m, ACT.Ln, bias=1.0).then_inc(*pre_act.inc(s + (0,)))
                elif s in mixes and part == "A0":
                    n, c = s[1:]
                    T = chunk_len(c)
                    act.wait_ge(*hg_diff.at(s))
                    for v in ([E[:, 0:8]] if c < NCH else [E[:, 0:2], E[:, 7:8]]):
                        v = v[:, :, :, 0:T]
                        for j in range(2):
                            nc.scalar.activation(v[:, :, j], v[:, :, j], ACT.Abs).then_inc(*act_done.inc())
                        act.wait_ge(*act_done.now())
                        for j in range(2):
                            nc.scalar.activation(v[:, :, j], v[:, :, j], ACT.Exp, scale=-1.0).then_inc(*act_done.inc())
                    nc.scalar.activation(E[:, 8, :, 0:T], hcum[:, :, cols(c)], ACT.Exp).then_inc(*hg_exp.inc(s))
                elif s in mixes and part == "B0":
                    br, n, c = s
                    T = chunk_len(c)
                    turn, tk = aux.t, s + ("turn",)
                    if before(mixes, s):
                        act.wait_ge(*y_done.at(before(mixes, s)))
                    act.wait_ge(*aux.full.at(tk))
                    if br == "ml":
                        nb = 1 if c < NCH else NB
                        g, sp_, em, wk, cs = (small[:, 4 * i:4 * i + 4] for i in range(5))
                        cs = small[:, 16:16 + 2 * nb]
                        nc.scalar.activation(small[0:T, 0:4], turn[0:T, 256:260], ACT.Copy).then_inc(*act_done.inc())
                        nc.scalar.activation(small[0:T, 4:8], turn[0:T, 260:264], ACT.Exp).then_inc(*act_done.inc())
                        nc.scalar.activation(small[0:T, 8:12], turn[0:T, 264:268], ACT.Exp, scale=-1.0).then_inc(*act_done.inc())
                        nc.scalar.activation(small[0:T, 12:16], turn[0:T, 268:272], ACT.Exp).then_inc(*act_done.inc())
                        nc.scalar.activation(cs, turn[:, 272:272 + 2 * nb], ACT.Exp).then_inc(*act_done.inc())
                        act.wait_ge(*act_done.now())
                        for h in range(4):
                            nc.scalar.activation(kT[0:T, h * 64:h * 64 + 64], turn[0:T, h * 64:h * 64 + 64], ACT.Copy,
                                                 scale=small[0:T, 12 + h:13 + h]).then_inc(*(aux.free.inc(tk) if h == 3 else act_done.inc()))
                        act.wait_ge(*ex_add.at(s))
                        for h in range(4):
                            v = ex[0:T, h * T:h * T + T]
                            nc.scalar.activation(v, v, ACT.Exp, bias=small[0:T, h:h + 1]).then_inc(*(ex_exp.inc(s) if h == 3 else act_done.inc()))
                    elif br == "hg":
                        nc.scalar.activation(small[0:T, 0:4], turn[0:T, 256:260], ACT.Copy).then_inc(*act_done.inc())
                        nc.scalar.activation(kT[0:T, :], turn[0:T, 0:256], ACT.Copy).then_inc(*aux.free.inc(tk))
                    else:
                        nc.scalar.activation(kT[0:T, 0:128], turn[0:T, 0:128], ACT.Copy).then_inc(*aux.free.inc(tk))
                elif s in mixes and part == "C":
                    br, n, c = s
                    if c == NCH:
                        act.wait_ge(*upd.full.at(s + ("inter",)))
                        r = 65 if br == "ml" else 64
                        nc.scalar.activation(oT[0:r, :, :], upd.t[0:r, 0:128].rearrange("p (h t) -> p h t", h=4), ACT.Copy).then_inc(*upd.free.inc(s + ("inter",)))
                elif s in mixes and part == "D":
                    br, n, c = s
                    T = chunk_len(c)
                    mk_ = s + ("mixed",)
                    act.wait_ge(*aux.full.at(mk_))
                    nc.scalar.activation(mixT[:, mix_tile[br]:mix_tile[br] + 2, cols(c)],
                                         aux.t[:, 0:256].rearrange("p (j t) -> p j t", j=2)[:, :, 0:T], ACT.Copy).then_inc(*aux.free.inc(mk_))
                elif s[0] == "final":
                    square_sum(("final", part))

        @block.vector
        def _(dve):
            keep_phase = []

            def settle():
                dve.wait_ge(*dve_done.now())

            dve.wait_ge(*const_in.at(4))
            mx = small[:, 32:34]
            dve.wait_ge(*pool_setup.at("all"))
            nc.vector.tensor_copy(cm[:, :], cm_wide).then_inc(*dve_done.inc())
            nc.vector.tensor_tensor(mx, lb[:, 0:2], lb[:, 2:4], ALU.max).then_inc(*dve_done.inc())
            settle()
            nc.vector.tensor_tensor(lb[:, 4:6], lb[:, 0:2], mx, ALU.subtract).then_inc(*dve_done.inc())
            nc.vector.tensor_tensor(lb[:, 6:8], lb[:, 2:4], mx, ALU.subtract).then_inc(*lb_done.inc("diff"))
            dve.wait_ge(*lb_exp.at("in"))
            nc.vector.tensor_tensor(mx, lb[:, 4:6], lb[:, 6:8], ALU.add).then_inc(*dve_done.inc())
            settle()
            nc.vector.reciprocal(mx, mx).then_inc(*dve_done.inc())
            settle()
            nc.vector.tensor_tensor(lb[:, 0:2], lb[:, 6:8], mx, ALU.mult).then_inc(*dve_done.inc())
            nc.vector.tensor_tensor(lb[:, 2:4], lb[:, 4:6], mx, ALU.mult).then_inc(*lb_done.inc("all"))
            dve.wait_ge(*lb_done.at("all"))

            def scale_rows(k):
                sl = tslot[k]
                r = P if k[1] != (NCH if k[0] != "final" else 2 * NCH) else TS
                dve.wait_ge(*rstd_done.at(k))
                nc.vector.scalar_tensor_tensor(xt[0:r, sl, :], xt[0:r, sl, :], rstd[0:r, sl:sl + 1], normw[0:r, :],
                                               ALU.mult, ALU.mult).then_inc(*h_done.inc(k))

            def q_side(c, j):
                for i, w in enumerate(levels(c)):
                    for par in range(2):
                        r = slice(par * 64, par * 64 + 64)
                        nc.vector.tensor_tensor(QE[r, i, par, 0:chunk_len(c) // 2].rearrange("p (n w) -> p n w", w=w),
                                                split(E[r, i, j, 0:chunk_len(c)], w)[:, :, 1], split(hq[r, j, cols(c)], w)[:, :, 1],
                                                ALU.mult).then_inc(*dve_done.inc())
                settle()

            def take_piece(k):
                n, name = k[:2]
                bank = PB[bank_of[k]]
                ps, at, ln = piece_psum(k)
                kind = BLOCK[name][4]
                if kind == "a":
                    return
                if kind == "av":
                    dve.wait_ge(*th_done.at(k))
                    i = th_keys.index(k) % 2
                    if name in ("hg_q", "s5_g"):
                        v, dst = th[:, i, 0:ln], (hq if name == "hg_q" else mixT)[:, k[2], at:at + ln]
                    else:
                        v, dst = th[0:ln, i, 0:256], gate_of[name[:2]][0:ln, at, :]
                    if name == "ml_ifg":
                        ps = ps[:, 8:264]
                    nc.vector.scalar_tensor_tensor(dst, v, 1.0, ps, ALU.add, ALU.mult).then_inc(*bank.free.inc(k))
                    return
                dve.wait_ge(*bank.full.at(k))
                dve.wait_ge(*tab_in.at(n))
                q = k[2] == 0
                a, b = rtmp[:, 0, 0:ln], rtmp[:, 1, 0:ln]
                if dve_done.n:
                    settle()
                nc.vector.stream_shuffle(a, ps, [(i + 16) % 32 for i in range(32)]).then_inc(*dve_done.inc())
                nc.vector.tensor_tensor(b, ps, rtab[:, 0 if q else 2, at:at + ln], ALU.mult).then_inc(*bank.free.inc(k))
                settle()
                nc.vector.tensor_tensor(a, a, rtab[:, 1 if q else 3, at:at + ln], ALU.mult).then_inc(*dve_done.inc())
                settle()
                dve.wait_ge(*bank.free.at(k))
                if q:
                    for h in range(4):
                        r = slice(32 * h, 32 * h + 32)
                        nc.vector.tensor_tensor(rq[r, h, at:at + ln], a[r, :], b[r, :], ALU.add).then_inc(*dve_done.inc())
                else:
                    nc.vector.tensor_tensor(rk[:, at:at + ln], a, b, ALU.add).then_inc(*dve_done.inc())
                if k == last_piece[k[:2]]:
                    settle()
                    nc.vector.memset(small[0:1, 63:64], 0.0).then_inc(*rot_done.inc(n))

            for s, part in plan:
                if s[0] == "norm":
                    n, t = s[1], part
                    if t == 0:
                        dve.wait_ge(*nw_in.at(n))
                        scale_rows((n, 0))
                    if t + 1 in tiles_of(n):
                        scale_rows((n, t + 1))
                    r = chunk_len(t)
                    for g in range(2):
                        u = ("norm", n, t, g)
                        bank = PB[bank_of[u]]
                        dve.wait_ge(*hhi_done.at((n, t, g)))
                        c = slice(t * P, t * P + r)
                        nc.vector.tensor_tensor(hlo[:, 4 * g:4 * g + 4, c], bank.t.rearrange("p (k c) -> p k c", k=4)[:, :, 0:r],
                                                hhi[:, 4 * g:4 * g + 4, c].bitcast(F32), ALU.subtract).then_inc(*bank.free.inc(u))
                elif s[0] == "proj" and part[0] == "mm":
                    n = s[1]
                    if part[1] == (n, "ml_ifg", 0):
                        if n:
                            dve.wait_ge(*y_done.at([m for m in mixes if m[1] < n and m[0] == "ml"][-1]))
                        if s5n and n < 2:
                            dve.wait_ge(*set_out.at(("s5set", n, 10)))
                        nc.vector.memset(mq, 0.0).then_inc(*dve_done.inc())
                        nc.vector.memset(mvv[:, :, :, 64:65], 1.0).then_inc(*ml_clear.inc(n))
                    if part[1] == (n, "rt_qk", 0, 0):
                        if n and n % 2 == 0:
                            dve.wait_ge(*ps_out.at([q for q in last_prompt if q[0] == "rt" and q[1] < n][-1] + (0,)))
                        if n % 2 == 0:
                            nc.vector.memset(S_rt[:, :], 0.0).then_inc(*dve_done.inc())
                        nc.vector.memset(rq, 0.0).then_inc(*dve_done.inc())
                        settle()
                elif s[0] == "proj":
                    take_piece(part[1])
                elif s[0] == "s5set" and part in ("c", "v"):
                    l = s[1]

                    def tt(o, a, b, op):
                        nc.vector.tensor_tensor(o, a, b, op).then_inc(*dve_done.inc())

                    def cmul(o, a, b, t, u, conj=False, neg=False):
                        tt(t, a[0], b[0], ALU.mult)
                        tt(u, a[1], b[1], ALU.mult)
                        settle()
                        tt(o[0], t, u, ALU.subtract)
                        settle()
                        tt(t, a[0], b[1], ALU.mult)
                        tt(u, a[1], b[0], ALU.mult)
                        settle()
                        if neg:
                            nc.vector.scalar_tensor_tensor(o[1], t, -1.0, u, ALU.mult, ALU.subtract).then_inc(*dve_done.inc())
                        else:
                            tt(o[1], t, u, ALU.add)
                        settle()

                    LR, LI, DT, T2, T3, UR, UI, DEN, FR, FI, RR = (s5v[:, i, :] for i in range(11))
                    XX, PH2, SN2, CS2, E2, Q2, Z2 = (s5v[:, 12 + 2 * i:14 + 2 * i, :] for i in range(7))

                    def ts(o, a, x, y, op0, op1=None):
                        (nc.vector.tensor_scalar(o, a, x, y, op0, op1) if op1 is not None else nc.vector.tensor_scalar(o, a, x, None, op0)).then_inc(*dve_done.inc())
                        settle()

                    if not l and part == "c":
                        dve.wait_ge(*vec_in.at(8))
                        ts(T2, DT, 1 / np.log(2), 12582912.0, ALU.mult, ALU.add)
                        ts(T2, T2, -12582912.0, -126.0, ALU.add, ALU.max)
                        ts(T2, T2, 127.0, None, ALU.min)
                        for piece in (0.693359375, np.log(2) - 0.693359375):
                            nc.vector.scalar_tensor_tensor(DT, T2, -piece, DT, ALU.mult, ALU.add).then_inc(*dve_done.inc())
                            settle()
                        ts(T3, DT, 1 / 7, 1.0, ALU.mult, ALU.add)
                        for k in (6, 5, 4, 3, 2, 1):
                            nc.vector.scalar_tensor_tensor(T3, T3, 1 / k, DT, ALU.mult, ALU.mult).then_inc(*dve_done.inc())
                            settle()
                            ts(T3, T3, 1.0, None, ALU.add)
                        ts(s5i[:, :], T2, 127.0, float(1 << 23), ALU.add, ALU.mult)
                        tt(DT, T3, s5i[:, :].bitcast(F32), ALU.mult)
                        settle()
                        tt(XX[:, 0], LR, DT, ALU.mult)
                        tt(PH2[:, 0], LI, DT, ALU.mult)
                        settle()

                        def less_turns(ph):
                            ts(T2, ph, 1 / (2 * np.pi), 12582912.0, ALU.mult, ALU.add)
                            ts(T2, T2, -12582912.0, None, ALU.add)
                            for piece in (6.28125, 2 * np.pi - 6.28125):
                                nc.vector.scalar_tensor_tensor(ph, T2, -piece, ph, ALU.mult, ALU.add).then_inc(*dve_done.inc())
                                settle()

                        less_turns(PH2[:, 0])
                        ts(PH2[:, 1], PH2[:, 0], 8.0, None, ALU.mult)
                        less_turns(PH2[:, 1])
                        ts(XX[:, 1], XX[:, 0], 8.0, None, ALU.mult)
                        nc.vector.memset(small[0:1, 57:58], 0.0).then_inc(*vec_dve.inc("phase"))
                        ts(XX, XX, 1 / 128, None, ALU.mult)
                        ts(E2, XX, 1 / 5, 1.0, ALU.mult, ALU.add)
                        for k in (4, 3, 2):
                            nc.vector.scalar_tensor_tensor(E2, E2, 1 / k, XX, ALU.mult, ALU.mult).then_inc(*dve_done.inc())
                            settle()
                            ts(E2, E2, 1.0, None, ALU.add)
                        tt(E2, E2, XX, ALU.mult)
                        settle()
                        for _ in range(7):
                            nc.vector.scalar_tensor_tensor(XX, E2, 2.0, E2, ALU.add, ALU.mult).then_inc(*dve_done.inc())
                            settle()
                            E2, XX = XX, E2
                        dve.wait_ge(*vec_act.at("sin"))
                        nc.vector.scalar_tensor_tensor(Q2, SN2, -2.0, SN2, ALU.mult, ALU.mult).then_inc(*dve_done.inc())
                        nc.vector.scalar_tensor_tensor(Z2, SN2, 2.0, CS2, ALU.mult, ALU.mult).then_inc(*dve_done.inc())
                        settle()
                        ts(PH2, Q2, 1.0, None, ALU.add)
                        nc.vector.scalar_tensor_tensor(UI, E2[:, 0], 1.0, Z2[:, 0], ALU.add, ALU.mult).then_inc(*dve_done.inc())
                        tt(UR, E2[:, 0], PH2[:, 0], ALU.mult)
                        settle()
                        tt(UR, UR, Q2[:, 0], ALU.add)
                        settle()
                        tt(T2, LR, LR, ALU.mult)
                        settle()
                        tt(T3, LI, LI, ALU.mult)
                        settle()
                        tt(DEN, T2, T3, ALU.add)
                        settle()
                        nc.vector.reciprocal(DEN, DEN).then_inc(*dve_done.inc())
                        tt(T2, UR, LR, ALU.mult)
                        settle()
                        tt(T3, UI, LI, ALU.mult)
                        settle()
                        tt(FR, T2, T3, ALU.add)
                        settle()
                        tt(T2, UI, LR, ALU.mult)
                        settle()
                        tt(T3, UR, LI, ALU.mult)
                        settle()
                        tt(FI, T2, T3, ALU.subtract)
                        settle()
                        tt(FR, FR, DEN, ALU.mult)
                        settle()
                        tt(FI, FI, DEN, ALU.mult)
                        settle()
                        ts(RR, E2[:, 1], 1.0, None, ALU.add)
                        s5_phase = (PH2[:, 1], Z2[:, 1])
                        pw = lambda i, lo, hi: s5p[:, i, :, lo:hi]
                        nc.vector.memset(s5p[:, 0, :, 0], 1.0).then_inc(*dve_done.inc())
                        nc.vector.memset(s5p[:, 1, :, 0], 0.0).then_inc(*dve_done.inc())
                        ts(s5p[:, 0, :, 1], UR, 1.0, None, ALU.add)
                        nc.vector.tensor_copy(s5p[:, 1, :, 1], UI).then_inc(*dve_done.inc())
                        settle()
                        for k in (1, 2, 4):
                            t, u = (x[:, 0:16 * k].rearrange("p (s k) -> p s k", k=k) for x in ct)
                            cmul((pw(0, k + 1, 2 * k + 1), pw(1, k + 1, 2 * k + 1)), (pw(0, 1, k + 1), pw(1, 1, k + 1)),
                                 tuple(pw(i, k, k + 1).broadcast_to([P, 16, k]) for i in range(2)), t, u)
                        for ll in range(DEPTH):
                            for i in range(2):
                                nc.vector.tensor_copy(s5c[:, ll, i, :], s5p[:, i, 8 * ll:8 * ll + 8, 4]).then_inc(*dve_done.inc())
                            nc.vector.tensor_copy(s5c[:, ll, 2, :], RR[:, 8 * ll:8 * ll + 8]).then_inc(*dve_done.inc())
                        settle()
                        keep_phase[:] = [s5_phase, (FR, FI)]
                    (zr, zi), (fr, fi) = keep_phase
                    ly = slice(8 * l, 8 * l + 8)
                    if part == "c":
                        nc.vector.tensor_copy(cE[:, 0, :, 0], zr[:, ly]).then_inc(*dve_done.inc())
                        nc.vector.tensor_scalar(cE[:, 1, :, 0], zi[:, ly], -1.0, None, ALU.mult).then_inc(*dve_done.inc())
                        settle()
                        for k in (1, 2, 4, 8, 16, 32):
                            t, u = (x[:, 0:8 * k].rearrange("p (s k) -> p s k", k=k) for x in ct)
                            cmul((cE[:, 0, :, k:2 * k], cE[:, 1, :, k:2 * k]), (cE[:, 0, :, 0:k], cE[:, 1, :, 0:k]),
                                 tuple(cE[:, i, :, k - 1:k].broadcast_to([P, 8, k]) for i in range(2)), t, u)
                        t, u = (x[:, 0:512].rearrange("p (s k) -> p s k", k=64) for x in ct)
                        tt(t, cE[:, 0], cE[:, 0], ALU.mult)
                        tt(u, cE[:, 1], cE[:, 1], ALU.mult)
                        settle()
                        tt(t, t, u, ALU.add)
                        settle()
                        ts(t, t, -0.5, 1.5, ALU.mult, ALU.add)
                        tt(cE[:, 0], cE[:, 0], t, ALU.mult)
                        tt(cE[:, 1], cE[:, 1], t, ALU.mult)
                        settle()
                        nc.vector.memset(small[0:1, 57:58], 0.0).then_inc(*set_dve.inc(s + ("E",)))
                    elif part == "v":
                        dve.wait_ge(*set_in.at(s + (5,)))
                        t, u = (x[:, 0:128].rearrange("p (q c) -> p q c", c=16) for x in ct)
                        o1 = lambda v, w: v.rearrange("p (q o) -> p q o", o=1).broadcast_to([P, 8, w])
                        cmul((cBb[:, 0], cBb[:, 1]), (o1(fr[:, ly], 16), o1(fi[:, ly], 16)), (cB[:, 0], cB[:, 1]), t, u)
                        dve.wait_ge(*aux.free.at(s + ("C",)))
                        pj = lambda i, lo, hi: s5p[:, i, ly, lo:hi].rearrange("p q (j o) -> p q j o", o=1).broadcast_to([P, 8, hi - lo, 16])
                        cc_ = lambda v, k: v.rearrange("p q (o c) -> p q o c", o=1).broadcast_to([P, 8, k, 16])
                        t, u = (x[:, :].rearrange("p (q j c) -> p q j c", j=9, c=16) for x in ct)
                        cmul((cV[:, 0], cV[:, 1]), (pj(0, 0, 9), pj(1, 0, 9)), (cc_(cCT[:, 0], 9), cc_(cCT[:, 1], 9)), t, u, neg=True)
                        nc.vector.memset(small[0:1, 57:58], 0.0).then_inc(*set_dve.inc(s + ("V",)))
                        for s_ in range(8):
                            t, u = (x[:, 128 * s_:128 * s_ + 128].rearrange("p (q c) -> p q c", c=16) for x in ct)
                            pj1 = lambda i: s5p[:, i, ly, 7 - s_:8 - s_].broadcast_to([P, 8, 16])
                            cmul((cW[:, 0, :, s_, :], cW[:, 1, :, s_, :]), (pj1(0), pj1(1)), (cBb[:, 0], cBb[:, 1]), t, u)
                        nc.vector.memset(small[0:1, 57:58], 0.0).then_inc(*set_dve.inc(s + ("W",)))
                elif s[0] == "s5" and part == "w":
                    n, l = s[1], s[1] // 2
                    odd = n % 2

                    def tt(o, a, b, op, inc=None):
                        nc.vector.tensor_tensor(o, a, b, op).then_inc(*(inc or dve_done.inc()))

                    if not odd:
                        if n:
                            dve.wait_ge(*s5_out.at(("s5", n - 1, 1, NB - 1)))
                        nc.vector.memset(s5x[:, :, :], 0.0).then_inc(*dve_done.inc())
                    wr, wi = (scores.t[:, i, :].rearrange("p (q b) -> p q b", q=8) for i in range(2))
                    Er, Ei = sE[:, 0], sE[:, 1]
                    t, u = stmp
                    dve.wait_ge(*s5_in["E"].at(s))
                    dve.wait_ge(*scores.full.at(s + (0,)))
                    tt(t, Er, wr, ALU.mult)
                    tt(u, Ei, wi, ALU.mult)
                    settle()
                    tt(sG[:, 0], t, u, ALU.subtract)
                    settle()
                    tt(t, Er, wi, ALU.mult)
                    tt(u, Ei, wr, ALU.mult, scores.free.inc(s + (0,)))
                    settle()
                    dve.wait_ge(*scores.free.at(s + (0,)))
                    tt(sG[:, 1], t, u, ALU.add)
                    settle()
                    for i in range(2):
                        for q in range(8):
                            nc.vector.tensor_tensor_scan(sG[:, i, q, :], s5c[:, l, 2, q:q + 1].broadcast_to([P, 64]), sG[:, i, q, :],
                                                         s5x[:, i, q:q + 1], ALU.mult, ALU.add).then_inc(*dve_done.inc())
                    nc.vector.tensor_copy(sX[:, :, :, 0], s5x[:, :, :]).then_inc(*dve_done.inc())
                    settle()
                    tt(t, Er, sG[:, 0], ALU.mult)
                    tt(u, Ei, sG[:, 1], ALU.mult)
                    settle()
                    tt(sX[:, 0, :, 1:65], t, u, ALU.add)
                    settle()
                    tt(t, Er, sG[:, 1], ALU.mult)
                    tt(u, Ei, sG[:, 0], ALU.mult)
                    settle()
                    tt(sX[:, 1, :, 1:65], t, u, ALU.subtract)
                    settle()
                    nc.vector.tensor_copy(s5x[:, :, :], sX[:, :, :, 64]).then_inc(*dve_done.inc())
                    if odd:
                        dve.wait_ge(*s5_xi.at(s + (1, NB - 1)))
                        dve.wait_ge(*upd.full.at(s + ("w",)))
                        A = [s5c[:, l, i, :].rearrange("p (q o) -> p q o", o=1).broadcast_to([P, 8, NB]) for i in range(2)]
                        t8, u8 = (x[:, :, 0:NB] for x in stmp)
                        ws = upd.t[:, 0:16 * NB].rearrange("p (r q b) -> p r q b", r=2, q=8)
                        for i, op in ((0, ALU.subtract), (1, ALU.add)):
                            settle()
                            tt(t8, A[0], sX0[:, i], ALU.mult)
                            tt(u8, A[1], sX0[:, 1 - i], ALU.mult)
                            settle()
                            tt(sXf[:, i], t8, u8, op)
                        settle()
                        tt(sXf, sXf, ws, ALU.add, upd.free.inc(s + ("w",)))
                        dve.wait_ge(*upd.free.at(s + ("w",)))
                    settle()
                    nc.vector.memset(small[0:1, 57:58], 0.0).then_inc(*s5_rot.inc(s))
                elif s[0] == "s5" and part == "g":
                    n, l = s[1], s[1] // 2
                    Wn = HALF + TS * (n % 2)
                    dve.wait_ge(*s5_in["Y"].at(s))
                    for j in range(2):
                        nc.vector.scalar_tensor_tensor(yT[:, j, 0:Wn], ux[:, j, 0:Wn], s5d[:, l, j:j + 1], yT[:, j, 0:Wn], ALU.mult, ALU.add).then_inc(
                            *(s5_dve.inc(s + ("skip",)) if j else dve_done.inc()))
                    dve.wait_ge(*s5_act.at(s + ("sq",)))
                    g, yy = gt[:, :, 0:Wn], yT[:, :, 0:Wn]
                    nc.vector.tensor_scalar(g, g, 0.044715, 1.0, ALU.mult, ALU.add).then_inc(*dve_done.inc())
                    settle()
                    dve.wait_ge(*s5_dve.at(s + ("skip",)))
                    nc.vector.tensor_tensor(g, g, yy, ALU.mult).then_inc(*s5_dve.inc(s + ("cube",)))
                    dve.wait_ge(*s5_act.at(s + ("tanh",)))
                    for j in range(2):
                        nc.vector.scalar_tensor_tensor(yg[:, j, 0:Wn], gt[:, j, 0:Wn], 1.0, yT[:, j, 0:Wn], ALU.add, ALU.mult).then_inc(
                            *(s5_dve.inc(s + ("gelu",)) if j else dve_done.inc()))
                elif s[0] == "s5" and part == "z":
                    odd = s[1] % 2
                    Wn = HALF + TS * odd
                    dve.wait_ge(*scores.free.at(s + (2,)))
                    if odd:
                        dve.wait_ge(*upd.free.at(s + ("glu",)))
                    settle()
                    for j in range(2):
                        nc.vector.scalar_tensor_tensor(yT[:, j, 0:Wn], gt[:, j, 0:Wn], 1.0, yg[:, j, 0:Wn], ALU.add, ALU.mult).then_inc(*dve_done.inc())
                    settle()
                    for lo, hi, tau in ((0, HALF, 8), (HALF, W, DSEQ))[:1 + odd]:
                        for j in range(2):
                            m = mixT[:, j, lo:hi].rearrange("p (b t) -> p t b", t=tau)
                            nc.vector.scalar_tensor_tensor(m, yT[:, j, lo:hi].rearrange("p (t b) -> p t b", t=tau), 0.125, m, ALU.mult, ALU.mult).then_inc(*dve_done.inc())
                    settle()
                    nc.vector.memset(small[0:1, 57:58], 0.0).then_inc(*s5_dve.inc(s + ("mixed",)))
                elif s[0] == "hgpre":
                    n, Wn = s[1], HALF + TS * (s[1] % 2)
                    f, u, cum, kk = hf[:, :, 0:Wn], hu[:, :, 0:Wn], hcum[:, :, 0:Wn], hk[:, :, 0:Wn]
                    dve.wait_ge(*pre_act.at(s + (0,)))
                    for j in range(2):
                        nc.vector.scalar_tensor_tensor(cum[:, j], f[:, j], 0.0, u[:, j], ALU.min, ALU.subtract).then_inc(*dve_done.inc())
                    settle()
                    nc.vector.tensor_tensor(f, cum, f, ALU.subtract).then_inc(*pre_dve.inc(s + (0,)))
                    dve.wait_ge(*pre_act.at(s + (1,)))
                    if n // 2:
                        for j in range(2):
                            nc.vector.tensor_scalar(u[:, j], u[:, j], lb[:, 2 + j:3 + j], lb[:, j:j + 1], ALU.mult, ALU.add).then_inc(*dve_done.inc())
                            nc.vector.tensor_scalar(kk[:, j], kk[:, j], lb[:, 2 + j:3 + j], None, ALU.mult).then_inc(*dve_done.inc())
                        settle()
                        nc.vector.tensor_scalar(u, u, 2.0 ** -60, None, ALU.max).then_inc(*pre_dve.inc(s + (1,)))
                        dve.wait_ge(*pre_act.at(s + (2,)))
                    for j in range(2):
                        nc.vector.tensor_tensor_scan(cum[:, j], C("reset")[:, 0:Wn], cum[:, j], 0.0, ALU.mult, ALU.add).then_inc(*dve_done.inc())
                    settle()
                    if n % 2 == 0:
                        if n:
                            dve.wait_ge(*ps_out.at([m for m in last_prompt if m[0] == "hg" and m[1] < n][-1] + (3,)))
                        nc.vector.memset(S_hg[:, :, :], 0.0).then_inc(*state_zero.inc((n // 2, "hg")))
                        dve.wait_ge(*state_zero.at((n // 2, "hg")))
                elif s[0] == "mlpre" and part is None:
                    n, l = s[1], s[1] // 2
                    Wn = W if n % 2 else HALF
                    dve.wait_ge(*pre_act.at(s + (0,)))
                    lf, cum, m, g, a = (rows[:, i, 0:Wn] for i in (SP_, WK_, M_, G_, A_))
                    nc.vector.scalar_tensor_tensor(lf, lf, 0.0, m, ALU.min, ALU.subtract).then_inc(*dve_done.inc())
                    if n % 2 == 0:
                        if n:
                            dve.wait_ge(*ps_out.at([q for q in last_prompt if q[0] == "ml" and q[1] < n][-1] + (7,)))
                            dve.wait_ge(*m_out.at((l - 1, 1)))
                        nc.vector.memset(S_ml[:, :, :], 0.0).then_inc(*dve_done.inc())
                        nc.vector.memset(gb[:, 4:5], 0.0).then_inc(*dve_done.inc())
                    settle()
                    nc.vector.tensor_copy(a, g).then_inc(*dve_done.inc())
                    nc.vector.tensor_tensor_scan(cum, C("reset")[0:4, 0:Wn], lf, 0.0, ALU.mult, ALU.add).then_inc(*dve_done.inc())
                    settle()
                    first = slice(HALF, W, DSEQ)
                    if n % 2:
                        dve.wait_ge(*m_in.at(l))
                        nc.vector.tensor_tensor(rows[:, M_, 0:NB], rows[:, SP_, first], m0[:, :], ALU.add).then_inc(*dve_done.inc())
                        settle()
                        nc.vector.tensor_tensor(rows[:, A_, first], rows[:, M_, 0:NB], rows[:, G_, first], ALU.max).then_inc(*dve_done.inc())
                        nc.vector.memset(rows[:, SP_, first], -1e30).then_inc(*dve_done.inc())
                        settle()
                    nc.vector.tensor_copy(mp[:, 0:1], gb[:, 4:5]).then_inc(*dve_done.inc())
                    nc.vector.tensor_tensor_scan(m, lf, a, gb[:, 4:5], ALU.add, ALU.max).then_inc(*dve_done.inc())
                    settle()
                    nc.vector.tensor_tensor(g, g, cum, ALU.subtract).then_inc(*dve_done.inc())
                    nc.vector.tensor_tensor(a, cum, m, ALU.subtract).then_inc(*dve_done.inc())
                    nc.vector.tensor_copy(mp[:, 1:NCH], rows[:, M_, CH - 1:HALF - 1:CH]).then_inc(*dve_done.inc())
                    nc.vector.tensor_copy(gb[:, 4:5], rows[:, M_, HALF - 1:HALF]).then_inc(*dve_done.inc())
                    settle()

                    def per_chunk(slot, lo, hi, w):
                        return rows[:, slot, lo:hi].rearrange("p (c w) -> p c w", w=w)

                    for lo, hi, w, prev in ((0, HALF, CH, mp), (HALF, W, DSEQ, m0))[:1 + n % 2]:
                        k = (hi - lo) // w
                        nc.vector.tensor_tensor(per_chunk(SP_, lo, hi, w), per_chunk(A_, lo, hi, w),
                                                prev[:, :].rearrange("p (c o) -> p c o", o=1).broadcast_to([4, k, w]), ALU.add).then_inc(*dve_done.inc())
                        nc.vector.tensor_tensor(per_chunk(WK_, lo, hi, w), per_chunk(G_, lo, hi, w),
                                                per_chunk(A_, lo, hi, w)[:, :, w - 1:w].broadcast_to([4, k, w]), ALU.add).then_inc(*dve_done.inc())
                    settle()
                    nc.vector.memset(small[0:4, 62:63], 0.0).then_inc(*pre_dve.inc(s + (0,)))
                elif s in mixes and part == "A0":
                    n, c = s[1:]
                    T, cc = chunk_len(c), cols(c)
                    if c:
                        dve.wait_ge(*scores.full.at(("hg", n, c - 1, 1)))
                    for i, w in [*enumerate(levels(c)), (7, None)]:
                        blk, at = (2 * w, w) if w else ((CH if c < NCH else DSEQ),) * 2
                        x, e = (v.rearrange("p j (n w) -> p j n w", w=blk) for v in (hcum[:, :, cc], E[:, i, :, 0:T]))
                        nc.vector.tensor_tensor(e, x, x[:, :, :, at - 1:at].broadcast_to([P, 2, T // blk, blk]), ALU.subtract).then_inc(
                            *(dve_done.inc() if w else hg_diff.inc(s)))
                    nc.vector.tensor_tensor(E[:, 9, :, 0:T], hq[:, :, cc], hk[:, :, cc], ALU.mult).then_inc(*dve_done.inc())
                elif s in mixes and part == "A1":
                    n, c = s[1:]
                    T, cc = chunk_len(c), cols(c)
                    nb, L = (1, CH) if c < NCH else (NB, DSEQ)
                    prev = before(mixes, s)
                    if prev:
                        dve.wait_ge(*outb.full.at(prev))
                    if c in (0, NCH):
                        nc.vector.memset(QD, 0.0).then_inc(*dve_done.inc())
                    settle()
                    dve.wait_ge(*hg_exp.at(s))
                    nc.vector.tensor_copy(hdec[:, :, 0:nb], E[:, 8, :, L - 1:T:L]).then_inc(*dve_done.inc())
                    for i, w in enumerate(levels(c)):
                        ks = [v.rearrange("p j (n g w) -> p j n g w", g=2, w=w)[:, :, :, 0] for v in (E[:, i, :, 0:T], hk[:, :, cc])]
                        nc.vector.tensor_tensor(ks[0], ks[0], ks[1], ALU.mult).then_inc(*dve_done.inc())
                    nc.vector.tensor_tensor(E[:, 7, :, 0:T], E[:, 7, :, 0:T], hk[:, :, cc], ALU.mult).then_inc(*dve_done.inc())
                    for par in range(2):
                        r = slice(par * 64, par * 64 + 64)
                        nc.vector.tensor_tensor(QD[r, :, par, 0:T], E[r, 8, :, 0:T], hq[r, :, cc], ALU.mult).then_inc(*dve_done.inc())
                    q_side(c, 0)
                    nc.vector.memset(small[0:1, 61:62], 0.0).then_inc(*hg_prod.inc(s + (0,)))
                elif s in mixes and part in ("B0", "B1"):
                    br, n, c = s
                    T = chunk_len(c)
                    prev = before(mixes, s)
                    stt = ST if c < NCH else STs
                    if prev:
                        dve.wait_ge(*outb.full.at(prev))
                    if br == "hg":
                        j = 0 if part == "B0" else 1
                        dve.wait_ge(*scores.full.at(s + (j,)))
                        if j == 0:
                            q_side(c, 1)
                            nc.vector.memset(small[0:1, 61:62], 0.0).then_inc(*hg_prod.inc(s + (1,)))
                        ls = levels(c)
                        u = T // 2
                        base = 0 if c < NCH else NL * 64
                        for i, w in enumerate(ls):
                            if i:
                                settle()
                            o = stt[0:T, 2 * j:2 * j + 2, 0:T].rearrange("p h (n g w) -> p h n g w", g=2, w=w)[:, :, :, 1]
                            mask = cm[0:T, base + i * u:base + (i + 1) * u].rearrange("p (o n w) -> p o n w", o=1, w=w).broadcast_to([T, 2, u // w, w])
                            dat = scores.t[0:T, i // 4, i % 4 * 2 * u:(i % 4 + 1) * 2 * u].rearrange("p (h n w) -> p h n w", h=2, w=w)
                            nc.vector.copy_predicated(o, mask, dat).then_inc(
                                *(scores.free.inc(s + (j,)) if i == len(ls) - 1 else dve_done.inc()))
                        dve.wait_ge(*scores.free.at(s + (j,)))
                        if j:
                            dve.wait_ge(*aux.free.at(s + ("turn",)))
                            settle()
                            nc.vector.copy_predicated(stt[0:T, :, 0:T], cm[0:T, NL * 64 + 32:NL * 64 + 32 + T].rearrange("p (o t) -> p o t", o=1).broadcast_to([T, 4, T]),
                                                      small[0:T, 0:4].rearrange("p (h o) -> p h o", o=1).broadcast_to([T, 4, T])).then_inc(*st_done.inc(s))
                    elif br == "rt":
                        dve.wait_ge(*scores.full.at(s + (0,)))
                        mask = (C("causal") if c < NCH else C("causal_s")).rearrange("p (o t) -> p o t", o=1).broadcast_to([T, 4, T])
                        nc.vector.tensor_tensor(stt[0:T, :, 0:T], scores.t[0:T, 0, 0:4 * T].rearrange("p (h t) -> p h t", h=4), mask,
                                                ALU.mult).then_inc(*scores.free.inc(s + (0,)))
                        dve.wait_ge(*scores.free.at(s + (0,)))
                        nc.vector.memset(small[0:1, 60:61], 0.0).then_inc(*st_done.inc(s))
                    else:
                        dve.wait_ge(*scores.full.at(s + (0,)))
                        mask = (C("cneg") if c < NCH else C("cneg_s")).rearrange("p (o t) -> p o t", o=1).broadcast_to([T, 4, T])
                        e4 = ex[0:T, 0:4 * T].rearrange("p (h t) -> p h t", h=4)
                        nc.vector.tensor_tensor(e4, scores.t[0:T, 1, 0:4 * T].rearrange("p (h t) -> p h t", h=4), mask, ALU.add).then_inc(*ex_add.inc(s))
                        dve.wait_ge(*ex_exp.at(s))
                        nc.vector.tensor_tensor(stt[0:T, :, 0:T], e4, scores.t[0:T, 0, 0:4 * T].rearrange("p (h t) -> p h t", h=4),
                                                ALU.mult).then_inc(*scores.free.inc(s + (0,)))
                        dve.wait_ge(*scores.free.at(s + (0,)))
                        nc.vector.memset(small[0:1, 60:61], 0.0).then_inc(*st_done.inc(s))

                elif s in mixes and part == "C":
                    br, n, c = s
                    T, cc = chunk_len(c), cols(c)
                    nb = 1 if c < NCH else NB
                    prev = before(mixes, s)
                    stt = ST if c < NCH else STs
                    dv = 65 if br == "ml" else 64
                    v_all = {"hg": hv, "rt": rv}.get(br)
                    dve.wait_ge(*outb.full.at(s))
                    if prev:
                        dve.wait_ge(*aux.full.at(prev + ("mixed",)))
                    yf = y[0:T, :, :]
                    gate = gate_of[br][0:T, c, :].rearrange("p (h v) -> p h v", h=4)
                    if br == "ml":
                        num = ex[0:T, 0:260].rearrange("p (h v) -> p h v", h=4)
                        dve.wait_ge(*scores.full.at(s + (1,)))
                        dve.wait_ge(*aux.free.at(s + ("turn",)))
                        nc.vector.tensor_tensor(num, scores.t[0:T, 0, 0:260].rearrange("p (h v) -> p h v", h=4),
                                                small[0:T, 4:8].rearrange("p (h o) -> p h o", o=1).broadcast_to([T, 4, 65]), ALU.mult).then_inc(*scores.free.inc(s + (1,)))
                        dve.wait_ge(*scores.free.at(s + (1,)))
                        nc.vector.tensor_tensor(num, num, outb.t[0:T, 0:260].rearrange("p (h v) -> p h v", h=4), ALU.add).then_inc(*outb.free.inc(s))
                        dve.wait_ge(*outb.free.at(s))
                        den = small[0:T, 32:36]
                        nc.vector.scalar_tensor_tensor(den, ex[0:T, 64:260:65], -1.0, ex[0:T, 64:260:65], ALU.mult, ALU.max).then_inc(*dve_done.inc())
                        nc.vector.scalar_tensor_tensor(yf.rearrange("p h v -> p (h v)").rearrange("p (h v) -> p h v", h=4), mo[0:T, c, :].rearrange("p (h v) -> p h v", h=4), 1.0, num[:, :, 0:64], ALU.add, ALU.mult).then_inc(*dve_done.inc())
                        settle()
                        nc.vector.tensor_tensor(den, den, small[0:T, 8:12], ALU.max).then_inc(*dve_done.inc())
                        settle()
                        nc.vector.reciprocal(den, den).then_inc(*dve_done.inc())
                        settle()
                        nc.vector.tensor_tensor(yf, yf, den.rearrange("p (h o) -> p h o", o=1).broadcast_to([T, 4, 64]), ALU.mult).then_inc(*dve_done.inc())
                        settle()
                        src = yf
                    else:
                        src = outb.t[0:T, 0:256].rearrange("p (h v) -> p h v", h=4)
                    for h in range(4):
                        nc.vector.bn_stats(stats[0:T, h, :], src[:, h, :]).then_inc(*dve_done.inc())
                    settle()
                    for h in range(4):
                        nc.vector.bn_aggr(mv[0:T, h, :], stats[0:T, h, :]).then_inc(*(mv_done.inc(s) if h == 3 else dve_done.inc()))
                    settle()
                    dve.wait_ge(*mv_done.at(s))
                    for h in range(4):
                        nc.vector.scalar_tensor_tensor(yf[:, h, :], src[:, h, :], mv[0:T, h, 0:1], gate[:, h, :], ALU.subtract, ALU.mult).then_inc(
                            *(outb.free.inc(s) if h == 3 and br != "ml" else dve_done.inc()))
                    if nb == 1:
                        dve.wait_ge(*upd.full.at(s + ("U",)))
                        if br == "rt":
                            nc.vector.tensor_tensor(S_rt[:, :], S_rt[:, :], upd.t[:, 0:64], ALU.add).then_inc(*dve_done.inc())
                            settle()
                            nc.vector.tensor_scalar(S_rt[:, :], S_rt[:, :], C("gam")[:, 0:1], None, ALU.mult).then_inc(*upd.free.inc(s + ("U",)))
                        else:
                            S = S_hg if br == "hg" else S_ml
                            for j in range(2):
                                dec = hdec[:, j, 0:1] if br == "hg" else small[:, 16 + j:17 + j]
                                nc.vector.scalar_tensor_tensor(S[:, j, :], S[:, j, :], dec, upd.t[:, j * dv:(j + 1) * dv], ALU.mult, ALU.add).then_inc(
                                    *(upd.free.inc(s + ("U",)) if j else dve_done.inc()))
                        dve.wait_ge(*upd.free.at(s + ("U",)))
                    else:
                        for h in range(4):
                            if h or samples.index(s):
                                i = samples.index(s)
                                dve.wait_ge(*vexp_used.at(s + (h - 1,) if h else samples[i - 1] + (3,)))
                            vs = (v_all[0:TS, c, h * 64:h * 64 + 64] if v_all is not None else mvv[0:TS, c, h, 0:64])
                            nc.vector.tensor_tensor(ex[0:TS, :].rearrange("p (b v) -> p b v", b=NB),
                                                    vs.rearrange("p (o v) -> p o v", o=1).broadcast_to([TS, NB, 64]),
                                                    C("bmask").rearrange("p (b o) -> p b o", o=1).broadcast_to([TS, NB, 64]), ALU.mult).then_inc(*vexp_done.inc(s + (h,)))
                        dve.wait_ge(*scores.full.at(s + ("su",)))
                        for j in range(1 if br == "rt" else 2):
                            sv = sst[:, j, :, 0:dv]
                            if br == "rt":
                                pass
                            else:
                                dec = (hdec[:, j, :] if br == "hg" else small[:, 16 + NB * j:16 + NB * j + NB])
                                nc.vector.tensor_tensor(sv, sv, dec.rearrange("p (b o) -> p b o", o=1).broadcast_to([P, NB, dv]), ALU.mult).then_inc(*dve_done.inc())
                                settle()
                            nc.vector.tensor_tensor(sst[:, j, :, 0:64], sst[:, j, :, 0:64], scores.t[:, j, :].rearrange("p (b v) -> p b v", b=NB), ALU.add).then_inc(
                                *(scores.free.inc(s + ("su",)) if j or br == "rt" else dve_done.inc()))
                            if br == "rt":
                                dve.wait_ge(*scores.free.at(s + ("su",)))
                                nc.vector.tensor_scalar(sst[:, j, :, 0:64], sst[:, j, :, 0:64], C("gam")[:, 1:2], None, ALU.mult).then_inc(*dve_done.inc())
                        if br == "ml":
                            dve.wait_ge(*upd.full.at(s + ("n",)))
                            dve.wait_ge(*scores.free.at(s + ("su",)))
                            nc.vector.tensor_tensor(sst[:, :, :, 64], sst[:, :, :, 64], upd.t[:, 0:2 * NB].rearrange("p (j b) -> p j b", j=2), ALU.add).then_inc(*upd.free.inc(s + ("n",)))
                            dve.wait_ge(*upd.free.at(s + ("n",)))
                        settle()
                        dve.wait_ge(*scores.free.at(s + ("su",)))
                        nc.vector.memset(small[0:1, 59:60], 0.0).then_inc(*ss_new.inc(s))
                    settle()
                    if br != "ml":
                        dve.wait_ge(*outb.free.at(s))
                    dve.wait_ge(*rs_done.at(s))
                    nc.vector.tensor_tensor(yf, yf, rs[0:T, :].rearrange("p (h o) -> p h o", o=1).broadcast_to([T, 4, 64]), ALU.mult).then_inc(*y_done.inc(s))
                elif s[0] == "out":
                    k = part
                    r, sl = chunk_len(k[2]), oslot[k]
                    bank = PB[bank_of[k]]
                    dve.wait_ge(*xo_in[sl].at(k))
                    dve.wait_ge(*bank.full.at(k))
                    nc.vector.tensor_tensor(xo[0:r, sl, :], xo[0:r, sl, :], bank.t[0:r, 0:256], ALU.add).then_inc(*bank.free.inc(k))
                    dve.wait_ge(*bank.free.at(k))
                    nc.vector.memset(small[0:1, 58:59], 0.0).then_inc(*xo_sum.inc(k))
                elif s[0] == "final":
                    dve.wait_ge(*nw_in.at("final"))
                    scale_rows(("final", part))

        @block.tensor
        def _(pe):
            pe.wait_ge(*const_in.at(4))
            pe.wait_ge(*pool_setup.at("all"))
            for s, part in plan:
                if s[0] == "norm":
                    for t in [part]:
                        r = chunk_len(t)
                        pe.wait_ge(*h_done.at((s[1], t)))
                        for g in range(2):
                            u = ("norm", s[1], t, g)
                            bank = PB[bank_of[u]]
                            bank.claim(pe, u)
                            for k in range(4):
                                mm = nc.tensor.transpose(bank.t[:, k * P:k * P + r], xt[0:r, tslot[(s[1], t)], (4 * g + k) * P:(4 * g + k + 1) * P],
                                                         ident[0:r, 0:r])
                            mm.then_inc(*bank.full.inc(u))
                elif s[0] == "proj" and part[0] == "mm":
                    b, n = s[1:], s[1]
                    pe.wait_ge(*whi_done.at(b))
                    pe.wait_ge(*wlo_done.at(b))
                    sl = hslot[b]
                    for k in [part[1]]:
                        bank = PB[bank_of[k]]
                        bank.claim(pe, k)
                        if k == [q for q in pieces if q[:2] == b][0]:
                            for t in tiles_of(n):
                                for g in range(2):
                                    u = ("norm", n, t, g)
                                    pe.wait_ge(*PB[bank_of[u]].free.at(u))
                        for kt in range(KT):
                            for x, w in ((hhi, whi), (hhi, wlo), (hlo, whi)):
                                first, last = kt == 0 and w is whi and x is hhi, kt == KT - 1 and x is hlo
                                if BLOCK[b[1]][3] == "ch":
                                    _, c0, ln = piece_psum(k)
                                    c = slice(c0, c0 + ln)
                                    mm = nc.tensor.matmul(bank.t[:, 0:c.stop - c.start], w[:, sl, kt, k[2] * P:(k[2] + 1) * P], x[:, kt, c],
                                                          start=first, stop=last)
                                else:
                                    c = slice(k[2] * P, k[2] * P + P) if k[2] < NCH else slice(W - P, W)
                                    width = BLOCK[b[1]][2]
                                    mm = nc.tensor.matmul(bank.t[:, 0:width], x[:, kt, c], w[:, sl, kt, 0:width], start=first, stop=last)
                        mm.then_inc(*bank.full.inc(k))
                elif s[0] == "s5set" and part == "c":
                    k = s + ("C",)
                    aux.claim(pe, k)
                    pe.wait_ge(*set_in.at(s + (5,)))
                    for ri in range(2):
                        for f in range(2):
                            mm = nc.tensor.transpose(aux.t[:, (2 * ri + f) * P:(2 * ri + f + 1) * P], cCn[:, ri, f, :], ident)
                    mm.then_inc(*aux.full.inc(k))
                elif s[0] == "s5set" and part == "w":
                    pe.wait_ge(*set_dve.at(s + ("W",)))
                    for ri in range(2):
                        scores.claim(pe, s + (ri,))
                        for q in range(8):
                            mm = nc.tensor.transpose(scores.t[:, q // 4, q % 4 * P:(q % 4 + 1) * P], cW[:, ri, q].rearrange("p s c -> p (s c)"), ident)
                        mm.then_inc(*scores.full.inc(s + (ri,)))
                    for r in range(2):
                        scores.claim(pe, s + (2 + r,))
                        for a in range(2):
                            h = slice(64 * a, 64 * a + 64)
                            for q in range(4):
                                for ri in range(2):
                                    mm = nc.tensor.matmul(scores.t[0:16, a, q * P:(q + 1) * P], cBb[h, ri, 4 * r + q, :],
                                                          cV[h, ri, 4 * r + q, 0:8].rearrange("p j c -> p (j c)"), start=ri == 0, stop=ri == 1)
                        mm.then_inc(*scores.full.inc(s + (2 + r,)))
                elif s[0] == "s5" and part == "w":
                    n = s[1]
                    odd = n % 2
                    pe.wait_ge(*s5_in["W"].at(s))
                    pe.wait_ge(*s5_u.at(s + (7 + 4 * odd,)))
                    scores.claim(pe, s + (0,))
                    for ri in range(2):
                        for q in range(8):
                            for a in range(2):
                                mm = nc.tensor.matmul(scores.t[64 * a:64 * a + 64, ri, q * 64:(q + 1) * 64], sWT[:, q, ri, 64 * a:64 * a + 64],
                                                      U[:, 2 * q + a, 0:64], start=True, stop=True)
                    mm.then_inc(*scores.full.inc(s + (0,)))
                    if odd:
                        upd.claim(pe, s + ("w",))
                        for ri in range(2):
                            for q in range(8):
                                for a in range(2):
                                    mm = nc.tensor.matmul(upd.t[64 * a:64 * a + 64, (8 * ri + q) * NB:(8 * ri + q + 1) * NB], sWT[:, q, ri, 64 * a:64 * a + 64],
                                                          U[:, 2 * q + a, 64:72], start=True, stop=True)
                        mm.then_inc(*upd.full.inc(s + ("w",)))
                elif s[0] == "s5" and part == "y":
                    odd = s[1] % 2
                    pe.wait_ge(*s5_in["T"].at(s))
                    pe.wait_ge(*s5_in["V"].at(s))
                    pe.wait_ge(*s5_rot.at(s))
                    scores.claim(pe, s + (1,))
                    for a in range(2):
                        h = slice(64 * a, 64 * a + 64)
                        for q in range(8):
                            o = scores.t[:, a, q * 64:(q + 1) * 64]
                            nc.tensor.matmul(o, sT[:, 2 * q + a, :], U[:, 2 * q + a, 0:64], start=True, stop=False)
                            nc.tensor.matmul(o, sV[h, 0, q, :], sX[h, 0, q, 0:64], start=False, stop=False)
                            mm = nc.tensor.matmul(o, sV[h, 1, q, :], sX[h, 1, q, 0:64], start=False, stop=True)
                    mm.then_inc(*scores.full.inc(s + (1,)))
                    if odd:
                        for a, bank in enumerate((upd, aux)):
                            bank.claim(pe, s + ("y",))
                            h = slice(64 * a, 64 * a + 64)
                            for q in range(8):
                                o = bank.t[0:64, q * NB:(q + 1) * NB]
                                nc.tensor.matmul(o, sT[:, 2 * q + a, 64:128], U[:, 2 * q + a, 64:72], start=True, stop=False)
                                nc.tensor.matmul(o, sV[h, 0, q, 0:64], sX0[h, 0, q, :], start=False, stop=False)
                                mm = nc.tensor.matmul(o, sV[h, 1, q, 0:64], sX0[h, 1, q, :], start=False, stop=True)
                            mm.then_inc(*bank.full.inc(s + ("y",)))
                elif s[0] == "s5" and part == "z":
                    odd = s[1] % 2
                    pe.wait_ge(*s5_in["G"].at(s))
                    pe.wait_ge(*s5_dve.at(s + ("gelu",)))
                    scores.claim(pe, s + (2,))
                    for j in range(2):
                        for kt in range(2):
                            mm = nc.tensor.matmul(scores.t[:, j, :], wglu[:, kt, j * P:(j + 1) * P], yg[:, kt, 0:HALF], start=kt == 0, stop=kt == 1)
                    mm.then_inc(*scores.full.inc(s + (2,)))
                    if odd:
                        upd.claim(pe, s + ("glu",))
                        for j in range(2):
                            for kt in range(2):
                                mm = nc.tensor.matmul(upd.t[:, j * TS:(j + 1) * TS], wglu[:, kt, j * P:(j + 1) * P], yg[:, kt, HALF:W], start=kt == 0, stop=kt == 1)
                        mm.then_inc(*upd.full.inc(s + ("glu",)))
                elif s[0] == "mlpre" and part is None:
                    n = s[1]
                    scores.claim(pe, s + (0,))
                    for k in [k for k in pieces if k[:2] == (n, "ml_ifg")]:
                        pe.wait_ge(*PB[bank_of[k]].free.at(k))
                    for t in range(NCH):
                        for i in range(2):
                            mm = nc.tensor.transpose(scores.t[0:4, i, t * P:(t + 1) * P], ifc[:, t, 4 * i:4 * i + 4], ident)
                    mm.then_inc(*scores.full.inc(s + (0,)))
                    if n % 2:
                        upd.claim(pe, s + ("s",))
                        for i in range(2):
                            mm = nc.tensor.transpose(upd.t[0:4, TS * i:TS * i + TS], ifc[0:TS, NCH, 4 * i:4 * i + 4], ident[0:TS, 0:TS])
                        mm.then_inc(*upd.full.inc(s + ("s",)))
                elif s in mixes and part in ("B0", "B1", "C"):
                    br, n, c = s
                    T, cc = chunk_len(c), cols(c)
                    sample = c == NCH
                    stt = ST if c < NCH else STs
                    dv = 65 if br == "ml" else 64
                    def v(h):
                        if br == "ml":
                            return mvv[0:T, c, h, :]
                        return (hv if br == "hg" else rv)[0:T, c, h * 64:h * 64 + 64]

                    def q(h):
                        if br == "hg":
                            return QD[:, h // 2, h % 2, 0:T]
                        return (rq if br == "rt" else mq)[:, h, cc]

                    def state(h, b=None):
                        j = 0 if br == "rt" else h // 2
                        if b is not None:
                            return sst[:, j, b, 0:dv]
                        return S_rt[:, :] if br == "rt" else (S_hg if br == "hg" else S_ml)[:, j, :]

                    def score_bank(j):
                        scores.claim(pe, s + (j,))
                        if br == "hg":
                            pe.wait_ge(*hg_prod.at(s + (j,)))
                            u = T // 2
                            for i in range(len(levels(c))):
                                mm = nc.tensor.matmul(scores.t[0:T, i // 4, i % 4 * 2 * u:(i % 4 + 1) * 2 * u].rearrange("p (h x) -> p h x", h=2),
                                                      E[:, i, j, 0:T], QE[:, i, :, 0:u], start=True, stop=True)
                        elif br == "rt":
                            mm = nc.tensor.matmul(scores.t[0:T, 0, 0:4 * T].rearrange("p (h t) -> p h t", h=4), rk[:, cc], rq[:, :, cc], start=True, stop=True)
                        else:
                            for i in range(2):
                                nc.tensor.matmul(scores.t[0:T, 0, i * 2 * T:(i + 1) * 2 * T].rearrange("p (h t) -> p h t", h=2),
                                                 mk[:, i, cc], mq[:, 2 * i:2 * i + 2, cc], start=True, stop=True)
                            for h in range(4):
                                mm = nc.tensor.matmul(scores.t[0:T, 1, h * T:(h + 1) * T], ident[0:4, h:h + 1].broadcast_to([4, T]),
                                                      rows[:, A_, cc], start=True, stop=True)
                        mm.then_inc(*scores.full.inc(s + (j,)))

                    tk = s + ("turn",)
                    if part == "B1":
                        score_bank(1)
                        continue
                    if part == "B0":
                        if br == "hg":
                            pe.wait_ge(*hg_prod.at(s + (0,)))
                        elif br == "rt":
                            pe.wait_ge(*rot_done.at(n))
                        else:
                            pe.wait_ge(*pre_dve.at(("mlpre", n, 0)))
                        if c in (0, NCH):
                            for k in [k for k in pieces if k[0] == n and k[1] in ("hg_i", "rt_v", "ml_v", "ml_k", "ml_q") and k[1][:2] == br]:
                                pe.wait_ge(*PB[bank_of[k]].free.at(k))
                        aux.claim(pe, tk)
                        if br == "rt":
                            mm = nc.tensor.transpose(aux.t[0:T, 0:P], rk[:, cc], ident)
                        else:
                            for j in range(2):
                                src = E[:, 7, j, 0:T] if br == "hg" else mk[:, j, cc]
                                mm = nc.tensor.transpose(aux.t[0:T, j * P:(j + 1) * P], src, ident)
                        if br == "hg":
                            for j in range(2):
                                mm = nc.tensor.matmul(aux.t[0:T, 256 + 2 * j:258 + 2 * j], E[:, 9, j, 0:T], C("headsel"), start=True, stop=True)
                        if br == "ml":
                            for i, slot in enumerate((G_, SP_, M_, WK_)):
                                nc.tensor.transpose(aux.t[0:T, 256 + 4 * i:260 + 4 * i], rows[:, slot, cc], ident[0:4, 0:4])
                            nb = NB if sample else 1
                            for j in range(2):
                                lhs = C("selj")[:, j * P:(j + 1) * P]
                                last = rows[:, SP_, HALF + DSEQ - 1:W:DSEQ] if sample else rows[:, SP_, cc.stop - 1:cc.stop]
                                mm = nc.tensor.matmul(aux.t[:, 272 + nb * j:272 + nb * (j + 1)], lhs, last, start=True, stop=True)
                        mm.then_inc(*aux.full.inc(tk))
                        score_bank(0)
                        continue
                    if sample:
                        ik = s + ("inter",)
                        upd.claim(pe, ik)
                        pe.wait_ge(*ss_in.at(s + (ss_parts[br] - 1,)))
                        for h in range(4):
                            for b in range(NB):
                                mm = nc.tensor.matmul(upd.t[0:dv, h * TS + DSEQ * b:h * TS + DSEQ * (b + 1)], state(h, b),
                                                      q(h)[:, DSEQ * b:DSEQ * (b + 1)], start=True, stop=True)
                        mm.then_inc(*upd.full.inc(ik))
                        pe.wait_ge(*upd.free.at(ik))
                    elif before(upd_keys, s + ("U",)):
                        pe.wait_ge(*upd.free.at(before(upd_keys, s + ("U",))))
                    pe.wait_ge(*st_done.at(s))
                    outb.claim(pe, s)
                    for h in range(4):
                        o = outb.t[0:T, h * dv:(h + 1) * dv]
                        if br != "ml":
                            if sample:
                                nc.tensor.matmul(o, oT[0:dv, h, :], ident[0:dv, 0:dv], start=True, stop=False)
                            else:
                                nc.tensor.matmul(o, q(h), state(h), start=True, stop=False)
                        mm = nc.tensor.matmul(o, stt[0:T, h, 0:T], v(h), start=br == "ml", stop=True)
                    mm.then_inc(*outb.full.inc(s))
                    if br == "ml":
                        ak = s + (1,)
                        scores.claim(pe, ak)
                        for h in range(4):
                            o = scores.t[0:T, 0, h * dv:(h + 1) * dv]
                            if sample:
                                mm = nc.tensor.matmul(o, oT[0:dv, h, :], ident[0:dv, 0:dv], start=True, stop=True)
                            else:
                                mm = nc.tensor.matmul(o, q(h), state(h), start=True, stop=True)
                        mm.then_inc(*scores.full.inc(ak))
                    pe.wait_ge(*aux.free.at(tk))
                    dk = 32 if br == "rt" else 64
                    if not sample:
                        uk = s + ("U",)
                        upd.claim(pe, uk)
                        for h in range(4):
                            p0 = 32 * h if br == "rt" else h % 2 * 64
                            c0 = 0 if br == "rt" else h // 2 * dv
                            mm = nc.tensor.matmul(upd.t[p0:p0 + dk, c0:c0 + dv], kT[0:T, h * dk:(h + 1) * dk], v(h), start=True, stop=True)
                        mm.then_inc(*upd.full.inc(uk))
                    else:
                        if br == "ml":
                            nk = s + ("n",)
                            upd.claim(pe, nk)
                            for h in range(4):
                                p0 = h % 2 * 64
                                mm = nc.tensor.matmul(upd.t[p0:p0 + 64, h // 2 * NB:(h // 2 + 1) * NB], kT[0:T, h * 64:h * 64 + 64], C("bmask"), start=True, stop=True)
                            mm.then_inc(*upd.full.inc(nk))
                        sk = s + ("su",)
                        scores.claim(pe, sk)
                        for h in range(4):
                            p0 = 32 * h if br == "rt" else h % 2 * 64
                            pe.wait_ge(*vexp_done.at(s + (h,)))
                            nc.tensor.matmul(scores.t[p0:p0 + dk, 0 if br == "rt" else h // 2, :], kT[0:T, h * dk:(h + 1) * dk], ex[0:T, :],
                                             start=True, stop=True).then_inc(*vexp_used.inc(s + (h,)))
                        pe.wait_ge(*vexp_used.at(s + (3,)))
                        nc.tensor.matmul(aux.t[0:1, 500:501], ident[:, 0:1], ident[:, 0:1], start=True, stop=True).then_inc(*scores.full.inc(sk))
                elif s in mixes and part == "D":
                    br, n, c = s
                    T = chunk_len(c)
                    pe.wait_ge(*y_done.at(s))
                    xk = s + ("mixed",)
                    aux.claim(pe, xk)
                    for j in range(2):
                        mm = nc.tensor.transpose(aux.t[:, j * P:j * P + T], y[0:T, 2 * j:2 * j + 2, :], ident[0:T, 0:T])
                    mm.then_inc(*aux.full.inc(xk))
                elif s[0] == "out":
                    n, k = s[1], part
                    if k == outs_of(n)[0]:
                        if s5n:
                            pe.wait_ge(*s5_dve.at(("s5", n, "mixed")))
                        done = [k for k in aux_keys if k[0] != "s5set" and k[1] <= n]
                        if done:
                            pe.wait_ge(*aux.free.at(done[-1]))
                    b = (n, "wo", k[1])
                    if k[2] == 0:
                        pe.wait_ge(*wr_in[wslot[b]].at(b))
                    bank = PB[bank_of[k]]
                    bank.claim(pe, k)
                    r = chunk_len(k[2])
                    for kt in range(8):
                        mm = nc.tensor.matmul(bank.t[0:r, 0:256], mixT[:, kt, k[2] * P:k[2] * P + r], wraw[:, wslot[b], kt, 0:256],
                                              start=kt == 0, stop=kt == 7)
                    mm.then_inc(*bank.full.inc(k))


OUTPUTS = {
    "y_prompt": (1, SEQ, D), "y_sample": (NB, DSEQ, D),
    "p_s5_re": (DEPTH, 1, 16, 64), "p_s5_im": (DEPTH, 1, 16, 64), "p_hgrn": (DEPTH, 1, 4, 64, 64),
    "p_mlstm_C": (DEPTH, 1, 4, 64, 64), "p_mlstm_n": (DEPTH, 1, 4, 64), "p_mlstm_m": (DEPTH, 1, 4),
    "p_ret": (DEPTH, 1, 4, 32, 64),
    "d_s5_re": (DEPTH, NB, 16, 64), "d_s5_im": (DEPTH, NB, 16, 64), "d_hgrn": (DEPTH, NB, 4, 64, 64),
    "d_mlstm_C": (DEPTH, NB, 4, 64, 64), "d_mlstm_n": (DEPTH, NB, 4, 64), "d_mlstm_m": (DEPTH, NB, 4),
    "d_ret": (DEPTH, NB, 4, 32, 64),
}


def kernel(**inputs):
    import concourse.bacc as bacc
    from concourse.bass_utils import run_bass_kernel_spmd

    nc = bacc.Bacc("TRN2", target_bir_lowering=False, num_devices=1)
    packed, masks, rot = constants()
    arrays = {"c_packed": packed, "c_masks": masks, "c_rot": rot}
    arrays.update({k: np.ascontiguousarray(v) for k, v in inputs.items()})
    inp = {k: nc.dram_tensor("in_" + k, a.shape, mybir.dt.from_np(a.dtype), kind="ExternalInput").ap() for k, a in arrays.items()}
    out = {k: nc.dram_tensor("out_" + k, shape, F32, kind="ExternalOutput").ap() for k, shape in OUTPUTS.items()}
    trunk_kernel(nc, inp, out)
    r = run_bass_kernel_spmd(nc, [{"in_" + k: a for k, a in arrays.items()}], core_ids=[0])
    return tuple(r.results[0]["out_" + k] for k in OUTPUTS)
```
